# Optimizing a Trainium2 kernel written in Bass

```python
import math
import jax
import jax.numpy as jnp
from jax import lax
import numpy as np

D_MODEL = 1024
BATCH = 1
SEQ = 256
DEPTH = 2

N_EVEN = (DEPTH + 1) // 2
N_ODD = DEPTH // 2
EPS = 1e-6
NEG = -1e30
FORCE_SCORE = 1e9
Q_BLOCK = 128

FOX_HEADS = 8
FOX_DH = 64
GDN_HEADS = 4
GDN_DH = 128
GDN_CONV = 4
GDN_CHUNK = 64
NSA_HEADS = 8
NSA_KV_HEADS = 2
NSA_GROUP = NSA_HEADS // NSA_KV_HEADS
NSA_DH = 64
CMP_LEN = 32
CMP_STRIDE = 16
CMP_HIDDEN = 256
SLC_LEN = 64
SLC_TOPK = 16
WINDOW = 512
GLA_HEADS = 4
GLA_DK = 64
GLA_DV = 128
GLA_GATE_RANK = 16
GLA_TAU = 16.0
GLA_CHUNK = 64
REL_BUCKETS = 32
REL_MAX_DIST = 128
N_EXPERTS = 64
TOP_K = 6
D_EXPERT = 256
D_SHARED = 256
N_GROUPS = 8
TOPK_GROUPS = 4
ROUTE_SCALE = 2.5
MOE_BLOCK = 128

FOX_W = FOX_HEADS * FOX_DH
GDN_W = GDN_HEADS * GDN_DH
NSA_W = NSA_HEADS * NSA_DH
NSA_KV_W = NSA_KV_HEADS * NSA_DH
GLA_KW = GLA_HEADS * GLA_DK
GLA_W = GLA_HEADS * GLA_DV
EV_SIZES = (FOX_W, FOX_W, FOX_W, FOX_HEADS, 3 * GDN_W, GDN_HEADS, GDN_HEADS, GDN_W)
OD_SIZES = (NSA_W,) + (NSA_KV_W,) * 6 + (3 * NSA_HEADS, GLA_KW, GLA_KW, GLA_W, GLA_GATE_RANK, GLA_W)
EV_IN = sum(EV_SIZES)
OD_IN = sum(OD_SIZES)
EV_OUT = FOX_W + GDN_W
OD_OUT = NSA_W + GLA_W

kernel_name = 'hybrid_fox_gdn_nsa_gla_moe_trunk'

F32 = jnp.float32

def _split(a, sizes):
    cuts = [int(s) for s in np.cumsum(sizes)[:-1]]
    return jnp.split(a, cuts, axis=-1)

def rms_norm(x, g):
    xf = x.astype(F32)
    y = xf * lax.rsqrt(jnp.mean(xf * xf, axis=-1, keepdims=True) + EPS)
    return (y * g.astype(F32)).astype(x.dtype)

def l2_norm(x):
    xf = x.astype(F32)
    return xf * lax.rsqrt(jnp.sum(xf * xf, axis=-1, keepdims=True) + EPS)

def masked_softmax(s, mask, axis=-1):
    p = jax.nn.softmax(jnp.where(mask, s, NEG), axis=axis)
    return jnp.where(mask, p, 0.0)

def t5_bucket(dist):
    n = jnp.maximum(dist, 0)
    exact = REL_BUCKETS // 2
    nf = jnp.maximum(n, 1).astype(F32)
    large = exact + (jnp.log(nf / exact) / math.log(REL_MAX_DIST / exact) * (REL_BUCKETS - exact)).astype(jnp.int32)
    large = jnp.minimum(large, REL_BUCKETS - 1)
    return jnp.where(n < exact, n, large)

def causal_depthwise_conv(x, w):
    k = w.shape[0]
    xp = jnp.pad(x, ((0, 0), (k - 1, 0), (0, 0)))
    return lax.conv_general_dilated(xp, w[:, None, :].astype(x.dtype), window_strides=(1,), padding='VALID',
                                    dimension_numbers=('NWC', 'WIO', 'NWC'), feature_group_count=x.shape[-1])

def _to_chunks(a, c):
    b, t = a.shape[:2]
    a = a.reshape(b, t // c, c, *a.shape[2:])
    return jnp.swapaxes(a, 2, 3)

def _from_chunks(o):
    n, b, h, c, d = o.shape
    return o.transpose(1, 0, 3, 2, 4).reshape(b, n * c, h, d)

def fox_attention(q, k, v, log_f):
    b, t, h, dh = q.shape
    nb = t // Q_BLOCK
    cum = jnp.cumsum(log_f, axis=1)
    cum_k = jnp.swapaxes(cum, 1, 2)
    q_blocks = q.reshape(b, nb, Q_BLOCK, h, dh).transpose(1, 0, 3, 2, 4)
    c_blocks = cum.reshape(b, nb, Q_BLOCK, h).transpose(1, 0, 3, 2)
    k_pos = jnp.arange(t)
    scale = dh ** -0.5

    def block(args):
        i, q_i, c_i = args
        q_pos = i * Q_BLOCK + jnp.arange(Q_BLOCK)
        s = jnp.einsum('bhqd,bthd->bhqt', q_i, k, preferred_element_type=F32) * scale
        s = s + c_i[..., None] - cum_k[:, :, None, :]
        p = masked_softmax(s, k_pos[None, :] <= q_pos[:, None])
        return jnp.einsum('bhqt,bthd->bqhd', p.astype(v.dtype), v)

    o = lax.map(block, (jnp.arange(nb), q_blocks, c_blocks))
    return o.transpose(1, 0, 2, 3, 4).reshape(b, t, h * dh)

def gated_delta_rule(q, k, v, g, beta):
    dk = q.shape[-1]
    dv = v.shape[-1]
    c = GDN_CHUNK
    q = _to_chunks(q.astype(F32), c) * dk ** -0.5
    k = _to_chunks(k.astype(F32), c)
    v = _to_chunks(v.astype(F32), c)
    beta = _to_chunks(beta.astype(F32), c)
    g = jnp.cumsum(_to_chunks(g.astype(F32), c), axis=-1)
    causal = jnp.tril(jnp.ones((c, c), dtype=bool))
    strict = jnp.tril(jnp.ones((c, c), dtype=bool), k=-1)
    decay = jnp.exp(jnp.where(causal, g[..., :, None] - g[..., None, :], NEG))
    kb = k * beta[..., None]
    lower = jnp.where(strict, jnp.einsum('bnhid,bnhjd->bnhij', kb, k) * decay, 0.0)
    rhs = jnp.concatenate([v * beta[..., None], kb * jnp.exp(g)[..., None]], axis=-1)
    sol = lax.linalg.triangular_solve(lower + jnp.eye(c, dtype=F32), rhs, left_side=True, lower=True,
                                      unit_diagonal=True)
    u, w = sol[..., :dv], sol[..., dv:]
    attn = jnp.where(causal, jnp.einsum('bnhid,bnhjd->bnhij', q, k) * decay, 0.0)
    q_dec = q * jnp.exp(g)[..., None]
    g_last = g[..., -1]
    k_dec = k * jnp.exp(g_last[..., None] - g)[..., None]

    def step(S, xs):
        u_n, w_n, a_n, q_n, k_n, gl_n = xs
        v_new = u_n - jnp.einsum('bhck,bhkv->bhcv', w_n, S)
        o = jnp.einsum('bhck,bhkv->bhcv', q_n, S) + jnp.einsum('bhij,bhjv->bhiv', a_n, v_new)
        S = S * jnp.exp(gl_n)[..., None, None] + jnp.einsum('bhck,bhcv->bhkv', k_n, v_new)
        return S, o

    xs = tuple(jnp.swapaxes(a, 0, 1) for a in (u, w, attn, q_dec, k_dec, g_last))
    b, _, h = q.shape[:3]
    _, o = lax.scan(step, jnp.zeros((b, h, dk, dv), F32), xs)
    return _from_chunks(o)

def gla_chunked(q, k, v, log_a):
    dk = q.shape[-1]
    dv = v.shape[-1]
    c = GLA_CHUNK
    q = _to_chunks(q.astype(F32), c) * dk ** -0.5
    k = _to_chunks(k.astype(F32), c)
    v = _to_chunks(v.astype(F32), c)
    G = jnp.cumsum(_to_chunks(log_a.astype(F32), c), axis=-2)
    q_dec = q * jnp.exp(G)
    causal = jnp.tril(jnp.ones((c, c), dtype=bool))
    attn = jnp.where(causal, jnp.einsum('bnhid,bnhjd->bnhij', q_dec, k * jnp.exp(-G)), 0.0)
    o_intra = jnp.einsum('bnhij,bnhjv->bnhiv', attn, v)
    G_last = G[..., -1, :]
    k_dec = k * jnp.exp(G_last[..., None, :] - G)

    def step(S, xs):
        q_n, k_n, v_n, gl_n = xs
        o = jnp.einsum('bhck,bhkv->bhcv', q_n, S)
        S = S * jnp.exp(gl_n)[..., None] + jnp.einsum('bhck,bhcv->bhkv', k_n, v_n)
        return S, o

    xs = tuple(jnp.swapaxes(a, 0, 1) for a in (q_dec, k_dec, v, G_last))
    b, _, h = q.shape[:3]
    _, o_inter = lax.scan(step, jnp.zeros((b, h, dk, dv), F32), xs)
    return _from_chunks(o_inter + jnp.swapaxes(o_intra, 0, 1))

def nsa_compress(kv, pos, w1, w2):
    b, t, kvh, dh = kv.shape
    n_cmp = (t - CMP_LEN) // CMP_STRIDE + 1
    idx = jnp.arange(n_cmp)[:, None] * CMP_STRIDE + jnp.arange(CMP_LEN)[None, :]
    blk = kv[:, idx] + pos[None, None, :, None, :].astype(kv.dtype)
    blk = blk.transpose(0, 1, 3, 2, 4).reshape(b, n_cmp, kvh, CMP_LEN * dh)
    out = jax.nn.silu(blk @ w1) @ w2
    return out.transpose(0, 2, 1, 3)

def nsa_attention(q, k_cmp, v_cmp, k_slc, v_slc, k_win, v_win, gate_logits, qn, kn, pos, cw1, cw2, rel_bias):
    b, t = q.shape[:2]
    kvh, grp, dh = NSA_KV_HEADS, NSA_GROUP, NSA_DH
    nb = t // Q_BLOCK
    n_cmp = (t - CMP_LEN) // CMP_STRIDE + 1
    n_slc = t // SLC_LEN
    top_n = min(SLC_TOPK, n_slc)
    scale = dh ** -0.5

    def heads(a):
        return a.reshape(b, t, kvh, dh)

    qh = rms_norm(q.reshape(b, t, NSA_HEADS, dh), qn)
    q_blocks = qh.reshape(b, nb, Q_BLOCK, kvh, grp, dh).transpose(1, 0, 3, 4, 2, 5)
    kc = rms_norm(nsa_compress(heads(k_cmp), pos[0], cw1[0], cw2[0]), kn)
    vc = nsa_compress(heads(v_cmp), pos[1], cw1[1], cw2[1])
    ks = rms_norm(heads(k_slc), kn).reshape(b, n_slc, SLC_LEN, kvh, dh).transpose(0, 3, 1, 2, 4)
    vs = heads(v_slc).reshape(b, n_slc, SLC_LEN, kvh, dh).transpose(0, 3, 1, 2, 4)
    pad = ((0, 0), (0, 0), (WINDOW, 0), (0, 0))
    kw = jnp.pad(jnp.swapaxes(rms_norm(heads(k_win), kn), 1, 2), pad)
    vw = jnp.pad(jnp.swapaxes(heads(v_win), 1, 2), pad)
    cmp_start = jnp.arange(n_cmp) * CMP_STRIDE
    cmp_end = cmp_start + CMP_LEN - 1
    slc_start = jnp.arange(n_slc) * SLC_LEN
    overlap = ((cmp_start[:, None] < slc_start[None, :] + SLC_LEN)
               & (cmp_start[:, None] + CMP_LEN > slc_start[None, :])).astype(F32)
    table_h = rel_bias.T.reshape(kvh, grp, REL_BUCKETS).astype(F32)
    table_kg = jnp.transpose(rel_bias.reshape(REL_BUCKETS, kvh, grp), (1, 0, 2)).astype(F32)
    gather_blocks = jax.vmap(jax.vmap(lambda blk, ix: blk[ix]))
    blk_id = jnp.arange(n_slc)

    def block(args):
        i, q_i = args
        q_pos = i * Q_BLOCK + jnp.arange(Q_BLOCK)
        s = jnp.einsum('bkgqd,bknd->bkgqn', q_i, kc, preferred_element_type=F32) * scale
        s = s + table_h[:, :, t5_bucket(q_pos[:, None] - cmp_end[None, :])]
        p_cmp = masked_softmax(s, cmp_end[None, :] <= q_pos[:, None])
        o_cmp = jnp.einsum('bkgqn,bknd->bkgqd', p_cmp.astype(vc.dtype), vc)
        imp = jnp.einsum('bkgqn,ns->bkqs', p_cmp, overlap)
        cur = q_pos // SLC_LEN
        forced = (blk_id[None, :] == 0) | (blk_id[None, :] == cur[:, None]) | (blk_id[None, :] == cur[:, None] - 1)
        imp = jnp.where(forced, FORCE_SCORE, jnp.where(blk_id[None, :] <= cur[:, None], imp, NEG))
        _, idx = lax.top_k(imp, top_n)
        k_sel = gather_blocks(ks, idx)
        v_sel = gather_blocks(vs, idx)
        sel_pos = idx[..., None] * SLC_LEN + jnp.arange(SLC_LEN)
        dist = q_pos[:, None, None] - sel_pos
        bias = jax.vmap(lambda tb, bk: tb[bk], in_axes=(0, 1), out_axes=1)(table_kg, t5_bucket(dist))
        s = jnp.einsum('bkgqd,bkqnld->bkgqnl', q_i, k_sel, preferred_element_type=F32) * scale
        s = s + jnp.moveaxis(bias, -1, 2)
        p_sel = masked_softmax(s, (dist >= 0)[:, :, None], axis=(-2, -1))
        o_slc = jnp.einsum('bkgqnl,bkqnld->bkgqd', p_sel.astype(v_sel.dtype), v_sel)
        k_i = lax.dynamic_slice_in_dim(kw, i * Q_BLOCK, Q_BLOCK + WINDOW, axis=2)
        v_i = lax.dynamic_slice_in_dim(vw, i * Q_BLOCK, Q_BLOCK + WINDOW, axis=2)
        w_pos = i * Q_BLOCK - WINDOW + jnp.arange(Q_BLOCK + WINDOW)
        dist_w = q_pos[:, None] - w_pos[None, :]
        s = jnp.einsum('bkgqd,bkwd->bkgqw', q_i, k_i, preferred_element_type=F32) * scale
        s = s + table_h[:, :, t5_bucket(dist_w)]
        p_win = masked_softmax(s, (dist_w >= 0) & (dist_w < WINDOW) & (w_pos[None, :] >= 0))
        o_win = jnp.einsum('bkgqw,bkwd->bkgqd', p_win.astype(v_i.dtype), v_i)
        return jnp.stack([o_cmp, o_slc, o_win], axis=-1)

    o = lax.map(block, (jnp.arange(nb), q_blocks))
    o = o.transpose(1, 0, 4, 2, 3, 5, 6).reshape(b, t, NSA_HEADS, dh, 3)
    gates = jax.nn.sigmoid(gate_logits.astype(F32)).reshape(b, t, NSA_HEADS, 1, 3)
    return jnp.sum(o.astype(F32) * gates, axis=-1).reshape(b, t, NSA_W)

def even_mixer(h, w_in, w_out, fox_fb, fox_qn, fox_kn, gdn_conv, gdn_a_log, gdn_dt_bias, gdn_on):
    b, t, _ = h.shape
    fq, fk, fv, ff, gqkv, ga, gb, gz = _split(h @ w_in, EV_SIZES)

    def heads(a, n, d):
        return a.reshape(b, t, n, d)

    log_f = jax.nn.log_sigmoid((ff + fox_fb).astype(F32))
    o_fox = fox_attention(rms_norm(heads(fq, FOX_HEADS, FOX_DH), fox_qn),
                          rms_norm(heads(fk, FOX_HEADS, FOX_DH), fox_kn),
                          heads(fv, FOX_HEADS, FOX_DH), log_f)
    gq, gk, gv = jnp.split(jax.nn.silu(causal_depthwise_conv(gqkv, gdn_conv)), 3, axis=-1)
    g = -jnp.exp(gdn_a_log.astype(F32)) * jax.nn.softplus((ga + gdn_dt_bias).astype(F32))
    beta = jax.nn.sigmoid(gb.astype(F32))
    o = gated_delta_rule(l2_norm(heads(gq, GDN_HEADS, GDN_DH)), l2_norm(heads(gk, GDN_HEADS, GDN_DH)),
                         heads(gv, GDN_HEADS, GDN_DH), g, beta)
    o_gdn = rms_norm(o, gdn_on) * jax.nn.silu(heads(gz, GDN_HEADS, GDN_DH).astype(F32))
    y = jnp.concatenate([o_fox, o_gdn.reshape(b, t, GDN_W).astype(h.dtype)], axis=-1)
    return y @ w_out

def odd_mixer(h, w_in, w_out, nsa_qn, nsa_kn, nsa_pos, nsa_cmp_w1, nsa_cmp_w2, gla_wg_up, gla_bg, gla_on, rel_bias):
    b, t, _ = h.shape
    nq, kc, vc, ks, vs, kw, vw, ng, lq, lk, lv, lg, lr = _split(h @ w_in, OD_SIZES)
    o_nsa = nsa_attention(nq, kc, vc, ks, vs, kw, vw, ng, nsa_qn, nsa_kn, nsa_pos, nsa_cmp_w1, nsa_cmp_w2, rel_bias)
    log_a = jax.nn.log_sigmoid((lg @ gla_wg_up + gla_bg).astype(F32)) / GLA_TAU
    o = gla_chunked(lq.reshape(b, t, GLA_HEADS, GLA_DK), lk.reshape(b, t, GLA_HEADS, GLA_DK),
                    lv.reshape(b, t, GLA_HEADS, GLA_DV), log_a.reshape(b, t, GLA_HEADS, GLA_DK))
    o_gla = rms_norm(o, gla_on) * jax.nn.silu(lr.reshape(b, t, GLA_HEADS, GLA_DV).astype(F32))
    y = jnp.concatenate([o_nsa.astype(h.dtype), o_gla.reshape(b, t, GLA_W).astype(h.dtype)], axis=-1)
    return y @ w_out

def swiglu(x, wg, wu, wd):
    return (jax.nn.silu(x @ wg) * (x @ wu)) @ wd

def moe_ffn(h, router, e_bias, wg, wu, wd, sg, su, sd):
    b, t, d = h.shape
    xt = h.reshape(b * t, d)
    nt = b * t
    scores = jax.nn.sigmoid((xt @ router).astype(F32))
    biased = scores + e_bias.astype(F32)
    grp_score = lax.top_k(biased.reshape(nt, N_GROUPS, N_EXPERTS // N_GROUPS), 2)[0].sum(-1)
    _, top_g = lax.top_k(grp_score, TOPK_GROUPS)
    gmask = jax.nn.one_hot(top_g, N_GROUPS, dtype=F32).sum(axis=1) > 0
    emask = jnp.repeat(gmask, N_EXPERTS // N_GROUPS, axis=1)
    _, top_e = lax.top_k(jnp.where(emask, biased, -jnp.inf), TOP_K)
    w = jnp.take_along_axis(scores, top_e, axis=1)
    w = w / jnp.sum(w, axis=-1, keepdims=True) * ROUTE_SCALE
    n_assign = nt * TOP_K
    eid = top_e.reshape(-1)
    tok = jnp.repeat(jnp.arange(nt, dtype=jnp.int32), TOP_K)
    wts = w.reshape(-1)
    order = jnp.argsort(eid)
    e_sorted = eid[order]
    counts = jnp.zeros((N_EXPERTS,), jnp.int32).at[eid].add(1)
    starts = jnp.cumsum(counts) - counts
    pcounts = (counts + MOE_BLOCK - 1) // MOE_BLOCK * MOE_BLOCK
    pends = jnp.cumsum(pcounts)
    pstarts = pends - pcounts
    dest = pstarts[e_sorted] + jnp.arange(n_assign, dtype=jnp.int32) - starts[e_sorted]
    nblk = -(-(n_assign + N_EXPERTS * (MOE_BLOCK - 1)) // MOE_BLOCK)
    rows = nblk * MOE_BLOCK
    row_tok = jnp.full((rows,), nt, jnp.int32).at[dest].set(tok[order])
    row_w = jnp.zeros((rows,), F32).at[dest].set(wts[order])
    blk_e = jnp.minimum(jnp.sum(jnp.arange(nblk)[:, None] * MOE_BLOCK >= pends[None, :], axis=1), N_EXPERTS - 1)
    x_pad = jnp.concatenate([xt, jnp.zeros((1, d), xt.dtype)], axis=0)

    def step(acc, xs):
        rt, rw, e = xs
        y = swiglu(x_pad[rt], wg[e], wu[e], wd[e])
        return acc.at[rt].add(y * rw[:, None].astype(y.dtype)), None

    acc, _ = lax.scan(step, jnp.zeros((nt + 1, d), h.dtype),
                      (row_tok.reshape(nblk, MOE_BLOCK), row_w.reshape(nblk, MOE_BLOCK), blk_e))
    out = acc[:nt] + swiglu(xt, sg, su, sd)
    return out.reshape(b, t, d)

def setup_inputs(seed: int = 0) -> dict:
    key = jax.random.key(seed)
    ks = iter(jax.random.split(key, 40))

    def nrm(shape, std):
        return std * jax.random.normal(next(ks), shape, F32)

    def gain(shape):
        return 1.0 + 0.05 * jax.random.normal(next(ks), shape, F32)

    D = D_MODEL
    dt = jnp.exp(jax.random.uniform(next(ks), (N_EVEN, GDN_HEADS), F32, math.log(1e-3), math.log(1e-1)))
    return {
        'x': nrm((BATCH, SEQ, D), 1.0),
        'c': nrm((BATCH, D), 1.0),
        'ada_w': nrm((DEPTH, D, 6 * D), 0.5 * D ** -0.5),
        'ada_b': nrm((DEPTH, 6 * D), 0.02),
        'norm_mix': gain((DEPTH, D)),
        'norm_ffn': gain((DEPTH, D)),
        'rel_bias': nrm((REL_BUCKETS, NSA_HEADS), 0.2),
        'ev_w_in': nrm((N_EVEN, D, EV_IN), D ** -0.5),
        'ev_w_out': nrm((N_EVEN, EV_OUT, D), EV_OUT ** -0.5),
        'fox_fb': 3.0 + 0.5 * jax.random.normal(next(ks), (N_EVEN, FOX_HEADS), F32),
        'fox_qn': gain((N_EVEN, FOX_DH)),
        'fox_kn': gain((N_EVEN, FOX_DH)),
        'gdn_conv': nrm((N_EVEN, GDN_CONV, 3 * GDN_W), GDN_CONV ** -0.5),
        'gdn_a_log': jnp.log(jax.random.uniform(next(ks), (N_EVEN, GDN_HEADS), F32, 1.0, 16.0)),
        'gdn_dt_bias': dt + jnp.log(-jnp.expm1(-dt)),
        'gdn_on': gain((N_EVEN, GDN_DH)),
        'od_w_in': nrm((N_ODD, D, OD_IN), D ** -0.5),
        'od_w_out': nrm((N_ODD, OD_OUT, D), OD_OUT ** -0.5),
        'nsa_qn': gain((N_ODD, NSA_DH)),
        'nsa_kn': gain((N_ODD, NSA_DH)),
        'nsa_pos': nrm((N_ODD, 2, CMP_LEN, NSA_DH), 0.1),
        'nsa_cmp_w1': nrm((N_ODD, 2, CMP_LEN * NSA_DH, CMP_HIDDEN), (CMP_LEN * NSA_DH) ** -0.5),
        'nsa_cmp_w2': nrm((N_ODD, 2, CMP_HIDDEN, NSA_DH), CMP_HIDDEN ** -0.5),
        'gla_wg_up': nrm((N_ODD, GLA_GATE_RANK, GLA_KW), GLA_GATE_RANK ** -0.5),
        'gla_bg': nrm((N_ODD, GLA_KW), 0.1),
        'gla_on': gain((N_ODD, GLA_DV)),
        'moe_router': nrm((DEPTH, D, N_EXPERTS), D ** -0.5),
        'moe_bias': nrm((DEPTH, N_EXPERTS), 0.01),
        'moe_wg': nrm((DEPTH, N_EXPERTS, D, D_EXPERT), D ** -0.5),
        'moe_wu': nrm((DEPTH, N_EXPERTS, D, D_EXPERT), D ** -0.5),
        'moe_wd': nrm((DEPTH, N_EXPERTS, D_EXPERT, D), D_EXPERT ** -0.5),
        'sh_wg': nrm((DEPTH, D, D_SHARED), D ** -0.5),
        'sh_wu': nrm((DEPTH, D, D_SHARED), D ** -0.5),
        'sh_wd': nrm((DEPTH, D_SHARED, D), D_SHARED ** -0.5),
    }

def reference(x, c, ada_w, ada_b, norm_mix, norm_ffn, rel_bias, ev_w_in, ev_w_out, fox_fb, fox_qn, fox_kn,
              gdn_conv, gdn_a_log, gdn_dt_bias, gdn_on, od_w_in, od_w_out, nsa_qn, nsa_kn, nsa_pos, nsa_cmp_w1,
              nsa_cmp_w2, gla_wg_up, gla_bg, gla_on, moe_router, moe_bias, moe_wg, moe_wu, moe_wd, sh_wg, sh_wu,
              sh_wd):
    cond = jax.nn.silu(c)
    for layer in range(DEPTH):
        mod = (cond @ ada_w[layer] + ada_b[layer])[:, None, :]
        sh1, sc1, g1, sh2, sc2, g2 = jnp.split(mod, 6, axis=-1)
        h = rms_norm(x, norm_mix[layer]) * (1.0 + sc1) + sh1
        j = layer // 2
        if layer % 2 == 0:
            y = even_mixer(h, ev_w_in[j], ev_w_out[j], fox_fb[j], fox_qn[j], fox_kn[j], gdn_conv[j],
                           gdn_a_log[j], gdn_dt_bias[j], gdn_on[j])
        else:
            y = odd_mixer(h, od_w_in[j], od_w_out[j], nsa_qn[j], nsa_kn[j], nsa_pos[j], nsa_cmp_w1[j],
                          nsa_cmp_w2[j], gla_wg_up[j], gla_bg[j], gla_on[j], rel_bias)
        x = x + g1 * y
        h = rms_norm(x, norm_ffn[layer]) * (1.0 + sc2) + sh2
        x = x + g2 * moe_ffn(h, moe_router[layer], moe_bias[layer], moe_wg[layer], moe_wu[layer],
                             moe_wd[layer], sh_wg[layer], sh_wu[layer], sh_wd[layer])
    return x


_drawn_inputs = setup_inputs


def setup_inputs(seed=0):
    import zlib

    import numpy as np

    out = dict(_drawn_inputs(seed))
    spreads = {}
    factors = {'nsa_qn': 4.346, 'nsa_kn': 6.026, 'gla_bg': 2.896, 'rel_bias': 3.13, 'gla_on': 2.801}
    for name, (base, spread) in spreads.items():
        noise = np.random.default_rng([zlib.crc32(name.encode()), seed]).standard_normal(out[name].shape)
        drawn = base * np.exp(spread * noise) if base else spread * noise
        out[name] = jnp.asarray(drawn.astype(out[name].dtype))
    for name, factor in factors.items():
        out[name] = (out[name] * factor).astype(out[name].dtype)
    return out
```

```python
import math
from contextlib import ExitStack

import numpy as np
import concourse.bass as bass
from concourse import mybir

F32 = mybir.dt.float32
ALU = mybir.AluOpType
ACT = mybir.ActivationFunctionType
AX = mybir.AxisListType

P = 128
D = 1024
T = 256
NT = T // P
KT = D // P
LAYERS = 2
EPS = 1e-6
NEG = -1e30
CHUNK = 64
NCH = T // CHUNK
FH, FDH = 8, 64
GH, GD = 4, 128
NH, NDH, NKV = 8, 64, 2
CMP_LEN, CMP_STRIDE = 32, 16
NCMP = (T - CMP_LEN) // CMP_STRIDE + 1
ROW = 2 * T
CHID = 256
LH, LDK, LDV, LRANK = 4, 64, 128, 16
TAU = 16.0
BUCKETS, MAXDIST = 32, 128
E, TOPK, GROUPS, TOPG = 64, 6, 8, 4
FE = 256
ROUTE_SCALE = 2.5
SLOTW = 3 * KT * FE
SLOTS = 3
SC = SLOTW // KT
BODY = SLOTS
PEEL = E % BODY
LEVELS = (1, 2, 4, 8, 16, 32)
INVX = 4 * (len(LEVELS) - 1)

EV_SMALL = FH + 2 * GH
OD_TOK = 2 * NKV * NDH + LH * LDV
OD_GATES = 3 * NH
EV_TILES = 24
OD_TILES = 18


def columns(parts):
    at, where = 0, {}
    for name, width in parts:
        where[name] = (at, at + width)
        at += width
    return where, at


PAR, PARW = columns([
    ("c", KT), ("ada_b", LAYERS * 48), ("norm_mix", LAYERS * KT), ("norm_ffn", LAYERS * KT),
    ("router", LAYERS * KT * E), ("e_bias", LAYERS * E), ("fox_fb", FH), ("fox_qn", 1), ("fox_kn", 1),
    ("conv", 48), ("a_log", GH), ("dt_bias", GH), ("gdn_on", 1), ("nsa_qn", 1), ("nsa_kn", 1),
    ("pos", 2 * 16), ("wg_up", 256), ("bg", 256), ("gla_on", 1), ("rel", NH)])
CST, CSTW = columns([
    ("ident", P), ("ones", P), ("bd", P), ("tri", P), ("ntri", 2 * P), ("maskq", P), ("mpos", P), ("mneg", P),
    ("tril", P), ("levt", 6 * P), ("lev1", P), ("ohr", 512), ("ohf", 512), ("cmask", NT * NCMP), ("eps", 8),
    ("half", 2)])
EPS1, EPS64, EPS128, ONE, ZERO = range(5)


SML, SMALLW = columns([
    ("sml", 2 * 16), ("logf", 16), ("gate", 8), ("z", 32), ("lg", 32), ("beta", 8), ("be", 8), ("gc", 8),
    ("ngc", 8), ("eg", 8), ("ea", 4), ("kdc", 16), ("mx", 12), ("nmx", 12), ("rs", 12), ("rg", 12),
    ("ngate", 48), ("chid", 120), ("kcn", 16), ("csq", 16), ("crms", 16),
    ("m8", 128), ("gs", 16), ("g8", 16), ("e8", 16), ("gm", 16), ("left", 4), ("wsum", 4)])


def constants():
    c = np.zeros((P, CSTW), np.float32)

    def put(name, a):
        c[: a.shape[0], CST[name][0]:CST[name][0] + a.shape[1]] = a

    i, j = np.arange(P)[:, None], np.arange(P)[None, :]
    same = i // CHUNK == j // CHUNK
    put("ident", np.eye(P))
    put("ones", np.ones((P, P)))
    put("bd", (i // 64 == j // 64) * 1.0)
    put("tri", (same & (i <= j)) * 1.0)
    put("ntri", np.concatenate([(i <= j) * -1.0, -np.ones((P, P))], 1))
    put("maskq", np.where(j > i, NEG, 0.0))
    put("mpos", np.where(same & (j <= i), 0.0, -NEG))
    put("mneg", np.where(same & (j >= i), 0.0, NEG))
    put("tril", (same & (j >= i)) * 1.0)

    def level(m):
        return ((i // (2 * m) == j // (2 * m)) & (i // m % 2 == 1) & (j // m % 2 == 0)) * 1.0

    put("levt", np.concatenate([level(m).T for m in LEVELS], 1))
    put("lev1", level(1))
    dist = 255 - np.arange(512)
    exact = BUCKETS // 2
    n = np.maximum(dist, 0)
    large = exact + (np.log(np.maximum(n, 1).astype(np.float32) / np.float32(exact))
                     / np.float32(math.log(MAXDIST / exact)) * np.float32(BUCKETS - exact)).astype(np.int32)
    bucket = np.where(n < exact, n, np.minimum(large, BUCKETS - 1))
    oh = np.zeros((BUCKETS + 1, 512), np.float32)
    oh[bucket, np.arange(512)] = 1.0
    oh[BUCKETS] = np.where(dist < 0, NEG, 0.0)
    put("ohr", oh)
    put("ohf", oh[:, ::-1])
    q = np.arange(T).reshape(NT, P).T
    end = np.arange(NCMP) * CMP_STRIDE + CMP_LEN - 1
    put("cmask", (end[None, None, :] <= q[:, :, None]).reshape(P, -1) * 1.0)
    put("eps", np.tile(np.array([[EPS, 64 * EPS, 128 * EPS, 1.0, 0.0, 0, 0, 0]]), (P, 1)))
    put("half", np.stack([(np.arange(P) < 64), (np.arange(P) >= 64)], 1) * 1.0)
    return c


def mixer_loads():
    names = [f"ada0.{s}" for s in range(4)] + [f"in0.{s}" for s in range(5)]
    names += [f"ada0.{s}" for s in range(4, 8)] + [f"ada1.{s}" for s in range(8)] + ["out0.0", "out0.1"]
    names += [f"in1.{s}" for s in range(5)] + ["cmp.0", "cmp.1", "out1.0", "out1.1"]
    return names


NAMES = mixer_loads()


def width_of(name):
    if name == "in0.0":
        return KT * (FH * FDH + EV_SMALL)
    if name == "in1.1":
        return KT * (OD_GATES + LRANK)
    if name.startswith("cmp"):
        return 16 * CHID + (512 if name == "cmp.0" else 128)
    if name.startswith("out"):
        return KT * 512
    return SLOTW


def program(nc, xT_in, par_in, cst_in, mix_in, moe_in, outT):
    with ExitStack() as ctx:
        def sb(name, shape):
            return ctx.enter_context(nc.sbuf_tensor(name, shape, F32))

        sems = {}

        def S(name):
            if name not in sems:
                sems[name] = ctx.enter_context(nc.semaphore(name))
            return sems[name]

        bank = [ctx.enter_context(nc.psum_tensor(f"bank{i}", [P, 512], F32)) for i in range(8)]
        ring = [sb(f"ring{i}", [P, SLOTW]) for i in range(SLOTS)]
        route_w = [sb(f"route_w{i}", [P, T]) for i in range(SLOTS)]
        par = sb("par_sb", [P, PARW])
        cst = sb("cst_sb", [P, CSTW])
        xT = sb("xT", [P, KT, T])
        hT = sb("hT", [P, KT, T])
        yT = sb("yT", [P, KT, T])
        mod = sb("mod", [P, LAYERS * 48])
        cond = sb("cond", [P, KT])
        gain = sb("gain", [P, KT])
        rms = sb("rms", [P, T])
        feat = sb("feat", [P, EV_TILES, T])
        scr = sb("scr", [P, 48, T])
        relrow = sb("relrow", [NH, 512])
        relc = sb("relc", [P, NT, NCMP, NH])
        small = sb("small", [P, SMALLW])

        def flat(tensor, first, blocks):
            return tensor[:, first:first + blocks, :].rearrange("p a b -> p (a b)")

        def blocks(first, shape):
            n = int(np.prod(shape))
            letters = "abcd"[:len(shape)]
            dims = " ".join(letters)
            return flat(scr, first, -(-n // T))[:, 0:n].rearrange(
                f"p ({dims}) -> p {dims}", **dict(zip(letters, shape)))

        def sl(name, shape):
            lo, hi = SML[name]
            letters = "abcd"[:len(shape)]
            dims = " ".join(letters)
            return small[:, lo:hi].rearrange(f"p ({dims}) -> p {dims}", **dict(zip(letters, shape)))

        sml = sl("sml", (NT, EV_SMALL))
        logf = sl("logf", (NT, FH))
        gate = sl("gate", (NT, GH))
        qpad = blocks(0, (FH, T))
        vpad = blocks(8, (NT, FH, P))
        prob = [blocks(16 + i, (T,)) for i in range(2)]
        probT = [blocks(18 + i, (T,)) for i in range(2)]
        conv = blocks(20, (12, T))
        frms = blocks(32, (8, T))
        squares = blocks(40, (8, T))
        vb, kbe = blocks(0, (NT, GH, P)), blocks(4, (NT, GH, P))
        kd = [blocks(8, (NT, GH, P)), blocks(12, (NT, GH, P))]
        state, vnew = blocks(16, (GH, P)), blocks(18, (GH, P))
        Eb, Dm, DT = (blocks(b, (NT, GH, P)) for b in (20, 24, 28))
        Am, attnT = Dm, DT
        X, XT = blocks(32, (NT, GH, P)), blocks(36, (NT, GH, P))
        ATm = [blocks(40, (NT, GH, P)), blocks(44, (NT, GH, P))]
        og, osq = blocks(32, (GH, T)), blocks(36, (GH, T))
        orms = blocks(40, (GH, T))

        def feat4(first):
            return flat(feat, first, 4).rearrange("p (a b c) -> p a b c", a=NT, b=GH)

        Pm, AT, u_sb, wT = feat4(0), feat4(4), feat4(12), feat4(16)
        nvpad = blocks(8, (NT, 2, NKV, P))
        vcpad = blocks(12, (NKV, P))
        lgT = blocks(13, (T,))
        Brel = blocks(16, (NT, NH, T))
        nrms = blocks(32, (6, T))
        npr = blocks(32, (2, 640))
        npT = blocks(37, (2, 640))
        nprob = [npr[:, i, :] for i in range(2)]
        nprobT = [npT[:, i, :] for i in range(2)]
        blk = blocks(42, (2, 16, NKV * NCMP))
        chid = sl("chid", (2, 2, NKV * NCMP))
        kcn = sl("kcn", (16,))[:, 0:NCMP]
        csq = sl("csq", (16,))[:, 0:NCMP]
        toks = flat(feat, 18, 4).rearrange("p (a b) -> p a b", a=NT)
        lz, loga = blocks(46, (NT, T)), blocks(14, (NT, T))
        G, EG, EnG, edG = (blocks(b, (2, T)) for b in (0, 2, 4, 6))
        lki, lkd = blocks(8, (2, T)), blocks(10, (2, T))
        lqd, lkt = blocks(16, (LH, T)), blocks(20, (2, NT, 2, P))
        lattn, lstate = blocks(24, (NT, LH, P)), blocks(28, (LH, P))
        rscore, rbias = blocks(10, (NT, E)), blocks(11, (NT, E))
        rbuf = [blocks(14 + i, (NT, E)) for i in range(4)]
        act = [blocks(2 * i, (2, T)) for i in range(4)]
        silu_g = blocks(8, (2, T))
        wroute = blocks(12, (NT, E))
        wTs = blocks(13, (T,))

        w_dram = [nc.dram_tensor(f"route{l}", [E, T], F32) for l in range(LAYERS)]
        rel_dram = nc.dram_tensor("rel_rows", [NH, P * (ROW + 1)], F32)

        def pr(name, a=0, b=None):
            lo, hi = PAR[name]
            return par[:, lo + a:(hi if b is None else lo + b)]

        def cs(name, a=0, b=None):
            lo, hi = CST[name]
            return cst[:, lo + a:(hi if b is None else lo + b)]

        def eps(k):
            return cs("eps", k, k + 1)

        ident, ones = cs("ident"), cs("ones")

        order = [("mix", n) for n in NAMES[:NAMES.index("in1.0")]] + [("shared", 0), ("experts", 0)]
        order += [("mix", n) for n in NAMES[NAMES.index("in1.0"):]] + [("shared", 1), ("experts", 1)]
        place, n_load, landed = {}, 0, [0] * SLOTS
        for key in order:
            slot = n_load % SLOTS
            if key[0] == "experts":
                first = [landed[(n_load + e) % SLOTS] + 32 * (e // SLOTS + 1) for e in range(E)]
                place[key] = (n_load, first)
                for e in range(E):
                    landed[(n_load + e) % SLOTS] += 32
                n_load += E
            else:
                landed[slot] += 16
                place[key] = (n_load, landed[slot])
                n_load += 1

        def slot_of(key):
            return ring[place[key][0] % SLOTS]

        block = ctx.enter_context(nc.Block())

        @block.sync
        def _(sp):
            sp.dma_start(par[:, :], par_in).then_inc(S("params_landed"), 16)
            sp.dma_start(cst[:, :], cst_in).then_inc(S("params_landed"), 16)
            sp.dma_start(xT[:, :, :], xT_in).then_inc(S("x_landed"), 16)

            adas = [n for n in NAMES if n.startswith("ada")]

            def released(key, e=0):
                if key[0] == "experts":
                    return "expert_used", key[1] * (E + 1) + e + 2
                if key[0] == "shared":
                    return "expert_used", key[1] * (E + 1) + 1
                name = key[1]
                layer, s = int(name[-3]) if name[0] != "c" else 1, int(name[-1])
                if name.startswith("ada"):
                    return "ada_used", adas.index(name) + 1
                if name.startswith("in0"):
                    return ("tok_ready", 1) if s == 0 else ("feat_ready", 6 * s)
                if name.startswith("in1"):
                    return [("tok_half", 1), ("tok_ready", 2)][s] if s < 2 else ("feat_ready", EV_TILES + 6 * (s - 1))
                if name.startswith("out"):
                    return "proj_ready", KT * layer + 4 * (s + 1)
                return "cmp_o", s + 1

            loads = []
            for key in order:
                loads += [(key, e) for e in range(E)] if key[0] == "experts" else [(key, 0)]

            def await_slot(n):
                if n >= SLOTS:
                    name, value = released(*loads[n - SLOTS])
                    sp.wait_ge(S(name), value)

            def stream(key):
                n = place[key][0]
                await_slot(n)
                if key[0] == "mix":
                    w = width_of(key[1])
                    src = mix_in[NAMES.index(key[1]), :, 0:w]
                else:
                    w, src = SLOTW, moe_in[key[1] * (E + 1), :, :]
                sp.dma_start(ring[n % SLOTS][:, 0:w], src).then_inc(S(f"slot_full{n % SLOTS}"), 16)

            def stream_experts(layer):
                n = place["experts", layer][0]

                def load_expert(e, r):
                    sp.dma_start(ring[r][:, :], moe_in[bass.ds(e + layer * (E + 1) + 1, 1), :, :]
                                 .rearrange("a p n -> (a p) n")).then_inc(S(f"slot_full{r}"), 16)

                def load_route(e, r):
                    sp.dma_start(route_w[r][:, :], w_dram[layer].ap()[bass.ds(e, 1), :].to_broadcast([P, T])
                                 ).then_inc(S(f"slot_full{r}"), 16)

                for e in range(SLOTS):
                    await_slot(n + e)
                    load_expert(e, (n + e) % SLOTS)
                sp.wait_ge(S("route_stored"), 16 * (layer + 1))
                for e in range(SLOTS):
                    load_route(e, (n + e) % SLOTS)
                for e in range(SLOTS, PEEL + BODY):
                    await_slot(n + e)
                    load_expert(e, (n + e) % SLOTS)
                    load_route(e, (n + e) % SLOTS)
                with sp.Fori(1, E // BODY) as step:
                    for k in range(BODY):
                        sp.wait_ge(S("expert_used"), step * BODY + (layer * (E + 1) + PEEL + k - SLOTS + 2))
                        load_expert(step * BODY + (PEEL + k), (n + PEEL + k) % SLOTS)
                        load_route(step * BODY + (PEEL + k), (n + PEEL + k) % SLOTS)

            for key in order:
                if key == ("mix", "out0.0"):
                    sp.wait_ge(S("rel_copied"), 2)
                    dst = bass.AP(rel_dram, 0, [[P * (ROW + 1), NH], [ROW + 1, P], [1, ROW]])
                    sp.dma_start(dst, relrow[:, :].unsqueeze(1).to_broadcast([NH, P, ROW])
                                 ).then_inc(S("rel_stored"), 16)
                if key == ("mix", "in1.2"):
                    sp.wait_ge(S("rel_stored"), 16)
                    sp.wait_ge(S("y_ready"), 2)
                    sp.wait_ge(S("gdn_o"), NCH)
                    for t in range(NT):
                        src = bass.AP(rel_dram, 255 - P * t, [[ROW, P], [P * (ROW + 1), NH], [1, T]])
                        sp.dma_start(Brel[:, t, :, :], src).then_inc(S("brel_landed"), 16)
                if key[0] == "experts":
                    stream_experts(key[1])
                else:
                    stream(key)
            for m in range(KT):
                sp.wait_ge(S("x_added"), 3 * KT + m + 1)
                sp.dma_start(outT[:, m, :], xT[:, m, :]).then_inc(S("out_stored"), 16)
            sp.wait_ge(S("out_stored"), 16 * KT)

        @block.tensor
        def _(pe):
            def mm(out, lhsT, rhs, start, stop):
                return pe.matmul(out, lhsT, rhs, start=start, stop=stop)

            def tr(out, in_):
                return pe.transpose(out, in_, ident)

            def full(key):
                n, value = place[key]
                pe.wait_ge(S(f"slot_full{n % SLOTS}"), value)
                return slot_of(key)

            def modulation(layer, s):
                w = full(("mix", f"ada{layer}.{s}"))[:, :].rearrange("p (k n) -> p k n", k=KT)
                for m in range(6):
                    col = 48 * layer + 6 * s + m
                    for k in range(KT):
                        last = mm(bank[7][:, col:col + 1], w[:, k, m * P:(m + 1) * P], cond[:, k:k + 1],
                                  k == 0, k == KT - 1)
                last.then_inc(S("ada_used"), 1)

            def feature_sum(n):
                pe.wait_ge(S("sq_ready"), n)
                for k in range(KT):
                    last = mm(bank[4][:, 0:T], ones, yT[:, k, :], k == 0, k == KT - 1)
                last.then_inc(S("ss_ready"), 1)

            def project_tokens(w, c0, c1, dst):
                for t in range(NT):
                    for k in range(KT):
                        last = mm(dst[t], hT[:, k, t * P:(t + 1) * P], w[:, k, c0:c1], k == 0, k == KT - 1)
                return last

            def project_features(w, tiles, j0, first_tile):
                for m in range(tiles):
                    j = j0 + m
                    if j >= 3:
                        pe.wait_ge(S("feat_copied"), first_tile + j - 2)
                    for k in range(KT):
                        last = mm(bank[4 + j % 3][:, 0:T], w[:, k, m * P:(m + 1) * P], hT[:, k, :],
                                  k == 0, k == KT - 1)
                    last.then_inc(S("feat_ready"), 1)

            def out_projection(layer):
                pe.wait_ge(S("y_ready"), 2 * (layer + 1))
                pe.wait_ge(S("fox_o" if layer == 0 else "nsa_o"), 4)
                for s in range(2):
                    w = full(("mix", f"out{layer}.{s}"))[:, 0:KT * 512].rearrange("p (k n) -> p k n", k=KT)
                    for m in range(4):
                        j = 4 * s + m
                        if j >= 4:
                            pe.wait_ge(S("x_added"), 2 * KT * layer + j - 3)
                        for k in range(KT):
                            last = mm(bank[j % 4][:, 0:T], w[:, k, m * P:(m + 1) * P], yT[:, k, :],
                                      k == 0, k == KT - 1)
                        last.then_inc(S("proj_ready"), 1)

            def head_sums(weights, sq, tiles, banks):
                for b in range(tiles // 2):
                    last = mm(bank[banks[b]][:, :], weights, sq[:, 2 * b:2 * b + 2, :], True, True)
                return last

            def expert_up(w, ft, gu_bank):
                for part in range(2):
                    for k in range(KT):
                        c = part * KT * FE + k * FE + ft * P
                        last = mm(gu_bank[:, part * T:(part + 1) * T], w[:, c:c + P], hT[:, k, :],
                                  k == 0, k == KT - 1)
                last.then_inc(S("gu_ready"), 1)

            def expert_down(w, ft, a, open_banks):
                for m in range(KT):
                    c = 2 * KT * FE + ft * D + m * P
                    first = open_banks and ft == 0 and m % 2 == 0
                    last = pe.matmul(bank[m // 2][:, (m % 2) * T:(m % 2 + 1) * T], w[:, c:c + P], a[:, ft, :],
                                     start=first, stop=first, skip_group_check=not first)
                return last

            def moe(layer):
                base = layer * 2 * (E + 1)
                feature_sum(2 * layer + 2)
                pe.wait_ge(S("h_ready"), 2 * layer + 2)
                for t in range(NT):
                    for k in range(KT):
                        last = mm(bank[6][:, t * E:(t + 1) * E], hT[:, k, t * P:(t + 1) * P],
                                  pr("router")[:, (layer * KT + k) * E:(layer * KT + k + 1) * E],
                                  k == 0, k == KT - 1)
                last.then_inc(S("router_ready"), 1)
                w = full(("shared", layer))
                for ft in range(2):
                    expert_up(w, ft, bank[4 + ft])
                for ft in range(2):
                    pe.wait_ge(S("a_ready"), base + ft + 1)
                    last = expert_down(w, ft, act[BODY], True)
                last.then_inc(S("expert_used"), 1)
                pe.wait_ge(S("route_ready"), layer + 1)
                for t in range(NT):
                    last = tr(bank[7][0:E, t * P:(t + 1) * P], wroute[:, t, :])
                last.then_inc(S("route_turned"), 1)
                n, first = place["experts", layer]

                def expert(r, value, base_a, a):
                    pe.wait_ge(S(f"slot_full{r}"), value)
                    for ft in range(2):
                        expert_up(ring[r], ft, bank[4 + ft])
                    for ft in range(2):
                        pe.wait_ge(S("a_ready"), base_a + ft + 1)
                        last = expert_down(ring[r], ft, a, False)
                    last.then_inc(S("expert_used"), 1)

                for e in range(PEEL):
                    expert((n + e) % SLOTS, first[e], base + 2 * (e + 1), act[BODY])
                with pe.Fori(0, E // BODY) as step:
                    for k in range(BODY):
                        e = PEEL + k
                        expert((n + e) % SLOTS, step * 32 + first[e], step * (2 * BODY) + (base + 2 * (e + 1)), act[k])

            pe.wait_ge(S("params_landed"), 32)
            pe.wait_ge(S("cond_ready"), 1)
            for s in range(4):
                modulation(0, s)
            feature_sum(1)
            pe.wait_ge(S("h_ready"), 1)
            w = full(("mix", "in0.0"))[:, 0:KT * (FH * FDH + EV_SMALL)].rearrange("p (k n) -> p k n", k=KT)
            project_tokens(w, 0, FH * FDH, [bank[0][:, :], bank[1][:, :]])
            project_tokens(w, FH * FDH, FH * FDH + EV_SMALL, [bank[2][:, 0:16], bank[3][:, 0:16]]
                           ).then_inc(S("tok_ready"), 1)
            for s in range(4):
                w = full(("mix", f"in0.{s + 1}"))[:, :].rearrange("p (k n) -> p k n", k=KT)
                project_features(w, 6, 6 * s, 0)

            pe.wait_ge(S("tok_copied"), 6)
            rel = pr("rel")[0:BUCKETS + 1, :]
            mm(bank[0][0:NH, :], rel, cs("ohr")[0:BUCKETS + 1, :], True, True)
            for t in range(NT):
                for n in range(NCMP):
                    d0 = 256 + P * t - CMP_STRIDE * n - CMP_LEN + 1
                    last = mm(bank[1][:, (t * NCMP + n) * NH:(t * NCMP + n + 1) * NH],
                              cs("ohf")[0:BUCKETS + 1, d0:d0 + P], rel, True, True)
            last.then_inc(S("rel_ready"), 1)

            pe.wait_ge(S("rel_copied"), 2)
            pe.wait_ge(S("fox_sq"), 4)
            head_sums(cs("bd"), yT, 8, [0, 1, 2, 3]).then_inc(S("fox_ss"), 1)
            pe.wait_ge(S("fox_qk"), 3)
            pe.wait_ge(S("logf_ready"), 1)

            units = [(h0 + i, qt) for h0 in range(0, FH, 2) for qt in range(NT) for i in range(2)]

            def fox_scores(u):
                h, qt = units[u]
                keys = P * (qt + 1)
                if u >= 2:
                    pe.wait_ge(S("fox_exp"), u - 1)
                s = bank[u % 2]
                mm(s[:, 0:keys], qpad[:, h, qt * P:(qt + 1) * P], feat[:, 4 + h // 2, 0:keys], True, False)
                mm(s[:, qt * P:(qt + 1) * P], ident, cs("maskq"), False, False)
                last = mm(s[:, 0:keys], logf[:, 0, h:h + 1].to_broadcast([P, P]), cs("ntri")[:, 0:keys],
                          False, qt == 0)
                if qt:
                    last = mm(s[:, P:2 * P], logf[:, 1, h:h + 1].to_broadcast([P, P]), cs("ntri")[:, 0:P],
                              False, True)
                last.then_inc(S("fox_s"), 1)

            def fox_turn(u):
                h, qt = units[u]
                pe.wait_ge(S("fox_p"), u + 1)
                if u >= 2:
                    pe.wait_ge(S("fox_pT"), u - 1)
                for k in range(qt + 1):
                    last = tr(bank[2 + u % 2][:, k * P:(k + 1) * P], prob[u % 2][:, k * P:(k + 1) * P])
                last.then_inc(S("fox_turned"), 1)

            def fox_values(u):
                h, qt = units[u]
                pe.wait_ge(S("fox_pT"), u + 1)
                if u % 4 == 0 and u >= 8:
                    pe.wait_ge(S("fox_o"), u // 4 - 1)
                for k in range(qt + 1):
                    last = mm(bank[4 + u // 4 % 2][:, qt * P:(qt + 1) * P], vpad[:, k, h, :],
                              probT[u % 2][:, k * P:(k + 1) * P], h % 2 == 0 and k == 0, h % 2 == 1 and k == qt)
                last.then_inc(S("fox_pv"), 1)

            rest = [(0, s) for s in range(4, 8)] + [(1, s) for s in range(8)]
            pe.wait_ge(S("mod_copied"), 1)
            for u in range(len(units) + 2):
                if u < len(units):
                    fox_scores(u)
                if 1 <= u <= len(units):
                    fox_turn(u - 1)
                if u >= 2:
                    fox_values(u - 2)
                if u < len(rest):
                    modulation(*rest[u])

            pe.wait_ge(S("gdn_sq"), 4)
            pe.wait_ge(S("fox_pT"), len(units))
            head_sums(ones, squares, 8, [0, 1, 2, 3]).then_inc(S("gdn_ss"), 1)
            pe.wait_ge(S("gdn_g"), 1)
            for t in range(NT):
                last = mm(bank[6][:, t * GH:(t + 1) * GH], cs("tri"), gate[:, t, :], True, True)
            last.then_inc(S("gdn_cum"), 1)
            pe.wait_ge(S("gdn_qk"), 4)
            pe.wait_ge(S("gdn_rms"), 4)
            pe.wait_ge(S("fox_o"), 4)
            for t in range(NT):
                for h in range(GH):
                    cols = slice(h * P, (h + 1) * P)
                    g = gate[:, t, h:h + 1].to_broadcast([P, P])
                    mm(bank[3 * t][:, cols], g, cs("tri"), True, True)
                    mm(bank[3 * t + 1][:, cols], g, cs("tri"), True, False)
                    mm(bank[3 * t + 1][:, cols], ident, cs("mpos"), False, True)
                    mm(bank[3 * t + 2][:, cols], g, cs("tri"), True, False)
                    last = mm(bank[3 * t + 2][:, cols], ident, cs("mneg"), False, True)
            last.then_inc(S("gdn_gb"), 1)
            pe.wait_ge(S("gdn_gc"), 2)
            pe.wait_ge(S("mod_copied"), 2)
            for t in range(NT):
                for h in range(GH):
                    k = feat[:, 12 + h, t * P:(t + 1) * P]
                    last = mm(bank[6 + t][:, h * P:(h + 1) * P], k, k, True, True)
            last.then_inc(S("gdn_kk"), 1)
            pe.wait_ge(S("gdn_decay"), 18)
            for t in range(NT):
                for h in range(GH):
                    k = feat[:, 12 + h, t * P:(t + 1) * P]
                    mm(bank[t][:, h * P:(h + 1) * P], k, feat[:, 8 + h, t * P:(t + 1) * P], True, True)
                    tr(bank[2 + t][:, h * P:(h + 1) * P], k)
                    last = tr(bank[4 + t][:, h * P:(h + 1) * P], feat[:, 16 + h, t * P:(t + 1) * P])
            last.then_inc(S("gdn_turned"), 1)
            pe.wait_ge(S("gdn_a"), 8)
            for t in range(NT):
                for h in range(GH):
                    last = tr(bank[6 + t][:, h * P:(h + 1) * P], Am[:, t, h, :])
            last.then_inc(S("gdn_at"), 1)
            pe.wait_ge(S("gdn_kv"), 8)
            pe.wait_ge(S("gdn_attn"), 2)
            for lv in range(1, len(LEVELS)):
                pe.wait_ge(S("inv_x"), 2 + 4 * (lv - 1))
                pe.wait_ge(S("inv_atm"), lv)
                for t in range(NT):
                    for h in range(GH):
                        last = mm(bank[t][:, h * P:(h + 1) * P], ATm[lv % 2][:, t, h, :], X[:, t, h, :],
                                  True, True)
                last.then_inc(S("inv_p"), 1)
                pe.wait_ge(S("inv_pc"), 2 * lv)
                for t in range(NT):
                    for h in range(GH):
                        cols = slice(h * P, (h + 1) * P)
                        if lv < len(LEVELS) - 1:
                            mm(bank[2 + t][:, cols], XT[:, t, h, :], Pm[:, t, h, :], True, True)
                        last = mm(bank[4 + t][:, cols], Pm[:, t, h, :], XT[:, t, h, :], True, True)
                last.then_inc(S("inv_xp"), 1)
            pe.wait_ge(S("inv_x"), INVX)
            for t in range(NT):
                for h in range(GH):
                    cols = slice(h * P, (h + 1) * P)
                    mm(bank[6 + t][:, cols], XT[:, t, h, :], vb[:, t, h, :], True, True)
                    last = mm(bank[t][:, cols], kbe[:, t, h, :], XT[:, t, h, :], True, True)
            last.then_inc(S("gdn_uw"), 1)
            for n in range(NCH):
                t, half = n // 2, n % 2
                c0 = half * CHUNK
                if n:
                    pe.wait_ge(S("gdn_state"), 1 + GH * (n - 1))
                    pe.wait_ge(S("gdn_uwc"), 4)
                    for h in range(GH):
                        last = mm(bank[2][:, h * P:(h + 1) * P], wT[:, t, h, :], state[:, h, :], True, True)
                    last.then_inc(S("gdn_ws"), 1)
                pe.wait_ge(S("gdn_vn"), n + 1)
                if n < NCH - 1:
                    for h in range(GH):
                        last = mm(bank[4][:, h * P:(h + 1) * P], kd[half][:, t, h, :], vnew[:, h, :], True, True)
                    last.then_inc(S("gdn_su"), 1)
                if n:
                    pe.wait_ge(S("gdn_oc"), n)
                    pe.wait_ge(S("gdn_qd"), 2)
                for h in range(GH):
                    o = bank[3][:, h * CHUNK:(h + 1) * CHUNK]
                    if n:
                        mm(o, state[:, h, :], feat[:, 8 + h, t * P + c0:t * P + c0 + CHUNK], True, False)
                    last = mm(o, vnew[:, h, :], attnT[:, t, h, c0:c0 + CHUNK], n == 0, True)
                last.then_inc(S("gdn_o"), 1)
            pe.wait_ge(S("og_sq"), 2)
            for b in range(2):
                last = mm(bank[5 + b][:, :], ones, osq[:, 2 * b:2 * b + 2, :], True, True)
            last.then_inc(S("og_ss"), 1)
            out_projection(0)
            moe(0)

            feature_sum(3)
            pe.wait_ge(S("h_ready"), 3)
            w = full(("mix", "in1.0"))[:, :].rearrange("p (k n) -> p k n", k=KT)
            project_tokens(w, 0, 512, [bank[0][:, :], bank[1][:, :]])
            project_tokens(w, 512, OD_TOK, [bank[2][:, 0:256], bank[3][:, 0:256]]).then_inc(S("tok_half"), 1)
            w = full(("mix", "in1.1"))[:, 0:KT * (OD_GATES + LRANK)].rearrange("p (k n) -> p k n", k=KT)
            project_tokens(w, 0, OD_GATES, [bank[2][:, 256:256 + OD_GATES], bank[3][:, 256:256 + OD_GATES]])
            for k in range(KT):
                last = mm(bank[7][0:LRANK, 0:T], w[:, k, OD_GATES:OD_GATES + LRANK], hT[:, k, :],
                          k == 0, k == KT - 1)
            last.then_inc(S("tok_ready"), 1)
            for s in range(3):
                w = full(("mix", f"in1.{s + 2}"))[:, :].rearrange("p (k n) -> p k n", k=KT)
                project_features(w, 6, 6 * s, EV_TILES)
            pe.wait_ge(S("tok_copied"), 17)
            for t in range(NT):
                last = mm(bank[0][:, t * 256:(t + 1) * 256], lgT[0:LRANK, t * P:(t + 1) * P],
                          pr("wg_up")[0:LRANK, :], True, True)
            last.then_inc(S("gla_z"), 1)
            pe.wait_ge(S("cmp_blk"), 8)
            for kv in range(2):
                w = full(("mix", f"cmp.{kv}"))
                for ht in range(2):
                    for l in range(16):
                        last = mm(bank[2 + kv][:, ht * 32:ht * 32 + 2 * NCMP],
                                  w[:, l * CHID + ht * P:l * CHID + (ht + 1) * P], blk[:, kv, l, :],
                                  l == 0, l == 15)
                last.then_inc(S("cmp_h"), 1)
            for kv in range(2):
                w = full(("mix", f"cmp.{kv}"))
                pe.wait_ge(S("cmp_a"), kv + 1)
                if kv == 0:
                    for n, (ht, g) in enumerate([(a, b) for a in range(2) for b in range(2)]):
                        c = 16 * CHID + (ht * 2 + g) * P
                        last = mm(bank[2][:, 256:256 + NCMP], w[:, c:c + P],
                                  chid[:, kv, ht, g * NCMP:(g + 1) * NCMP], n == 0, n == 3)
                else:
                    for g in range(NKV):
                        for ht in range(2):
                            c = 16 * CHID + ht * NDH
                            last = mm(bank[3][0:NCMP, 256 + g * NDH:256 + (g + 1) * NDH],
                                      chid[:, kv, ht, g * NCMP:(g + 1) * NCMP], w[:, c:c + NDH],
                                      ht == 0, ht == 1)
                last.then_inc(S("cmp_o"), 1)
            pe.wait_ge(S("nsa_sq"), 3)
            pe.wait_ge(S("feat_copied"), EV_TILES + OD_TILES)
            for b in range(3):
                mm(bank[4 + b][:, :], cs("bd"), yT[:, 2 * b:2 * b + 2, :], True, True)
            pe.wait_ge(S("cmp_sq"), 1)
            mm(bank[7][:, 0:NCMP], cs("bd"), csq[:, :], True, True).then_inc(S("nsa_ss"), 1)
            pe.wait_ge(S("nsa_qk"), 4)
            pe.wait_ge(S("cmp_kv"), 3)
            pe.wait_ge(S("nsa_rms"), 4)
            pe.wait_ge(S("gla_zc"), 1)

            nunits = [(h0 + i, qt) for h0 in range(4) for qt in range(NT) for i in (0, 4)]

            def nsa_scores(u):
                h, qt = nunits[u]
                keys = P * (qt + 1)
                if u >= 2:
                    pe.wait_ge(S("nsa_b"), 2 * (u - 1))
                q = qpad[:, h, qt * P:(qt + 1) * P]
                for br in range(2):
                    mm(bank[u % 2][:, br * T:br * T + keys], q, feat[:, 4 + br, 0:keys], True, True)
                if u:
                    pe.wait_ge(S("nsa_b"), 2 * u)
                mm(bank[6][:, 0:NCMP], q, kcn[:, :], True, True).then_inc(S("nsa_s"), 1)

            def nsa_turn(u):
                h, qt = nunits[u]
                pe.wait_ge(S("nsa_p"), 3 * (u + 1))
                if u >= 2:
                    pe.wait_ge(S("nsa_pT"), 2 * (u - 1))
                for br in range(2):
                    for k in range(qt + 1):
                        c = br * T + k * P
                        tr(bank[2 + u % 2][:, c:c + P], nprob[u % 2][:, c:c + P])
                if u:
                    pe.wait_ge(S("nsa_pT"), 2 * u)
                tr(bank[7][0:NCMP, 0:P], nprob[u % 2][:, 512:512 + NCMP]
                   ).then_inc(S("nsa_turned"), 1)

            def nsa_values(u):
                h, qt = nunits[u]
                g = h // 4
                pe.wait_ge(S("nsa_pT"), 2 * (u + 1))
                if u % 4 == 0 and u >= 8:
                    pe.wait_ge(S("nsa_o"), u // 4 - 1)
                out = bank[4 + u // 4 % 2][:, qt * P:(qt + 1) * P]
                mm(out, vcpad[0:NCMP, g, :], nprobT[u % 2][0:NCMP, 512:512 + P], g == 0, False)
                for br in range(2):
                    for k in range(qt + 1):
                        c = br * T + k * P
                        last = mm(out, nvpad[:, k, br, g, :], nprobT[u % 2][:, c:c + P], False,
                                  g == 1 and br == 1 and k == qt)
                last.then_inc(S("nsa_pv"), 1)

            for u in range(len(nunits) + 2):
                if u < len(nunits):
                    nsa_scores(u)
                if 1 <= u <= len(nunits):
                    nsa_turn(u - 1)
                if u >= 2:
                    nsa_values(u - 2)

            pe.wait_ge(S("gla_loga"), 1)
            pe.wait_ge(S("nsa_pT"), 2 * len(nunits))
            pe.wait_ge(S("nsa_o"), 4)
            for f in range(2):
                for t in range(NT):
                    last = mm(bank[0][:, (f * NT + t) * P:(f * NT + t + 1) * P], loga[:, t, f * P:(f + 1) * P],
                              cs("tri"), True, True)
            last.then_inc(S("gla_G"), 1)
            pe.wait_ge(S("gla_qk"), 4)
            for t in range(NT):
                for h in range(LH):
                    last = mm(bank[1 + t][:, h * P:(h + 1) * P], lki[:, h // 2, t * P:(t + 1) * P],
                              lqd[:, h, t * P:(t + 1) * P], True, True)
            for t in range(NT):
                for f in range(2):
                    last = tr(bank[3][:, (t * 2 + f) * P:(t * 2 + f + 1) * P], lkd[:, f, t * P:(t + 1) * P])
            last.then_inc(S("gla_at"), 1)
            pe.wait_ge(S("gla_ready"), 4)
            for n in range(NCH):
                t, half = n // 2, n % 2
                c0 = t * P + half * CHUNK
                if n:
                    pe.wait_ge(S("gla_state"), 1 + LH * (n - 1))
                if n < NCH - 1:
                    for h in range(LH):
                        last = mm(bank[5][:, h * P:(h + 1) * P], lkt[:, half, t, h // 2, :],
                                  toks[:, t, h * P:(h + 1) * P], True, True)
                    last.then_inc(S("gla_su"), 1)
                if n:
                    pe.wait_ge(S("gla_oc"), n)
                for h in range(LH):
                    o = bank[6][:, h * CHUNK:(h + 1) * CHUNK]
                    if n:
                        mm(o, lstate[:, h, :], lqd[:, h, c0:c0 + CHUNK], True, False)
                    last = mm(o, toks[:, t, h * P:(h + 1) * P],
                              lattn[:, t, h, half * CHUNK:(half + 1) * CHUNK], n == 0, True)
                last.then_inc(S("gla_o"), 1)
            pe.wait_ge(S("og_sq"), 4)
            for b in range(2):
                last = mm(bank[1 + b][:, :], ones, osq[:, 2 * b:2 * b + 2, :], True, True)
            last.then_inc(S("og_ss"), 1)
            out_projection(1)
            moe(1)

        @block.scalar
        def _(sc):
            count = [0]

            def act(out, in_, func, name=None, **kw):
                kw.setdefault("bias", eps(ZERO)[0:out.shape[0], :])
                ins = sc.activation(out, in_, func, **kw)
                if name is None:
                    count[0] += 1
                    ins.then_inc(S("act_chain"), 1)
                    sc.wait_ge(S("act_chain"), count[0])
                else:
                    ins.then_inc(S(name), 1)

            def copy(out, in_, name):
                sc.activation(out, in_, ACT.Copy).then_inc(S(name), 1)

            def rms_root(n):
                sc.wait_ge(S("ss_ready"), n)
                act(rms[:, :], bank[4][:, 0:T], ACT.Sqrt, "rms_root", scale=1.0 / D, bias=eps(EPS1))

            def log_part(x, out, name):
                act(out, x, ACT.Abs)
                act(out, out, ACT.Exp, scale=-1.0)
                act(out, out, ACT.Ln, name, bias=eps(ONE))

            def copy_features(first, tiles):
                for j in range(first, first + tiles):
                    sc.wait_ge(S("feat_ready"), j + 1)
                    copy(feat[:, j - first, :], bank[4 + (j - first) % 3][:, 0:T], "feat_copied")

            def moe(layer):
                base = layer * 2 * (E + 1)
                rms_root(2 * layer + 2)
                sc.wait_ge(S("router_ready"), layer + 1)
                act(rscore, bank[6][:, 0:NT * E].rearrange("p (a b) -> p a b", a=NT), ACT.Sigmoid, "score_ready")

                def silu(value, ft):
                    sc.wait_ge(S("gu_ready"), value)
                    act(silu_g[:, ft, :], bank[4 + ft][:, 0:T], ACT.Silu, "silu_ready")

                for ft in range(2):
                    silu(base + ft + 1, ft)
                sc.wait_ge(S("route_turned"), layer + 1)
                copy(wTs[0:E, :], bank[7][0:E, 0:T], "route_copied")
                sc.wait_ge(S("route_copied"), layer + 1)
                sc.dma_start(w_dram[layer].ap(), wTs[0:E, :]).then_inc(S("route_stored"), 16)
                for e in range(PEEL):
                    for ft in range(2):
                        silu(base + 2 * (e + 1) + ft + 1, ft)
                with sc.Fori(0, E // BODY) as step:
                    for k in range(BODY):
                        for ft in range(2):
                            silu(step * (2 * BODY) + (base + 2 * (PEEL + k + 1) + ft + 1), ft)

            sc.wait_ge(S("params_landed"), 32)
            act(cond[:, :], pr("c"), ACT.Silu, "cond_ready")
            act(sl("ea", (GH,)), pr("a_log"), ACT.Exp, "ea_ready")
            rms_root(1)
            sc.wait_ge(S("pads_zero"), 2)
            sc.wait_ge(S("tok_ready"), 1)
            for t in range(NT):
                v = bank[t][:, :].rearrange("p (h d) -> p h d", d=FDH)
                for odd in range(2):
                    copy(vpad[:, t, odd::2, odd * FDH:(odd + 1) * FDH], v[:, odd::2, :], "tok_copied")
                copy(sml[:, t, :], bank[2 + t][:, 0:EV_SMALL], "tok_copied")
            copy_features(0, EV_TILES)
            z, lg = sl("z", (NT, EV_SMALL)), sl("lg", (NT, EV_SMALL))
            sc.wait_ge(S("z_ready"), 3)
            act(sl("beta", (NT, GH)), z[:, :, FH + GH:EV_SMALL], ACT.Sigmoid, "beta_ready")
            log_part(z[:, :, 0:FH + GH], lg[:, :, 0:FH + GH], "lg_ready")
            sc.wait_ge(S("rel_ready"), 1)
            copy(relrow[:, :], bank[0][0:NH, :], "rel_copied")
            copy(relc[:, :, :, :].rearrange("p a b c -> p (a b c)"), bank[1][:, 0:NT * NCMP * NH], "rel_copied")
            for b in range(4):
                sc.wait_ge(S("fox_ss"), 1)
                act(frms[:, 2 * b:2 * b + 2, :].rearrange("p a b -> p (a b)"), bank[b][:, :], ACT.Sqrt, "fox_rms",
                    scale=1.0 if b < 2 else 1.0 / FDH, bias=eps(EPS64 if b < 2 else EPS1))
            for u in range(4 * FH // 2 + 1):
                if u < 4 * FH // 2:
                    keys = P * (u // 2 % 2 + 1)
                    sc.wait_ge(S("fox_nmax"), u + 1)
                    if u >= 2:
                        sc.wait_ge(S("fox_turned"), u - 1)
                    act(prob[u % 2][:, 0:keys], bank[u % 2][:, 0:keys], ACT.Exp, "fox_exp",
                        bias=sl("nmx", (12,))[:, u % 2:u % 2 + 1], accum_out=sl("rs", (12,))[:, u % 2:u % 2 + 1])
                if u >= 1:
                    keys = P * ((u - 1) // 2 % 2 + 1)
                    sc.wait_ge(S("fox_turned"), u)
                    if u >= 3:
                        sc.wait_ge(S("fox_pv"), u - 2)
                    copy(probT[(u - 1) % 2][:, 0:keys], bank[2 + (u - 1) % 2][:, 0:keys], "fox_pT")
                if u >= 4 and u % 4 == 0 and u < 4 * FH // 2:
                    sc.wait_ge(S("fox_pv"), u)
                    copy(yT[:, u // 4 - 1, :], bank[4 + (u // 4 - 1) % 2][:, 0:T], "fox_o")
            sc.wait_ge(S("fox_pv"), 4 * FH // 2)
            copy(yT[:, FH // 2 - 1, :], bank[4 + (FH // 2 - 1) % 2][:, 0:T], "fox_o")

            sc.wait_ge(S("conv_ready"), 12)
            for b in range(6):
                act(feat[:, 8 + 2 * b:10 + 2 * b, :], conv[:, 2 * b:2 * b + 2, :], ACT.Silu, "gdn_silu")
            for b in range(2):
                act(feat[:, 20 + 2 * b:22 + 2 * b, :], feat[:, 20 + 2 * b:22 + 2 * b, :], ACT.Silu, "gdn_silu")
            sc.wait_ge(S("gdn_ss"), 1)
            for b in range(4):
                act(frms[:, 2 * b:2 * b + 2, :].rearrange("p a b -> p (a b)"), bank[b][:, :], ACT.Sqrt, "gdn_rms",
                    scale=float(GD) if b < 2 else 1.0, bias=eps(EPS128 if b < 2 else EPS1))
            sc.wait_ge(S("gdn_gc"), 2)
            gc, ngc = sl("gc", (8,)), sl("ngc", (8,))
            act(sl("eg", (8,)), gc, ACT.Exp, "gdn_eg")
            sc.wait_ge(S("gdn_gb"), 1)
            for t in range(NT):
                act(Eb[:, t, :, :].rearrange("p a b -> p (a b)"), bank[3 * t][:, :], ACT.Exp, "gdn_decay")
                for h in range(GH):
                    i, cols = t * GH + h, slice(h * P, (h + 1) * P)
                    act(Dm[:, t, h, :], bank[3 * t + 1][:, cols], ACT.Exp, "gdn_decay", scale=-1.0,
                        bias=gc[:, i:i + 1])
                    act(DT[:, t, h, :], bank[3 * t + 2][:, cols], ACT.Exp, "gdn_decay", bias=ngc[:, i:i + 1])
            sc.wait_ge(S("gdn_at"), 1)
            for t in range(NT):
                copy(AT[:, t, :, :].rearrange("p a b -> p (a b)"), bank[6 + t][:, :], "gdn_atc")
            for lv in range(1, len(LEVELS)):
                sc.wait_ge(S("inv_p"), lv)
                if lv > 1:
                    sc.wait_ge(S("inv_xp"), lv - 1)
                for t in range(NT):
                    copy(Pm[:, t, :, :].rearrange("p a b -> p (a b)"), bank[t][:, :], "inv_pc")
            sc.wait_ge(S("gdn_uw"), 1)
            for t in range(NT):
                copy(wT[:, t, :, :].rearrange("p a b -> p (a b)"), bank[t][:, :], "gdn_uwc")
            for n in range(NCH):
                sc.wait_ge(S("gdn_o"), n + 1)
                copy(og[:, :, n * CHUNK:(n + 1) * CHUNK], bank[3][:, 0:GH * CHUNK].rearrange(
                    "p (h c) -> p h c", h=GH), "gdn_oc")
            sc.wait_ge(S("og_ss"), 1)
            for b in range(2):
                act(orms[:, 2 * b:2 * b + 2, :].rearrange("p a b -> p (a b)"), bank[5 + b][:, :], ACT.Sqrt, "og_rms",
                    scale=1.0 / GD, bias=eps(EPS1))
            moe(0)

            rms_root(3)
            sc.wait_ge(S("pads_zero"), 5)
            sc.wait_ge(S("tok_ready"), 2)
            for t in range(NT):
                v = bank[t][:, 0:2 * NKV * NDH].rearrange("p (b g d) -> p b g d", b=2, g=NKV)
                for g in range(NKV):
                    copy(nvpad[:, t, :, g, g * NDH:(g + 1) * NDH], v[:, :, g, :], "tok_copied")
                copy(toks[:, t, 0:256], bank[t][:, 256:512], "tok_copied")
                copy(toks[:, t, 256:512], bank[2 + t][:, 0:256], "tok_copied")
            copy(lgT[0:LRANK, :], bank[7][0:LRANK, 0:T], "tok_copied")
            for t in range(NT):
                act(sl("ngate", (NT, OD_GATES))[:, t, :], bank[2 + t][:, 256:256 + OD_GATES], ACT.Sigmoid,
                    "tok_copied")
            copy_features(EV_TILES, OD_TILES)
            sc.wait_ge(S("gla_zc"), 1)
            log_part(lz, loga, "gla_lg")
            for kv in range(2):
                sc.wait_ge(S("cmp_h"), kv + 1)
                h = bank[2 + kv][:, 0:64].rearrange("p (a b) -> p a b", a=2)[:, :, 0:NKV * NCMP]
                act(chid[:, kv, :, :], h, ACT.Silu, "cmp_a")
            sc.wait_ge(S("cmp_o"), 1)
            copy(kcn, bank[2][:, 256:256 + NCMP], "cmp_kv")
            sc.wait_ge(S("cmp_o"), 2)
            for g in range(NKV):
                copy(vcpad[0:NCMP, g, g * NDH:(g + 1) * NDH], bank[3][0:NCMP, 256 + g * NDH:256 + (g + 1) * NDH],
                     "cmp_kv")
            sc.wait_ge(S("nsa_ss"), 1)
            for b in range(3):
                act(nrms[:, 2 * b:2 * b + 2, :].rearrange("p a b -> p (a b)"), bank[4 + b][:, :], ACT.Sqrt, "nsa_rms",
                    scale=1.0 if b < 2 else 1.0 / NDH, bias=eps(EPS64 if b < 2 else EPS1))
            act(sl("crms", (16,))[:, 0:NCMP], bank[7][:, 0:NCMP], ACT.Sqrt, "nsa_rms", scale=1.0 / NDH,
                bias=eps(EPS1))
            units = 2 * NH
            for u in range(units + 1):
                if u < units:
                    keys, c = P * (u // 2 % 2 + 1), 3 * (u % 2)
                    nm, rs = sl("nmx", (12,)), sl("rs", (12,))
                    sc.wait_ge(S("nsa_nmax"), u + 1)
                    act(nprob[u % 2][:, 512:512 + NCMP], nprob[u % 2][:, 512:512 + NCMP], ACT.Exp, "nsa_exp",
                        bias=nm[:, c:c + 1], accum_out=rs[:, c:c + 1])
                    for br in range(2):
                        p = nprob[u % 2][:, br * T:br * T + keys]
                        act(p, p, ACT.Exp, "nsa_exp", bias=nm[:, c + br + 1:c + br + 2],
                            accum_out=rs[:, c + br + 1:c + br + 2])
                if u >= 1:
                    v, qt = u - 1, (u - 1) // 2 % 2
                    sc.wait_ge(S("nsa_turned"), u)
                    if u >= 3:
                        sc.wait_ge(S("nsa_pv"), u - 2)
                    src, dst = (x[:, 0:512].rearrange("p (b k) -> p b k", b=2)[:, :, 0:P * (qt + 1)]
                                for x in (bank[2 + v % 2], nprobT[v % 2]))
                    copy(dst, src, "nsa_pT")
                    copy(nprobT[v % 2][0:NCMP, 512:512 + P], bank[7][0:NCMP, 0:P], "nsa_pT")
                if u >= 4 and u % 4 == 0 and u < units:
                    sc.wait_ge(S("nsa_pv"), u)
                    copy(yT[:, u // 4 - 1, :], bank[4 + (u // 4 - 1) % 2][:, 0:T], "nsa_o")
            sc.wait_ge(S("nsa_pv"), units)
            copy(yT[:, 3, :], bank[5][:, 0:T], "nsa_o")
            sc.wait_ge(S("gla_Gc"), 1)
            act(EG, G, ACT.Exp, "gla_exp")
            act(EnG, G, ACT.Exp, "gla_exp", scale=-1.0)
            sc.wait_ge(S("gla_dG"), 1)
            act(edG, edG, ACT.Exp, "gla_exp")
            for b in range(2):
                act(feat[:, 10 + 2 * b:12 + 2 * b, :], feat[:, 10 + 2 * b:12 + 2 * b, :], ACT.Silu, "gla_silu")
            for n in range(NCH):
                sc.wait_ge(S("gla_o"), n + 1)
                copy(og[:, :, n * CHUNK:(n + 1) * CHUNK], bank[6][:, 0:LH * CHUNK].rearrange(
                    "p (h c) -> p h c", h=LH), "gla_oc")
            sc.wait_ge(S("og_ss"), 2)
            for b in range(2):
                act(orms[:, 2 * b:2 * b + 2, :].rearrange("p a b -> p (a b)"), bank[1 + b][:, :], ACT.Sqrt, "og_rms",
                    scale=1.0 / LDV, bias=eps(EPS1))
            moe(1)

        @block.vector
        def _(ve):
            count = [0]

            def chain(ins):
                count[0] += 1
                ins.then_inc(S("vec_chain"), 1)
                ve.wait_ge(S("vec_chain"), count[0])

            def sig(ins, name):
                ins.then_inc(S(name), 1)

            def norm(n):
                layer, half = (n - 1) // 2, (n - 1) % 2
                for b in range(4):
                    x2 = xT[:, 2 * b:2 * b + 2, :]
                    last = ve.tensor_tensor(yT[:, 2 * b:2 * b + 2, :], x2, x2, ALU.mult)
                    if b < 3:
                        chain(last)
                sig(last, "sq_ready")
                if n == 1:
                    ve.wait_ge(S("ada_used"), 4)
                    chain(ve.tensor_tensor(mod[:, 0:24], bank[7][:, 0:24], pr("ada_b")[:, 0:24], ALU.add))
                    ve.engine_nop().then_inc(S("mod_copied"), 1)
                m0 = 48 * layer + 24 * half
                g0 = pr("norm_ffn" if half else "norm_mix")[:, layer * KT:(layer + 1) * KT]
                chain(ve.scalar_tensor_tensor(gain[:, :], mod[:, m0 + KT:m0 + 2 * KT], 1.0, g0, ALU.add, ALU.mult))
                ve.wait_ge(S("rms_root"), n)
                chain(ve.reciprocal(rms[:, :], rms[:, :]))
                for k in range(KT):
                    chain(ve.scalar_tensor_tensor(hT[:, k, :], xT[:, k, :], gain[:, k:k + 1], rms[:, :],
                                                  ALU.mult, ALU.mult))
                for k in range(KT):
                    last = ve.tensor_scalar(hT[:, k, :], hT[:, k, :], mod[:, m0 + k:m0 + k + 1], None, ALU.add)
                    if k < KT - 1:
                        chain(last)
                sig(last, "h_ready")

            def add_to_x(source, layer, half, m):
                g = 48 * layer + 24 * half + 2 * KT + m
                sig(ve.scalar_tensor_tensor(xT[:, m, :], source, mod[:, g:g + 1], xT[:, m, :], ALU.mult, ALU.add),
                    "x_added")
                ve.wait_ge(S("x_added"), 2 * KT * layer + KT * half + m + 1)

            def mixer_residual(layer):
                for m in range(KT):
                    ve.wait_ge(S("proj_ready"), KT * layer + m + 1)
                    add_to_x(bank[m % 4][:, 0:T], layer, 0, m)

            def pick(v, thr, k, n, out, buf):
                eq, gt, run = buf[0][:, :, 0:n], buf[1][:, :, 0:n], [buf[2][:, :, 0:n], buf[3][:, :, 0:n]]
                left = sl("left", (NT, 2))[:, :, 0:1]
                chain(ve.tensor_tensor(eq, v, thr.to_broadcast([P, NT, n]), ALU.is_equal))
                chain(ve.tensor_tensor(gt, v, thr.to_broadcast([P, NT, n]), ALU.is_gt))
                chain(ve.tensor_reduce(left, gt, AX.X, ALU.add))
                chain(ve.tensor_scalar(left, left, -1.0, float(k), ALU.mult, ALU.add))
                src, step, i = eq, 1, 0
                while step < n:
                    dst = run[i % 2]
                    chain(ve.tensor_copy(dst[:, :, 0:step], src[:, :, 0:step]))
                    chain(ve.tensor_tensor(dst[:, :, step:n], src[:, :, step:n], src[:, :, 0:n - step], ALU.add))
                    src, step, i = dst, 2 * step, i + 1
                other = run[i % 2]
                chain(ve.tensor_tensor(other, src, left.to_broadcast([P, NT, n]), ALU.is_le))
                chain(ve.tensor_tensor(other, other, eq, ALU.mult))
                chain(ve.tensor_tensor(out, other, gt, ALU.add))

            def routing(layer):
                ve.wait_ge(S("score_ready"), layer + 1)
                bias = pr("e_bias")[:, layer * E:(layer + 1) * E]
                for t in range(NT):
                    chain(ve.tensor_tensor(rbias[:, t, :], rscore[:, t, :], bias, ALU.add))
                m8, gs, gm = sl("m8", (NT * GROUPS, 8)), sl("gs", (NT, GROUPS)), sl("gm", (NT, GROUPS))
                for t in range(NT):
                    for g in range(GROUPS):
                        chain(ve.max(m8[:, t * GROUPS + g, :], rbias[:, t, g * 8:(g + 1) * 8]))
                chain(ve.tensor_tensor(gs.rearrange("p a b -> p (a b)"), m8[:, :, 0], m8[:, :, 1], ALU.add))
                g8, e8 = sl("g8", (NT, 8)), sl("e8", (NT, 8))
                for t in range(NT):
                    chain(ve.max(g8[:, t, :], gs[:, t, :]))
                pick(gs, g8[:, :, TOPG - 1:TOPG], TOPG, GROUPS, gm, rbuf)
                chain(ve.tensor_scalar(gs, gm, -1.0, -NEG, ALU.add, ALU.mult))
                per = E // GROUPS
                for t in range(NT):
                    r = rbias[:, t, :].rearrange("p (g j) -> p g j", j=per)
                    chain(ve.tensor_tensor(r, r, gs[:, t, :].unsqueeze(2).to_broadcast([P, GROUPS, per]), ALU.add))
                for t in range(NT):
                    chain(ve.max(e8[:, t, :], rbias[:, t, :]))
                pick(rbias, e8[:, :, TOPK - 1:TOPK], TOPK, E, wroute, rbuf)
                chain(ve.tensor_tensor(wroute, wroute, rscore, ALU.mult))
                ws = sl("wsum", (NT, 2))[:, :, 0:1]
                chain(ve.tensor_reduce(ws, wroute, AX.X, ALU.add))
                chain(ve.reciprocal(ws, ws))
                chain(ve.tensor_scalar(ws, ws, ROUTE_SCALE, None, ALU.mult))
                sig(ve.tensor_tensor(wroute, wroute, ws.to_broadcast([P, NT, E]), ALU.mult), "route_ready")

            def moe(layer):
                base = layer * 2 * (E + 1)
                norm(2 * layer + 2)
                routing(layer)

                def product(value, ft, a, r):
                    up = bank[4 + ft][:, T:2 * T]
                    ve.wait_ge(S("silu_ready"), value)
                    if r is None:
                        sig(ve.tensor_tensor(a[:, ft, :], silu_g[:, ft, :], up, ALU.mult), "a_ready")
                    else:
                        sig(ve.tensor_tensor(silu_g[:, ft, :], silu_g[:, ft, :], up, ALU.mult), "gu_product")
                        ve.wait_ge(S("gu_product"), value - 2 * (layer + 1))
                        sig(ve.tensor_tensor(a[:, ft, :], silu_g[:, ft, :], route_w[r][:, :], ALU.mult), "a_ready")

                n, first = place["experts", layer]
                for ft in range(2):
                    product(base + ft + 1, ft, act[BODY], None)

                def expert(e, k, slot_value, value):
                    r = (n + e) % SLOTS
                    ve.wait_ge(S(f"slot_full{r}"), slot_value)
                    for ft in range(2):
                        product(value + (ft + 1), ft, act[k], r)

                ve.wait_ge(S("expert_used"), layer * (E + 1) + 1)
                for e in range(PEEL):
                    expert(e, BODY, first[e], base + 2 * (e + 1))
                with ve.Fori(0, E // BODY) as step:
                    for k in range(BODY):
                        e = PEEL + k
                        expert(e, k, step * 32 + first[e], step * (2 * BODY) + (base + 2 * (e + 1)))
                ve.wait_ge(S("expert_used"), (layer + 1) * (E + 1))
                for m in range(KT):
                    add_to_x(bank[m // 2][:, (m % 2) * T:(m % 2 + 1) * T], layer, 1, m)

            def square(out, in_, name):
                sig(ve.tensor_tensor(out, in_, in_, ALU.mult), name)

            def output_norm(layer, on, silu_first):
                for b in range(2):
                    square(osq[:, 2 * b:2 * b + 2, :], og[:, 2 * b:2 * b + 2, :], "og_sq")
                ve.wait_ge(S("og_rms"), 2 * (layer + 1))
                for b in range(2):
                    r = orms[:, 2 * b:2 * b + 2, :]
                    o = og[:, 2 * b:2 * b + 2, :]
                    chain(ve.reciprocal(r, r))
                    chain(ve.scalar_tensor_tensor(o, o, on, r, ALU.mult, ALU.mult))
                    sig(ve.tensor_tensor(yT[:, 4 + 2 * b:6 + 2 * b, :], o,
                                         feat[:, silu_first + 2 * b:silu_first + 2 * b + 2, :], ALU.mult), "y_ready")

            ve.wait_ge(S("params_landed"), 32)
            ve.wait_ge(S("x_landed"), 16)
            norm(1)
            z, lg = sl("z", (NT, EV_SMALL)), sl("lg", (NT, EV_SMALL))
            ve.wait_ge(S("tok_copied"), 6)
            sig(ve.tensor_tensor(z[:, :, 0:FH], sml[:, :, 0:FH],
                                 pr("fox_fb").unsqueeze(1).to_broadcast([P, NT, FH]), ALU.add), "z_ready")
            sig(ve.tensor_tensor(z[:, :, FH:FH + GH], sml[:, :, FH:FH + GH],
                                 pr("dt_bias").unsqueeze(1).to_broadcast([P, NT, GH]), ALU.add), "z_ready")
            sig(ve.tensor_copy(z[:, :, FH + GH:EV_SMALL], sml[:, :, FH + GH:EV_SMALL]), "z_ready")
            for b in range(4):
                ve.wait_ge(S("feat_copied"), 2 * b + 2)
                f = feat[:, 2 * b:2 * b + 2, :]
                square(yT[:, 2 * b:2 * b + 2, :], f, "fox_sq")
            for j in range(12):
                ve.wait_ge(S("feat_copied"), 8 + j + 1)
                for tap in range(4):
                    w = pr("conv")[:, 4 * j + 3 - tap:4 * j + 4 - tap]
                    src, dst = feat[:, 8 + j, 0:T - tap], conv[:, j, tap:T]
                    if tap == 0:
                        chain(ve.tensor_scalar(dst, src, w, None, ALU.mult))
                    elif tap < 3:
                        chain(ve.scalar_tensor_tensor(dst, src, w, dst, ALU.mult, ALU.add))
                    else:
                        sig(ve.scalar_tensor_tensor(dst, src, w, dst, ALU.mult, ALU.add), "conv_ready")
            ve.wait_ge(S("lg_ready"), 1)
            ve.wait_ge(S("ea_ready"), 1)
            chain(ve.tensor_scalar(logf, z[:, :, 0:FH], 0.0, None, ALU.min))
            sig(ve.tensor_tensor(logf, logf, lg[:, :, 0:FH], ALU.subtract), "logf_ready")
            chain(ve.tensor_scalar(gate, z[:, :, FH:FH + GH], 0.0, None, ALU.max))
            chain(ve.tensor_tensor(gate, gate, lg[:, :, FH:FH + GH], ALU.add))
            chain(ve.tensor_scalar(gate, gate, -1.0, None, ALU.mult))
            sig(ve.tensor_tensor(gate, gate, sl("ea", (GH,)).unsqueeze(1).to_broadcast([P, NT, GH]), ALU.mult),
                "gdn_g")
            ve.wait_ge(S("fox_rms"), 4)
            for b in range(4):
                chain(ve.reciprocal(frms[:, 2 * b:2 * b + 2, :], frms[:, 2 * b:2 * b + 2, :]))
            for odd in range(2):
                rows = slice(64 * odd, 64 * odd + 64)
                sig(ve.scalar_tensor_tensor(qpad[rows, odd::2, :], feat[rows, 0:4, :], pr("fox_qn")[rows, :],
                                            frms[rows, 0:4, :], ALU.mult, ALU.mult), "fox_qk")
            sig(ve.scalar_tensor_tensor(feat[:, 4:8, :], feat[:, 4:8, :], pr("fox_kn"), frms[:, 4:8, :],
                                        ALU.mult, ALU.mult), "fox_qk")
            mx, nmx, rs = sl("mx", (12,)), sl("nmx", (12,)), sl("rs", (12,))
            for u in range(4 * FH // 2 + 1):
                if u < 4 * FH // 2:
                    keys, c = P * (u // 2 % 2 + 1), u % 2
                    ve.wait_ge(S("fox_s"), u + 1)
                    chain(ve.reduce_max(mx[:, c:c + 1], bank[c][:, 0:keys], AX.X))
                    if u >= 2:
                        ve.wait_ge(S("fox_exp"), u - 1)
                    sig(ve.tensor_scalar(nmx[:, c:c + 1], mx[:, c:c + 1], -1.0, None, ALU.mult), "fox_nmax")
                if u >= 1:
                    keys, c = P * ((u - 1) // 2 % 2 + 1), (u - 1) % 2
                    ve.wait_ge(S("fox_exp"), u)
                    chain(ve.reciprocal(rs[:, 4 + c:5 + c], rs[:, c:c + 1]))
                    p = prob[c][:, 0:keys]
                    sig(ve.tensor_scalar(p, p, rs[:, 4 + c:5 + c], None, ALU.mult), "fox_p")

            ve.wait_ge(S("ada_used"), 16)
            sig(ve.tensor_tensor(mod[:, 24:96], bank[7][:, 24:96], pr("ada_b")[:, 24:96], ALU.add), "mod_copied")
            ve.wait_ge(S("mod_copied"), 2)
            for b in range(4):
                ve.wait_ge(S("gdn_silu"), b + 1)
                f = feat[:, 8 + 2 * b:10 + 2 * b, :]
                square(squares[:, 2 * b:2 * b + 2, :], f, "gdn_sq")
            for b in range(4):
                ve.wait_ge(S("gdn_rms"), b + 1)
                r, f = frms[:, 2 * b:2 * b + 2, :], feat[:, 8 + 2 * b:10 + 2 * b, :]
                chain(ve.reciprocal(r, r))
                sig(ve.tensor_tensor(f, f, r, ALU.mult), "gdn_qk")
            gc, ngc, be, beta = sl("gc", (8,)), sl("ngc", (8,)), sl("be", (8,)), sl("beta", (8,))
            ve.wait_ge(S("gdn_cum"), 1)
            sig(ve.tensor_copy(gc, bank[6][:, 0:8]), "gdn_gc")
            sig(ve.tensor_scalar(ngc, bank[6][:, 0:8], -1.0, None, ALU.mult), "gdn_gc")
            ve.wait_ge(S("gdn_eg"), 1)
            ve.wait_ge(S("beta_ready"), 1)
            chain(ve.tensor_tensor(be, beta, sl("eg", (8,)), ALU.mult))
            ve.wait_ge(S("gdn_kk"), 1)
            ve.wait_ge(S("gdn_decay"), 18)
            for t in range(NT):
                for h in range(GH):
                    i = t * GH + h
                    sig(ve.scalar_tensor_tensor(Am[:, t, h, :], bank[6 + t][:, h * P:(h + 1) * P], beta[:, i:i + 1],
                                                Dm[:, t, h, :], ALU.mult, ALU.mult), "gdn_a")
            kdc = sl("kdc", (2, 8))
            for half in range(2):
                chain(ve.tensor_copy(kdc[:, half, :], DT.rearrange("p a b c -> p (a b) c")
                                     [:, :, half * CHUNK + CHUNK - 1]))
            ve.wait_ge(S("gdn_turned"), 1)
            ve.wait_ge(S("fox_pv"), 4 * FH // 2)

            def by4(b):
                return bank[b][:, :].rearrange("p (h d) -> p h d", h=GH)

            def col4(v, t):
                return v[:, t * GH:(t + 1) * GH].unsqueeze(2).to_broadcast([P, GH, P])

            for t in range(NT):
                sig(ve.tensor_tensor(attnT[:, t, :, :], by4(t), DT[:, t, :, :], ALU.mult), "gdn_attn")
                sig(ve.tensor_tensor(vb[:, t, :, :], by4(4 + t), col4(beta, t), ALU.mult), "gdn_kv")
                sig(ve.tensor_tensor(kbe[:, t, :, :], by4(2 + t), col4(be, t), ALU.mult), "gdn_kv")
                for half in range(2):
                    sig(ve.tensor_tensor(kd[half][:, t, :, :], by4(2 + t), col4(kdc[:, half, :], t), ALU.mult),
                        "gdn_kv")
                q = feat[:, 8:12, t * P:(t + 1) * P]
                sig(ve.tensor_tensor(q, q, Eb[:, t, :, :], ALU.mult), "gdn_qd")
            ve.wait_ge(S("gdn_qk"), 4)

            def by8(a):
                return a.rearrange("p a b c -> p (a b) c")

            def over8(m):
                return m.unsqueeze(1).to_broadcast([P, 2 * GH, P])

            ve.wait_ge(S("gdn_a"), 8)
            chain(ve.tensor_tensor(by8(X), by8(Am), over8(cs("lev1")), ALU.mult))
            sig(ve.tensor_tensor(by8(X), over8(ident), by8(X), ALU.subtract), "inv_x")
            ve.wait_ge(S("gdn_atc"), 2)
            chain(ve.tensor_tensor(by8(XT), by8(AT), over8(cs("levt", 0, P)), ALU.mult))
            sig(ve.tensor_tensor(by8(XT), over8(ident), by8(XT), ALU.subtract), "inv_x")
            for lv in range(1, len(LEVELS)):
                ve.wait_ge(S("inv_xp"), lv)
                for t in range(NT):
                    if lv < len(LEVELS) - 1:
                        sig(ve.tensor_tensor(X[:, t, :, :], X[:, t, :, :], by4(2 + t), ALU.subtract), "inv_x")
                    sig(ve.tensor_tensor(XT[:, t, :, :], XT[:, t, :, :], by4(4 + t), ALU.subtract), "inv_x")
                ve.wait_ge(S("inv_x"), 2 + 4 * lv if lv < len(LEVELS) - 1 else INVX)
            ve.wait_ge(S("gdn_uw"), 1)
            for t in range(NT):
                sig(ve.tensor_copy(u_sb[:, t, :, :], by4(6 + t)), "gdn_uwc")
            ve.wait_ge(S("gdn_uwc"), 4)
            for n in range(NCH):
                t, half = n // 2, n % 2
                if n == 0:
                    sig(ve.tensor_copy(vnew, u_sb[:, 0, :, :]), "gdn_vn")
                else:
                    ve.wait_ge(S("gdn_ws"), n)
                    ve.wait_ge(S("gdn_o"), n)
                    sig(ve.tensor_tensor(vnew, u_sb[:, t, :, :], by4(2), ALU.subtract), "gdn_vn")
                if n < NCH - 1:
                    ve.wait_ge(S("gdn_su"), n + 1)
                    ve.wait_ge(S("gdn_o"), n + 1)
                    if n == 0:
                        sig(ve.tensor_copy(state, by4(4)), "gdn_state")
                    else:
                        for h in range(GH):
                            c = half * CHUNK + CHUNK - 1
                            sig(ve.scalar_tensor_tensor(state[:, h, :], state[:, h, :], Eb[:, t, h, c:c + 1],
                                                        bank[4][:, h * P:(h + 1) * P], ALU.mult, ALU.add),
                                "gdn_state")
                    ve.wait_ge(S("gdn_state"), 1 + GH * n)
            ve.wait_ge(S("gdn_oc"), NCH)
            ve.wait_ge(S("gdn_silu"), 8)
            output_norm(0, pr("gdn_on"), 20)
            mixer_residual(0)
            moe(0)

            norm(3)
            ve.wait_ge(S("feat_copied"), EV_TILES + 6)
            for b in range(3):
                f = feat[:, 2 * b:2 * b + 2, :]
                square(yT[:, 2 * b:2 * b + 2, :], f, "nsa_sq")
            ve.wait_ge(S("feat_copied"), EV_TILES + OD_TILES)
            for kv in range(2):
                for g in range(NKV):
                    for s in range(2):
                        rows = slice(64 * s, 64 * s + 64)
                        src = feat[rows, 14 + 2 * kv + g, 16 * s:16 * s + 16 * NCMP].rearrange(
                            "p (n l) -> p l n", l=16)
                        pos = pr("pos")[rows, 16 * kv:16 * kv + 16].unsqueeze(2).to_broadcast([64, 16, NCMP])
                        sig(ve.tensor_tensor(blk[rows, kv, :, g * NCMP:(g + 1) * NCMP], src, pos, ALU.add),
                            "cmp_blk")
            ve.wait_ge(S("gla_z"), 1)
            sig(ve.tensor_tensor(lz, bank[0][:, :].rearrange("p (a b) -> p a b", a=NT),
                                 pr("bg").unsqueeze(1).to_broadcast([P, NT, 256]), ALU.add), "gla_zc")
            ve.wait_ge(S("gla_lg"), 1)
            chain(ve.tensor_scalar(lz, lz, 0.0, None, ALU.min))
            chain(ve.tensor_tensor(loga, lz, loga, ALU.subtract))
            sig(ve.tensor_scalar(loga, loga, 1.0 / TAU, None, ALU.mult), "gla_loga")
            ve.wait_ge(S("cmp_kv"), 1)
            square(csq, kcn, "cmp_sq")
            ve.wait_ge(S("nsa_rms"), 4)
            chain(ve.reciprocal(nrms, nrms))
            crms = sl("crms", (16,))[:, 0:NCMP]
            chain(ve.reciprocal(crms, crms))
            for odd in range(2):
                rows = slice(64 * odd, 64 * odd + 64)
                sig(ve.scalar_tensor_tensor(qpad[rows, 4 * odd:4 * odd + 4, :], feat[rows, 0:4, :],
                                            pr("nsa_qn")[rows, :], nrms[rows, 0:4, :], ALU.mult, ALU.mult), "nsa_qk")
            sig(ve.scalar_tensor_tensor(feat[:, 4:6, :], feat[:, 4:6, :], pr("nsa_kn"), nrms[:, 4:6, :],
                                        ALU.mult, ALU.mult), "nsa_qk")
            sig(ve.scalar_tensor_tensor(kcn, kcn, pr("nsa_kn"), crms, ALU.mult, ALU.mult), "nsa_qk")
            ve.wait_ge(S("nsa_qk"), 4)
            ve.wait_ge(S("brel_landed"), 32)
            units = [(h0 + i, qt) for h0 in range(4) for qt in range(NT) for i in (0, 4)]
            ngate = sl("ngate", (NT, OD_GATES))
            for u in range(len(units) + 1):
                if u < len(units):
                    h, qt = units[u]
                    keys, c = P * (qt + 1), 3 * (u % 2)
                    p = nprob[u % 2][:, 0:512].rearrange("p (b k) -> p b k", b=2)[:, :, 0:keys]
                    pc = nprob[u % 2][:, 512:512 + NCMP]
                    ve.wait_ge(S("nsa_s"), u + 1)
                    if u >= 2:
                        ve.wait_ge(S("nsa_turned"), u - 1)
                    sig(ve.tensor_tensor(p, bank[u % 2][:, :].rearrange("p (b k) -> p b k", b=2)[:, :, 0:keys],
                                         Brel[:, qt, h, 0:keys].unsqueeze(1).to_broadcast([P, 2, keys]), ALU.add),
                        "nsa_b")
                    sig(ve.tensor_tensor(pc, bank[6][:, 0:NCMP], relc[:, qt, :, h],
                                         ALU.add), "nsa_b")
                    ve.wait_ge(S("nsa_b"), 2 * (u + 1))
                    chain(ve.reduce_max(mx[:, c:c + 1], pc, AX.X))
                    chain(ve.reduce_max(mx[:, c + 1:c + 3], p, AX.X))
                    sig(ve.tensor_scalar(nmx[:, c:c + 3], mx[:, c:c + 3], -1.0, None, ALU.mult), "nsa_nmax")
                if u >= 1:
                    h, qt = units[u - 1]
                    keys, c = P * (qt + 1), 3 * ((u - 1) % 2)
                    rg = sl("rg", (12,))[:, c:c + 3]
                    ve.wait_ge(S("nsa_exp"), 3 * u)
                    chain(ve.reciprocal(rg, rs[:, c:c + 3]))
                    chain(ve.tensor_tensor(rg, rg, ngate[:, qt, 3 * h:3 * h + 3], ALU.mult))
                    pc = nprob[(u - 1) % 2][:, 512:512 + NCMP]
                    sig(ve.scalar_tensor_tensor(pc, pc, rg[:, 0:1], cs("cmask")[:, qt * NCMP:(qt + 1) * NCMP],
                                                ALU.mult, ALU.mult), "nsa_p")
                    for br in range(2):
                        p = nprob[(u - 1) % 2][:, br * T:br * T + keys]
                        sig(ve.tensor_scalar(p, p, rg[:, br + 1:br + 2], None, ALU.mult), "nsa_p")

            ve.wait_ge(S("gla_G"), 1)
            sig(ve.tensor_copy(G.rearrange("p a b -> p (a b)"), bank[0][:, :]), "gla_Gc")
            ve.wait_ge(S("gla_Gc"), 1)
            for f in range(2):
                g = G[:, f, :].rearrange("p (n c) -> p n c", c=CHUNK)
                last = ve.tensor_tensor(edG[:, f, :].rearrange("p (n c) -> p n c", c=CHUNK),
                                        g[:, :, CHUNK - 1:CHUNK].to_broadcast([P, NCH, CHUNK]), g, ALU.subtract)
                if f == 0:
                    chain(last)
            sig(last, "gla_dG")
            ve.wait_ge(S("gla_exp"), 3)
            ve.wait_ge(S("pads_zero"), 6)
            for odd in range(2):
                rows = slice(64 * odd, 64 * odd + 64)
                sig(ve.scalar_tensor_tensor(lqd[rows, odd::2, :], feat[rows, 6:8, :], LDK ** -0.5, EG[rows, :, :],
                                            ALU.mult, ALU.mult), "gla_qk")
            sig(ve.tensor_tensor(lki, feat[:, 8:10, :], EnG, ALU.mult), "gla_qk")
            sig(ve.tensor_tensor(lkd, feat[:, 8:10, :], edG, ALU.mult), "gla_qk")
            ve.wait_ge(S("gla_at"), 1)
            for t in range(NT):
                sig(ve.tensor_tensor(lattn[:, t, :, :], by4(1 + t), cs("tril").unsqueeze(1).to_broadcast([P, LH, P]),
                                     ALU.mult), "gla_ready")
            for half in range(2):
                sig(ve.tensor_scalar(lkt[:, half, :, :, :].rearrange("p a b c -> p (a b c)"), bank[3][:, :],
                                     cs("half")[:, half:half + 1], None, ALU.mult), "gla_ready")
            for n in range(NCH - 1):
                ve.wait_ge(S("gla_su"), n + 1)
                ve.wait_ge(S("gla_o"), n + 1)
                if n == 0:
                    sig(ve.tensor_copy(lstate, by4(5)), "gla_state")
                else:
                    for h in range(LH):
                        c = n * CHUNK + CHUNK - 1
                        sig(ve.scalar_tensor_tensor(lstate[:, h, :], lstate[:, h, :], EG[:, h // 2, c:c + 1],
                                                    bank[5][:, h * P:(h + 1) * P], ALU.mult, ALU.add), "gla_state")
                ve.wait_ge(S("gla_state"), 1 + LH * n)
            ve.wait_ge(S("gla_oc"), NCH)
            ve.wait_ge(S("gla_silu"), 2)
            output_norm(1, pr("gla_on"), 10)
            mixer_residual(1)
            moe(1)

        @block.gpsimd
        def _(gp):
            gp.memset(qpad, 0.0).then_inc(S("pads_zero"), 1)
            gp.memset(vpad, 0.0).then_inc(S("pads_zero"), 1)
            gp.wait_ge(S("gdn_atc"), 2)
            gp.wait_ge(S("params_landed"), 32)
            gp.wait_ge(S("gdn_ss"), 1)
            for lv in range(1, len(LEVELS)):
                if lv > 2:
                    gp.wait_ge(S("inv_p"), lv - 2)
                gp.tensor_tensor(ATm[lv % 2].rearrange("p a b c -> p (a b) c"), AT.rearrange("p a b c -> p (a b) c"),
                                 cs("levt", lv * P, (lv + 1) * P).unsqueeze(1).to_broadcast([P, 2 * GH, P]),
                                 ALU.mult).then_inc(S("inv_atm"), 1)
            gp.wait_ge(S("x_added"), 2 * KT)
            gp.memset(qpad, 0.0).then_inc(S("pads_zero"), 1)
            gp.memset(nvpad, 0.0).then_inc(S("pads_zero"), 1)
            gp.memset(vcpad, 0.0).then_inc(S("pads_zero"), 1)
            gp.wait_ge(S("nsa_nmax"), 2 * NH)
            gp.memset(lqd, 0.0).then_inc(S("pads_zero"), 1)


def tiles(a, width=P):
    r, c = a.shape
    return a.reshape(r // width, width, c).transpose(1, 0, 2).reshape(width, -1)


def lay_out(i):
    def rep(v):
        return np.broadcast_to(np.asarray(v).reshape(1, -1), (P, np.asarray(v).size))

    def cols(v):
        return np.asarray(v).reshape(-1, P).T

    def twice(v):
        return np.concatenate([v, v])[:, None]

    par = np.zeros((P, PARW), np.float32)

    def put(name, a):
        par[: a.shape[0], PAR[name][0]:PAR[name][0] + a.shape[1]] = a

    put("c", cols(i["c"][0]))
    put("ada_b", cols(i["ada_b"]))
    put("norm_mix", cols(i["norm_mix"]))
    put("norm_ffn", cols(i["norm_ffn"]))
    put("router", tiles(i["moe_router"].reshape(LAYERS * D, E)))
    put("e_bias", rep(i["moe_bias"]))
    put("fox_fb", rep(i["fox_fb"]))
    put("fox_qn", twice(i["fox_qn"][0]))
    put("fox_kn", twice(i["fox_kn"][0]))
    put("conv", i["gdn_conv"][0].T.reshape(12, P, 4).transpose(1, 0, 2).reshape(P, 48))
    put("a_log", rep(i["gdn_a_log"]))
    put("dt_bias", rep(i["gdn_dt_bias"]))
    put("gdn_on", i["gdn_on"][0][:, None])
    put("nsa_qn", twice(i["nsa_qn"][0]))
    put("nsa_kn", twice(i["nsa_kn"][0]))
    pos = i["nsa_pos"][0].reshape(2, 2, 16, NDH)
    put("pos", pos.transpose(1, 3, 0, 2).reshape(P, 32))
    put("wg_up", i["gla_wg_up"][0])
    put("bg", rep(i["gla_bg"]))
    put("gla_on", i["gla_on"][0][:, None])
    put("rel", np.concatenate([i["rel_bias"], np.ones((1, NH), np.float32)]))

    pair = np.concatenate([np.r_[64 * h:64 * h + 64, 64 * (h + 4):64 * (h + 4) + 64] for h in range(4)])
    ev, od = i["ev_w_in"][0], i["od_w_in"][0]
    ev_cut = np.cumsum([0, 512, 512, 512, 8, 1536, 4, 4, 512])
    fq, fk, fv, ff, gqkv, ga, gb, gz = (ev[:, a:b] for a, b in zip(ev_cut, ev_cut[1:]))
    od_cut = np.cumsum([0, 512] + [128] * 6 + [24, 256, 256, 512, 16, 512])
    nq, kc, vc, ks, vs, kw, vw, ng, lq, lk, lv, lg, lr = (od[:, a:b] for a, b in zip(od_cut, od_cut[1:]))
    double = [x[:, 64 * g:64 * g + 64] for x in (kc, vc) for g in range(2) for _ in range(2)]
    full = {"in0.0": np.concatenate([fv, ff, ga, gb], 1), "in1.0": np.concatenate([vs, vw, lv], 1),
            "in1.1": np.concatenate([ng, lg], 1)}
    feat0 = np.concatenate([fq, fk, gqkv, gz], 1)
    feat1 = np.concatenate([nq[:, pair], ks, kw, lq, lk, lr] + double, 1)
    out1 = i["od_w_out"][0]
    outs = [i["ev_w_out"][0], np.concatenate([out1[:512][pair], out1[512:]])]
    w1, w2 = i["nsa_cmp_w1"][0], i["nsa_cmp_w2"][0]
    mix = np.zeros((len(NAMES), P, SLOTW), np.float32)
    for n, name in enumerate(NAMES):
        s = int(name[-1])
        if name in full:
            a = tiles(full[name])
        elif name.startswith("ada"):
            a = tiles(i["ada_w"][int(name[3])][:, SC * s:SC * (s + 1)])
        elif name.startswith("in0"):
            a = tiles(feat0[:, SC * (s - 1):SC * s])
        elif name.startswith("in1"):
            a = tiles(feat1[:, SC * (s - 2):SC * (s - 1)])
        elif name.startswith("out"):
            a = tiles(outs[int(name[3])][:, 512 * s:512 * (s + 1)])
        else:
            first = w1[s].reshape(2, 16, NDH, CHID).transpose(0, 2, 1, 3).reshape(P, 16 * CHID)
            second = tiles(w2[s])
            if s == 0:
                second = second.reshape(P, 2, NDH)
                padded = np.zeros((P, 2, 2, P), np.float32)
                padded[:, :, 0, 0:NDH] = second
                padded[:, :, 1, NDH:P] = second
                second = padded.reshape(P, 512)
            a = np.concatenate([first, second], 1)
        mix[n, :, 0:a.shape[1]] = a

    moe = np.empty((LAYERS * (E + 1), P, SLOTW), np.float32)
    for l in range(LAYERS):
        at = l * (E + 1)
        third = KT * FE
        for j, (sh, ex) in enumerate((("sh_wg", "moe_wg"), ("sh_wu", "moe_wu"))):
            moe[at, :, j * third:(j + 1) * third] = tiles(i[sh][l])
            moe[at + 1:at + 1 + E, :, j * third:(j + 1) * third] = i[ex][l].reshape(E, KT, P, FE).transpose(
                0, 2, 1, 3).reshape(E, P, third)
        moe[at, :, 2 * third:] = tiles(i["sh_wd"][l])
        moe[at + 1:at + 1 + E, :, 2 * third:] = i["moe_wd"][l].reshape(E, 2, P, D).transpose(
            0, 2, 1, 3).reshape(E, P, third)
    x = i["x"][0].T.reshape(KT, P, T).transpose(1, 0, 2)
    return {"xT_in": np.ascontiguousarray(x), "par_in": par, "cst_in": constants(), "mix_in": mix, "moe_in": moe}


def kernel(**inputs):
    import concourse.bacc as _bacc
    from concourse.bass_utils import run_bass_kernel_spmd as _run

    arrays = lay_out({k: np.asarray(v) for k, v in inputs.items()})
    nc = _bacc.Bacc("TRN2", target_bir_lowering=False, num_devices=1)
    args = [nc.dram_tensor(n, a.shape, F32, kind="ExternalInput").ap() for n, a in arrays.items()]
    args.append(nc.dram_tensor("outT", (P, KT, T), F32, kind="ExternalOutput").ap())
    program(nc, *args)
    r = _run(nc, [arrays], core_ids=[0])
    out = r.results[0]["outT"]
    return np.ascontiguousarray(out.transpose(1, 0, 2).reshape(D, T).T.reshape(1, T, D))
```

```python
import math
from contextlib import ExitStack

import numpy as np
import concourse.bass as bass
from concourse import mybir

F32 = mybir.dt.float32
F32R = mybir.dt.float32r
ALU = mybir.AluOpType
ACT = mybir.ActivationFunctionType
AX = mybir.AxisListType

P = 128
D = 1024
T = 256
NT = T // P
KT = D // P
LAYERS = 2
EPS = 1e-6
NEG = -1e30
CHUNK = 64
NCH = T // CHUNK
FH, FDH = 8, 64
GH, GD = 4, 128
NH, NDH, NKV = 8, 64, 2
CMP_LEN, CMP_STRIDE = 32, 16
NCMP = (T - CMP_LEN) // CMP_STRIDE + 1
ROW = 2 * T
CHID = 256
LH, LDK, LDV, LRANK = 4, 64, 128, 16
TAU = 16.0
BUCKETS, MAXDIST = 32, 128
E, TOPK, GROUPS, TOPG = 64, 6, 8, 4
FE = 256
ROUTE_SCALE = 2.5
SLOTW = 3 * KT * FE
SLOTS = 3
SC = SLOTW // KT
X = E + 1
BODY = SLOTS
LOOPS = (X - 5) // BODY
TAIL = LOOPS * BODY + 1
PIECE = (2048, 2048, 1024, 1024)
AT_PIECE = (0, 2048, 4096, 5120)
LEVELS = (1, 2, 4, 8, 16, 32)
INVX = 4 * (len(LEVELS) - 1)

EV_SMALL = FH + 2 * GH
OD_TOK = 2 * NKV * NDH + LH * LDV
OD_GATES = 3 * NH
EV_TILES = 24
OD_TILES = 18


def columns(parts):
    at, where = 0, {}
    for name, width in parts:
        where[name] = (at, at + width)
        at += width
    return where, at


PAR, PARW = columns([
    ("c", KT), ("ada_b", LAYERS * 48), ("norm_mix", LAYERS * KT), ("norm_ffn", LAYERS * KT),
    ("router", LAYERS * KT * E), ("e_bias", LAYERS * E), ("fox_fb", FH), ("fox_qn", 1), ("fox_kn", 1),
    ("conv", 48), ("a_log", GH), ("dt_bias", GH), ("gdn_on", 1), ("nsa_qn", 1), ("nsa_kn", 1),
    ("pos", 2 * 16), ("wg_up", 256), ("bg", 256), ("gla_on", 1), ("rel", NH)])
CST, CSTW = columns([
    ("ident", P), ("ones", P), ("bd", P), ("tri", P), ("ntri", 2 * P), ("maskq", P), ("mpos", P), ("mneg", P),
    ("tril", P), ("levt", 6 * P), ("lev1", P), ("ohr", 512), ("ohf", 512), ("cmask", NT * NCMP), ("eps", 8),
    ("half", 2)])
EPS1, EPS64, EPS128, ONE, ZERO = range(5)


SML, SMALLW = columns([
    ("sml", 2 * 16), ("logf", 16), ("gate", 8), ("z", 32), ("lg", 32), ("beta", 8), ("be", 8), ("gc", 8),
    ("ngc", 8), ("eg", 8), ("ea", 4), ("kdc", 16), ("mx", 12), ("nmx", 12), ("rs", 12), ("rg", 12),
    ("ngate", 48), ("chid", 120), ("kcn", 16), ("csq", 16), ("crms", 16),
    ("m8", 128), ("gs", 16), ("g8", 16), ("e8", 16), ("gm", 16), ("left", 4), ("wsum", 4)])


def constants():
    c = np.zeros((P, CSTW), np.float32)

    def put(name, a):
        c[: a.shape[0], CST[name][0]:CST[name][0] + a.shape[1]] = a

    i, j = np.arange(P)[:, None], np.arange(P)[None, :]
    same = i // CHUNK == j // CHUNK
    put("ident", np.eye(P))
    put("ones", np.ones((P, P)))
    put("bd", (i // 64 == j // 64) * 1.0)
    put("tri", (same & (i <= j)) * 1.0)
    put("ntri", np.concatenate([(i <= j) * -1.0, -np.ones((P, P))], 1))
    put("maskq", np.where(j > i, NEG, 0.0))
    put("mpos", np.where(same & (j <= i), 0.0, -NEG))
    put("mneg", np.where(same & (j >= i), 0.0, NEG))
    put("tril", (same & (j >= i)) * 1.0)

    def level(m):
        return ((i // (2 * m) == j // (2 * m)) & (i // m % 2 == 1) & (j // m % 2 == 0)) * 1.0

    put("levt", np.concatenate([level(m).T for m in LEVELS], 1))
    put("lev1", level(1))
    dist = 255 - np.arange(512)
    exact = BUCKETS // 2
    n = np.maximum(dist, 0)
    large = exact + (np.log(np.maximum(n, 1).astype(np.float32) / np.float32(exact))
                     / np.float32(math.log(MAXDIST / exact)) * np.float32(BUCKETS - exact)).astype(np.int32)
    bucket = np.where(n < exact, n, np.minimum(large, BUCKETS - 1))
    oh = np.zeros((BUCKETS + 1, 512), np.float32)
    oh[bucket, np.arange(512)] = 1.0
    oh[BUCKETS] = np.where(dist < 0, NEG, 0.0)
    put("ohr", oh)
    put("ohf", oh[:, ::-1])
    q = np.arange(T).reshape(NT, P).T
    end = np.arange(NCMP) * CMP_STRIDE + CMP_LEN - 1
    put("cmask", (end[None, None, :] <= q[:, :, None]).reshape(P, -1) * 1.0)
    put("eps", np.tile(np.array([[EPS, 64 * EPS, 128 * EPS, 1.0, 0.0, 0, 0, 0]]), (P, 1)))
    put("half", np.stack([(np.arange(P) < 64), (np.arange(P) >= 64)], 1) * 1.0)
    return c


def mixer_loads():
    names = [f"ada0.{s}" for s in range(4)] + [f"in0.{s}" for s in range(5)]
    names += [f"ada0.{s}" for s in range(4, 8)] + [f"ada1.{s}" for s in range(8)] + ["out0.0", "out0.1"]
    names += [f"in1.{s}" for s in range(5)] + ["cmp.0", "cmp.1", "out1.0", "out1.1"]
    return names


NAMES = mixer_loads()


def width_of(name):
    if name == "in0.0":
        return KT * (FH * FDH + EV_SMALL)
    if name == "in1.1":
        return KT * (OD_GATES + LRANK)
    if name.startswith("cmp"):
        return 16 * CHID + (512 if name == "cmp.0" else 128)
    if name.startswith("out"):
        return KT * 512
    return SLOTW


def program(nc, xT_in, par_in, cst_in, mix_in, moe_in, outT):
    with ExitStack() as ctx:
        def sb(name, shape):
            return ctx.enter_context(nc.sbuf_tensor(name, shape, F32))

        sems = {}

        def S(name):
            if name not in sems:
                sems[name] = ctx.enter_context(nc.semaphore(name))
            return sems[name]

        bank = [ctx.enter_context(nc.psum_tensor(f"bank{i}", [P, 512], F32)) for i in range(8)]
        ring = [sb(f"ring{i}", [P, SLOTW]) for i in range(SLOTS)]
        route_w = [sb(f"route_w{i}", [P, T]) for i in range(SLOTS)]
        par = sb("par_sb", [P, PARW])
        cst = sb("cst_sb", [P, CSTW])
        xT = sb("xT", [P, KT, T])
        hT = sb("hT", [P, KT, T])
        yT = sb("yT", [P, KT, T])
        mod = sb("mod", [P, LAYERS * 48])
        cond = sb("cond", [P, KT])
        gain = sb("gain", [P, KT])
        rms = sb("rms", [P, T])
        relrow = sb("relrow", [NH, 512])
        relc = sb("relc", [P, NT, NCMP, NH])
        small = sb("small", [P, SMALLW])
        modrow = sb("modrow", [1, SC])
        mixer_memory = ExitStack()

        def mb(name, shape):
            return mixer_memory.enter_context(nc.sbuf_tensor(name, shape, F32))

        feat = mb("feat", [P, EV_TILES, T])
        scr = mb("scr", [P, 48, T])

        def flat(tensor, first, blocks):
            return tensor[:, first:first + blocks, :].rearrange("p a b -> p (a b)")

        def blocks(first, shape):
            n = int(np.prod(shape))
            letters = "abcd"[:len(shape)]
            dims = " ".join(letters)
            return flat(scr, first, -(-n // T))[:, 0:n].rearrange(
                f"p ({dims}) -> p {dims}", **dict(zip(letters, shape)))

        def sl(name, shape):
            lo, hi = SML[name]
            letters = "abcd"[:len(shape)]
            dims = " ".join(letters)
            return small[:, lo:hi].rearrange(f"p ({dims}) -> p {dims}", **dict(zip(letters, shape)))

        sml = sl("sml", (NT, EV_SMALL))
        logf = sl("logf", (NT, FH))
        gate = sl("gate", (NT, GH))
        qpad = blocks(0, (FH, T))
        vpad = blocks(8, (NT, FH, P))
        prob = [blocks(16 + i, (T,)) for i in range(2)]
        probT = [blocks(18 + i, (T,)) for i in range(2)]
        conv = blocks(20, (12, T))
        frms = blocks(32, (8, T))
        squares = blocks(40, (8, T))
        vb, kbe = blocks(0, (NT, GH, P)), blocks(4, (NT, GH, P))
        kd = [blocks(8, (NT, GH, P)), blocks(12, (NT, GH, P))]
        state, vnew = blocks(16, (GH, P)), blocks(18, (GH, P))
        Eb, Dm, DT = (blocks(b, (NT, GH, P)) for b in (20, 24, 28))
        Am, attnT = Dm, DT
        Xi, XT = blocks(32, (NT, GH, P)), blocks(36, (NT, GH, P))
        ATm = [blocks(40, (NT, GH, P)), blocks(44, (NT, GH, P))]
        og, osq = blocks(32, (GH, T)), blocks(36, (GH, T))
        orms = blocks(40, (GH, T))

        def feat4(first):
            return flat(feat, first, 4).rearrange("p (a b c) -> p a b c", a=NT, b=GH)

        Pm, AT, u_sb, wT = feat4(0), feat4(4), feat4(12), feat4(16)
        nvpad = blocks(8, (NT, 2, NKV, P))
        vcpad = blocks(12, (NKV, P))
        lgT = blocks(13, (T,))
        Brel = blocks(16, (NT, NH, T))
        nrms = blocks(32, (6, T))
        npr = blocks(32, (2, 640))
        npT = blocks(37, (2, 640))
        nprob = [npr[:, i, :] for i in range(2)]
        nprobT = [npT[:, i, :] for i in range(2)]
        blk = blocks(42, (2, 16, NKV * NCMP))
        chid = sl("chid", (2, 2, NKV * NCMP))
        kcn = sl("kcn", (16,))[:, 0:NCMP]
        csq = sl("csq", (16,))[:, 0:NCMP]
        toks = flat(feat, 18, 4).rearrange("p (a b) -> p a b", a=NT)
        lz, loga = blocks(46, (NT, T)), blocks(14, (NT, T))
        G, EG, EnG, edG = (blocks(b, (2, T)) for b in (0, 2, 4, 6))
        lki, lkd = blocks(8, (2, T)), blocks(10, (2, T))
        lqd, lkt = blocks(16, (LH, T)), blocks(20, (2, NT, 2, P))
        lattn, lstate = blocks(24, (NT, LH, P)), blocks(28, (LH, P))
        mixer_memory.close()

        def split(name, shape):
            return tuple(ctx.enter_context(nc.sbuf_tensor(name + part, shape, F32R)) for part in ("_hi", "_lo"))

        piece = [split(f"piece{c}", [P, PIECE[c]]) for c in range(4)]
        h2 = split("h2", [P, KT, T])
        a2 = split("a2", [P, 2, T])
        silu_g = sb("silu_g", [P, 2, T])
        rscore, rbias, wroute = (sb(n, [P, NT, E]) for n in ("rscore", "rbias", "wroute"))
        rbuf = [sb(f"rbuf{i}", [P, NT, E]) for i in range(4)]
        wTs = sb("wTs", [E, T])

        w_dram = [nc.dram_tensor(f"route{l}", [E, T], F32) for l in range(LAYERS)]
        rel_dram = nc.dram_tensor("rel_rows", [NH, P * (ROW + 1)], F32)

        def pr(name, a=0, b=None):
            lo, hi = PAR[name]
            return par[:, lo + a:(hi if b is None else lo + b)]

        def cs(name, a=0, b=None):
            lo, hi = CST[name]
            return cst[:, lo + a:(hi if b is None else lo + b)]

        def eps(k):
            return cs("eps", k, k + 1)

        ident, ones = cs("ident"), cs("ones")

        order = [("mix", n) for n in NAMES[:NAMES.index("in1.0")]] + [("shared", 0), ("experts", 0)]
        order += [("mix", n) for n in NAMES[NAMES.index("in1.0"):]] + [("shared", 1), ("experts", 1)]
        place, n_load, landed = {}, 0, [0] * SLOTS
        for key in order:
            slot = n_load % SLOTS
            if key[0] == "experts":
                first = [landed[(n_load + e) % SLOTS] + 16 * (e // SLOTS + 1) for e in range(E)]
                place[key] = (n_load, first)
                for e in range(E):
                    landed[(n_load + e) % SLOTS] += 16
                n_load += E
            else:
                landed[slot] += 16
                place[key] = (n_load, landed[slot])
                n_load += 1

        def piece_split(layer, x, c):
            value = 4 * x + 1 if x == 0 and c == 0 else 4 * x + (0, 2, 3, 5)[c]
            return 4 * X * layer + (4 * X if (x, c) == (X - 1, 3) else value)

        ADAS = [(0, s) for s in range(8)] + [(1, s) for s in range(8)]

        def mod_banks(i):
            return (bank[2], bank[3]) if i < 4 and i % 2 else (bank[6], bank[7])

        def slot_of(key):
            return ring[place[key][0] % SLOTS]

        block = ctx.enter_context(nc.Block())

        @block.sync
        def _(sp):
            sp.dma_start(par[:, :], par_in).then_inc(S("params_landed"), 16)
            sp.dma_start(cst[:, :], cst_in).then_inc(S("params_landed"), 16)
            sp.dma_start(xT[:, :, :], xT_in).then_inc(S("x_landed"), 16)

            adas = [n for n in NAMES if n.startswith("ada")]

            def released(key, e=0):
                if key[0] == "experts":
                    return "lo_ready", piece_split(key[1], e + 1, 3)
                if key[0] == "shared":
                    return "lo_ready", piece_split(key[1], 0, 3)
                name = key[1]
                layer, s = int(name[-3]) if name[0] != "c" else 1, int(name[-1])
                if name.startswith("ada"):
                    return "ada_used", adas.index(name) + 1
                if name.startswith("in0"):
                    return ("tok_ready", 1) if s == 0 else ("feat_ready", 6 * s)
                if name.startswith("in1"):
                    return [("tok_half", 1), ("tok_ready", 2)][s] if s < 2 else ("feat_ready", EV_TILES + 6 * (s - 1))
                if name.startswith("out"):
                    return "proj_ready", KT * layer + 4 * (s + 1)
                return "cmp_o", s + 1

            loads = []
            for key in order:
                loads += [(key, e) for e in range(E)] if key[0] == "experts" else [(key, 0)]

            def await_slot(n):
                if n >= SLOTS:
                    name, value = released(*loads[n - SLOTS])
                    sp.wait_ge(S(name), value)

            def stream(key):
                n = place[key][0]
                await_slot(n)
                if key[0] == "mix":
                    w = width_of(key[1])
                    src = mix_in[NAMES.index(key[1]), :, 0:w]
                else:
                    w, src = SLOTW, moe_in[key[1] * X, :, :]
                sp.dma_start(ring[n % SLOTS][:, 0:w], src).then_inc(S(f"slot_full{n % SLOTS}"), 16)

            def stream_experts(layer):
                n = place["shared", layer][0]

                def load_expert(x, r):
                    sp.dma_start(ring[r][:, :], moe_in[bass.ds(x + layer * X, 1), :, :]
                                 .rearrange("a p n -> (a p) n")).then_inc(S(f"slot_full{r}"), 16)

                def load_route(x, r):
                    sp.dma_start(route_w[r][:, :], w_dram[layer].ap()[bass.ds(x - 1, 1), :].to_broadcast([P, T])
                                 ).then_inc(S(f"route_full{r}"), 16)

                def both(x, k):
                    sp.wait_ge(S("lo_ready"), (x - SLOTS) * 4 + (4 * X * layer + 5))
                    load_expert(x, (n + k) % SLOTS)
                    sp.wait_ge(S("a_ready"), (x - SLOTS) * 2 + (2 * X * layer + 2))
                    load_route(x, (n + k) % SLOTS)

                for x in range(1, SLOTS):
                    await_slot(n + x)
                    load_expert(x, (n + x) % SLOTS)
                sp.wait_ge(S("route_stored"), 16 * (layer + 1))
                if layer:
                    sp.wait_ge(S("a_ready"), 2 * X * layer)
                for x in range(1, SLOTS):
                    load_route(x, (n + x) % SLOTS)
                both(SLOTS, SLOTS)
                with sp.Fori(0, (X - SLOTS - 2) // BODY) as step:
                    for k in range(SLOTS + 1, SLOTS + 1 + BODY):
                        both(step * BODY + k, k)
                for x in range(SLOTS + 1 + (X - SLOTS - 2) // BODY * BODY, X):
                    both(x, x)

            for key in order:
                if key == ("mix", "out0.0"):
                    sp.wait_ge(S("rel_copied"), 2)
                    dst = bass.AP(rel_dram, 0, [[P * (ROW + 1), NH], [ROW + 1, P], [1, ROW]])
                    sp.dma_start(dst, relrow[:, :].unsqueeze(1).to_broadcast([NH, P, ROW])
                                 ).then_inc(S("rel_stored"), 16)
                if key == ("mix", "in1.3"):
                    sp.wait_ge(S("rel_stored"), 16)
                    sp.wait_ge(S("x_added"), 2 * KT)
                    for t in range(NT):
                        src = bass.AP(rel_dram, 255 - P * t, [[ROW, P], [P * (ROW + 1), NH], [1, T]])
                        sp.dma_start(Brel[:, t, :, :], src).then_inc(S("brel_landed"), 16)
                if key[0] == "experts":
                    stream_experts(key[1])
                else:
                    stream(key)
            for m in range(KT):
                sp.wait_ge(S("x_added"), 3 * KT + m + 1)
                sp.dma_start(outT[:, m, :], xT[:, m, :]).then_inc(S("out_stored"), 16)
            sp.wait_ge(S("out_stored"), 16 * KT)

        @block.tensor
        def _(pe):
            def mm(out, lhsT, rhs, start, stop):
                return pe.matmul(out, lhsT, rhs, start=start, stop=stop)

            def tr(out, in_):
                return pe.transpose(out, in_, ident)

            def full(key):
                n, value = place[key]
                pe.wait_ge(S(f"slot_full{n % SLOTS}"), value)
                return slot_of(key)

            def mod_rows(i):
                w = full(("mix", "ada%d.%d" % ADAS[i]))[:, :].rearrange("p (k n) -> p k n", k=KT)
                if i >= 4:
                    pe.wait_ge(S("mod_copied"), i)
                elif i >= 2:
                    pe.wait_ge(S("mod_copied"), i - 1)
                for half, b in enumerate(mod_banks(i)):
                    for k in range(KT):
                        last = mm(b[0:1, 0:SC // 2], cond[:, k:k + 1], w[:, k, half * SC // 2:(half + 1) * SC // 2],
                                  k == 0, k == KT - 1)
                last.then_inc(S("ada_used"), 1)

            def mod_columns(i):
                pe.wait_ge(S("mod_row"), 2 * (i + 1))
                for m in range(6):
                    last = pe.transpose(mod_banks(i)[1][:, 400 + m:401 + m], modrow[0:1, m * P:(m + 1) * P],
                                        ident[0:1, 0:1])
                last.then_inc(S("mod_turned"), 1)

            def feature_sum(n):
                pe.wait_ge(S("sq_ready"), n)
                for k in range(KT):
                    last = mm(bank[4][:, 0:T], ones, yT[:, k, :], k == 0, k == KT - 1)
                last.then_inc(S("ss_ready"), 1)

            def project_tokens(w, c0, c1, dst):
                for t in range(NT):
                    for k in range(KT):
                        last = mm(dst[t], hT[:, k, t * P:(t + 1) * P], w[:, k, c0:c1], k == 0, k == KT - 1)
                return last

            def project_features(w, tiles, j0, first_tile):
                for m in range(tiles):
                    j = j0 + m
                    if j >= 3:
                        pe.wait_ge(S("feat_copied"), first_tile + j - 2)
                    for k in range(KT):
                        last = mm(bank[4 + j % 3][:, 0:T], w[:, k, m * P:(m + 1) * P], hT[:, k, :],
                                  k == 0, k == KT - 1)
                    last.then_inc(S("feat_ready"), 1)

            def out_projection(layer):
                pe.wait_ge(S("y_ready"), 2 * (layer + 1))
                pe.wait_ge(S("fox_o" if layer == 0 else "nsa_o"), 4)
                for s in range(2):
                    w = full(("mix", f"out{layer}.{s}"))[:, 0:KT * 512].rearrange("p (k n) -> p k n", k=KT)
                    for m in range(4):
                        j = 4 * s + m
                        if j >= 4:
                            pe.wait_ge(S("x_added"), 2 * KT * layer + j - 3)
                        for k in range(KT):
                            last = mm(bank[j % 4][:, 0:T], w[:, k, m * P:(m + 1) * P], yT[:, k, :],
                                      k == 0, k == KT - 1)
                        last.then_inc(S("proj_ready"), 1)

            def head_sums(weights, sq, tiles, banks):
                for b in range(tiles // 2):
                    last = mm(bank[banks[b]][:, :], weights, sq[:, 2 * b:2 * b + 2, :], True, True)
                return last

            def three(out, w, c, x2, start):
                (w_hi, w_lo), (x_hi, x_lo) = w, x2
                pe.matmul(out, w_hi[:, c:c + P], x_hi, start=start, stop=start, skip_group_check=not start)
                pe.matmul(out, w_hi[:, c:c + P], x_lo, start=False, stop=False, skip_group_check=True)
                return pe.matmul(out, w_lo[:, c:c + P], x_hi, start=False, stop=False, skip_group_check=True)

            def expert_up(ft, split_value):
                pe.wait_ge(S("lo_ready"), split_value)
                for part in range(2):
                    for k in range(KT):
                        last = three(bank[4 + ft][:, part * T:(part + 1) * T], piece[ft], (part * KT + k) * P,
                                     (h2[0][:, k, :], h2[1][:, k, :]), k == 0)
                last.then_inc(S("gu_ready"), 1)

            def expert_down(ft, split_value, a_value, opens):
                pe.wait_ge(S("lo_ready"), split_value)
                pe.wait_ge(S("a_ready"), a_value)
                for m in range(KT):
                    last = three(bank[m // 2][:, (m % 2) * T:(m % 2 + 1) * T], piece[2 + ft], m * P,
                                 (a2[0][:, ft, :], a2[1][:, ft, :]), opens and m % 2 == 0)
                last.then_inc(S("down_done"), 1)

            def moe(layer):
                feature_sum(2 * layer + 2)
                pe.wait_ge(S("h_ready"), 2 * layer + 2)
                for t in range(NT):
                    for k in range(KT):
                        last = mm(bank[6][:, t * E:(t + 1) * E], hT[:, k, t * P:(t + 1) * P],
                                  pr("router")[:, (layer * KT + k) * E:(layer * KT + k + 1) * E],
                                  k == 0, k == KT - 1)
                last.then_inc(S("router_ready"), 1)
                pe.wait_ge(S("h_split"), 2 * (layer + 1))
                sp0, a0 = 4 * X * layer, 2 * X * layer

                def step(x, opens=False, last_expert=False):
                    expert_up(1, x * 4 + (sp0 + 2))
                    expert_down(0, x * 4 + (sp0 + 3), x * 2 + (a0 + 1), opens)
                    if not last_expert:
                        expert_up(0, x * 4 + (sp0 + 4))
                    expert_down(1, sp0 + 4 * X if last_expert else x * 4 + (sp0 + 5), x * 2 + (a0 + 2), False)

                expert_up(0, sp0 + 1)
                expert_up(1, sp0 + 2)
                expert_down(0, sp0 + 3, a0 + 1, True)
                pe.wait_ge(S("route_ready"), layer + 1)
                for t in range(NT):
                    last = tr(bank[7][0:E, t * P:(t + 1) * P], wroute[:, t, :])
                last.then_inc(S("route_turned"), 1)
                expert_up(0, sp0 + 4)
                expert_down(1, sp0 + 5, a0 + 2, False)
                with pe.Fori(1, X - 1) as x:
                    step(x)
                step(X - 1, last_expert=True)

            pe.wait_ge(S("params_landed"), 32)
            pe.wait_ge(S("cond_ready"), 1)
            mod_rows(0)
            for i in range(1, 4):
                mod_rows(i)
                mod_columns(i - 1)
            mod_columns(3)
            feature_sum(1)
            pe.wait_ge(S("h_ready"), 1)
            w = full(("mix", "in0.0"))[:, 0:KT * (FH * FDH + EV_SMALL)].rearrange("p (k n) -> p k n", k=KT)
            project_tokens(w, 0, FH * FDH, [bank[0][:, :], bank[1][:, :]])
            project_tokens(w, FH * FDH, FH * FDH + EV_SMALL, [bank[2][:, 0:16], bank[3][:, 0:16]]
                           ).then_inc(S("tok_ready"), 1)
            for s in range(4):
                w = full(("mix", f"in0.{s + 1}"))[:, :].rearrange("p (k n) -> p k n", k=KT)
                project_features(w, 6, 6 * s, 0)

            pe.wait_ge(S("tok_copied"), 6)
            rel = pr("rel")[0:BUCKETS + 1, :]
            mm(bank[0][0:NH, :], rel, cs("ohr")[0:BUCKETS + 1, :], True, True)
            for t in range(NT):
                for n in range(NCMP):
                    d0 = 256 + P * t - CMP_STRIDE * n - CMP_LEN + 1
                    last = mm(bank[1][:, (t * NCMP + n) * NH:(t * NCMP + n + 1) * NH],
                              cs("ohf")[0:BUCKETS + 1, d0:d0 + P], rel, True, True)
            last.then_inc(S("rel_ready"), 1)

            pe.wait_ge(S("rel_copied"), 2)
            pe.wait_ge(S("fox_sq"), 4)
            head_sums(cs("bd"), yT, 8, [0, 1, 2, 3]).then_inc(S("fox_ss"), 1)
            pe.wait_ge(S("fox_qk"), 3)
            pe.wait_ge(S("logf_ready"), 1)

            units = [(h0 + i, qt) for h0 in range(0, FH, 2) for qt in range(NT) for i in range(2)]

            def fox_scores(u):
                h, qt = units[u]
                keys = P * (qt + 1)
                if u >= 2:
                    pe.wait_ge(S("fox_exp"), u - 1)
                s = bank[u % 2]
                mm(s[:, 0:keys], qpad[:, h, qt * P:(qt + 1) * P], feat[:, 4 + h // 2, 0:keys], True, False)
                mm(s[:, qt * P:(qt + 1) * P], ident, cs("maskq"), False, False)
                last = mm(s[:, 0:keys], logf[:, 0, h:h + 1].to_broadcast([P, P]), cs("ntri")[:, 0:keys],
                          False, qt == 0)
                if qt:
                    last = mm(s[:, P:2 * P], logf[:, 1, h:h + 1].to_broadcast([P, P]), cs("ntri")[:, 0:P],
                              False, True)
                last.then_inc(S("fox_s"), 1)

            def fox_turn(u):
                h, qt = units[u]
                pe.wait_ge(S("fox_p"), u + 1)
                if u >= 2:
                    pe.wait_ge(S("fox_pT"), u - 1)
                for k in range(qt + 1):
                    last = tr(bank[2 + u % 2][:, k * P:(k + 1) * P], prob[u % 2][:, k * P:(k + 1) * P])
                last.then_inc(S("fox_turned"), 1)

            def fox_values(u):
                h, qt = units[u]
                pe.wait_ge(S("fox_pT"), u + 1)
                if u % 4 == 0 and u >= 8:
                    pe.wait_ge(S("fox_o"), u // 4 - 1)
                for k in range(qt + 1):
                    last = mm(bank[4 + u // 4 % 2][:, qt * P:(qt + 1) * P], vpad[:, k, h, :],
                              probT[u % 2][:, k * P:(k + 1) * P], h % 2 == 0 and k == 0, h % 2 == 1 and k == qt)
                last.then_inc(S("fox_pv"), 1)

            for u in range(len(units) + 2):
                if u < len(units):
                    fox_scores(u)
                if 1 <= u <= len(units):
                    fox_turn(u - 1)
                if u >= 2:
                    fox_values(u - 2)
                if 1 <= u < 12:
                    (mod_rows if u % 2 else mod_columns)(4 + (u - 1) // 2)

            pe.wait_ge(S("gdn_sq"), 4)
            pe.wait_ge(S("fox_pT"), len(units))
            head_sums(ones, squares, 8, [0, 1, 2, 3]).then_inc(S("gdn_ss"), 1)
            mod_columns(9)
            mod_rows(10)
            mod_columns(10)
            pe.wait_ge(S("mod_copied"), 11)
            pe.wait_ge(S("gdn_g"), 1)
            for t in range(NT):
                last = mm(bank[6][:, t * GH:(t + 1) * GH], cs("tri"), gate[:, t, :], True, True)
            last.then_inc(S("gdn_cum"), 1)
            pe.wait_ge(S("gdn_qk"), 4)
            pe.wait_ge(S("gdn_rms"), 4)
            pe.wait_ge(S("fox_o"), 4)
            for t in range(NT):
                for h in range(GH):
                    cols = slice(h * P, (h + 1) * P)
                    g = gate[:, t, h:h + 1].to_broadcast([P, P])
                    mm(bank[3 * t][:, cols], g, cs("tri"), True, True)
                    mm(bank[3 * t + 1][:, cols], g, cs("tri"), True, False)
                    mm(bank[3 * t + 1][:, cols], ident, cs("mpos"), False, True)
                    mm(bank[3 * t + 2][:, cols], g, cs("tri"), True, False)
                    last = mm(bank[3 * t + 2][:, cols], ident, cs("mneg"), False, True)
            last.then_inc(S("gdn_gb"), 1)
            pe.wait_ge(S("gdn_gc"), 2)
            for t in range(NT):
                for h in range(GH):
                    k = feat[:, 12 + h, t * P:(t + 1) * P]
                    last = mm(bank[6 + t][:, h * P:(h + 1) * P], k, k, True, True)
            last.then_inc(S("gdn_kk"), 1)
            pe.wait_ge(S("gdn_decay"), 18)
            for t in range(NT):
                for h in range(GH):
                    k = feat[:, 12 + h, t * P:(t + 1) * P]
                    mm(bank[t][:, h * P:(h + 1) * P], k, feat[:, 8 + h, t * P:(t + 1) * P], True, True)
                    tr(bank[2 + t][:, h * P:(h + 1) * P], k)
                    last = tr(bank[4 + t][:, h * P:(h + 1) * P], feat[:, 16 + h, t * P:(t + 1) * P])
            last.then_inc(S("gdn_turned"), 1)
            pe.wait_ge(S("gdn_a"), 8)
            for t in range(NT):
                for h in range(GH):
                    last = tr(bank[6 + t][:, h * P:(h + 1) * P], Am[:, t, h, :])
            last.then_inc(S("gdn_at"), 1)
            pe.wait_ge(S("gdn_kv"), 8)
            pe.wait_ge(S("gdn_attn"), 2)
            for lv in range(1, len(LEVELS)):
                pe.wait_ge(S("inv_x"), 2 + 4 * (lv - 1))
                pe.wait_ge(S("inv_atm"), lv)
                for t in range(NT):
                    for h in range(GH):
                        last = mm(bank[t][:, h * P:(h + 1) * P], ATm[lv % 2][:, t, h, :], Xi[:, t, h, :],
                                  True, True)
                last.then_inc(S("inv_p"), 1)
                if lv == 1:
                    pe.wait_ge(S("gdn_atc"), 2)
                if lv <= 4:
                    mod_rows(10 + lv)
                pe.wait_ge(S("inv_pc"), 2 * lv)
                for t in range(NT):
                    for h in range(GH):
                        cols = slice(h * P, (h + 1) * P)
                        if lv < len(LEVELS) - 1:
                            mm(bank[2 + t][:, cols], XT[:, t, h, :], Pm[:, t, h, :], True, True)
                        last = mm(bank[4 + t][:, cols], Pm[:, t, h, :], XT[:, t, h, :], True, True)
                last.then_inc(S("inv_xp"), 1)
                if lv <= 4:
                    mod_columns(10 + lv)
            pe.wait_ge(S("inv_x"), INVX)
            pe.wait_ge(S("mod_copied"), 15)
            for t in range(NT):
                for h in range(GH):
                    cols = slice(h * P, (h + 1) * P)
                    mm(bank[6 + t][:, cols], XT[:, t, h, :], vb[:, t, h, :], True, True)
                    last = mm(bank[t][:, cols], kbe[:, t, h, :], XT[:, t, h, :], True, True)
            last.then_inc(S("gdn_uw"), 1)
            for n in range(NCH):
                t, half = n // 2, n % 2
                c0 = half * CHUNK
                if n:
                    pe.wait_ge(S("gdn_state"), 1 + GH * (n - 1))
                    pe.wait_ge(S("gdn_uwc"), 4)
                    for h in range(GH):
                        last = mm(bank[2][:, h * P:(h + 1) * P], wT[:, t, h, :], state[:, h, :], True, True)
                    last.then_inc(S("gdn_ws"), 1)
                pe.wait_ge(S("gdn_vn"), n + 1)
                if n < NCH - 1:
                    for h in range(GH):
                        last = mm(bank[4][:, h * P:(h + 1) * P], kd[half][:, t, h, :], vnew[:, h, :], True, True)
                    last.then_inc(S("gdn_su"), 1)
                if n:
                    pe.wait_ge(S("gdn_oc"), n)
                    pe.wait_ge(S("gdn_qd"), 2)
                for h in range(GH):
                    o = bank[3][:, h * CHUNK:(h + 1) * CHUNK]
                    if n:
                        mm(o, state[:, h, :], feat[:, 8 + h, t * P + c0:t * P + c0 + CHUNK], True, False)
                    last = mm(o, vnew[:, h, :], attnT[:, t, h, c0:c0 + CHUNK], n == 0, True)
                last.then_inc(S("gdn_o"), 1)
            pe.wait_ge(S("og_sq"), 2)
            for b in range(2):
                last = mm(bank[5 + b][:, :], ones, osq[:, 2 * b:2 * b + 2, :], True, True)
            last.then_inc(S("og_ss"), 1)
            pe.wait_ge(S("og_rms"), 2)
            mod_rows(15)
            mod_columns(15)
            out_projection(0)
            moe(0)

            feature_sum(3)
            pe.wait_ge(S("h_ready"), 3)
            w = full(("mix", "in1.0"))[:, :].rearrange("p (k n) -> p k n", k=KT)
            project_tokens(w, 0, 512, [bank[0][:, :], bank[1][:, :]])
            project_tokens(w, 512, OD_TOK, [bank[2][:, 0:256], bank[3][:, 0:256]]).then_inc(S("tok_half"), 1)
            w = full(("mix", "in1.1"))[:, 0:KT * (OD_GATES + LRANK)].rearrange("p (k n) -> p k n", k=KT)
            project_tokens(w, 0, OD_GATES, [bank[2][:, 256:256 + OD_GATES], bank[3][:, 256:256 + OD_GATES]])
            for k in range(KT):
                last = mm(bank[7][0:LRANK, 0:T], w[:, k, OD_GATES:OD_GATES + LRANK], hT[:, k, :],
                          k == 0, k == KT - 1)
            last.then_inc(S("tok_ready"), 1)
            for s in range(3):
                w = full(("mix", f"in1.{s + 2}"))[:, :].rearrange("p (k n) -> p k n", k=KT)
                project_features(w, 6, 6 * s, EV_TILES)
            pe.wait_ge(S("tok_copied"), 17)
            for t in range(NT):
                last = mm(bank[0][:, t * 256:(t + 1) * 256], lgT[0:LRANK, t * P:(t + 1) * P],
                          pr("wg_up")[0:LRANK, :], True, True)
            last.then_inc(S("gla_z"), 1)
            pe.wait_ge(S("cmp_blk"), 8)
            for kv in range(2):
                w = full(("mix", f"cmp.{kv}"))
                for ht in range(2):
                    for l in range(16):
                        last = mm(bank[2 + kv][:, ht * 32:ht * 32 + 2 * NCMP],
                                  w[:, l * CHID + ht * P:l * CHID + (ht + 1) * P], blk[:, kv, l, :],
                                  l == 0, l == 15)
                last.then_inc(S("cmp_h"), 1)
            for kv in range(2):
                w = full(("mix", f"cmp.{kv}"))
                pe.wait_ge(S("cmp_a"), kv + 1)
                if kv == 0:
                    for n, (ht, g) in enumerate([(a, b) for a in range(2) for b in range(2)]):
                        c = 16 * CHID + (ht * 2 + g) * P
                        last = mm(bank[2][:, 256:256 + NCMP], w[:, c:c + P],
                                  chid[:, kv, ht, g * NCMP:(g + 1) * NCMP], n == 0, n == 3)
                else:
                    for g in range(NKV):
                        for ht in range(2):
                            c = 16 * CHID + ht * NDH
                            last = mm(bank[3][0:NCMP, 256 + g * NDH:256 + (g + 1) * NDH],
                                      chid[:, kv, ht, g * NCMP:(g + 1) * NCMP], w[:, c:c + NDH],
                                      ht == 0, ht == 1)
                last.then_inc(S("cmp_o"), 1)
            pe.wait_ge(S("nsa_sq"), 3)
            pe.wait_ge(S("feat_copied"), EV_TILES + OD_TILES)
            for b in range(3):
                mm(bank[4 + b][:, :], cs("bd"), yT[:, 2 * b:2 * b + 2, :], True, True)
            pe.wait_ge(S("cmp_sq"), 1)
            mm(bank[7][:, 0:NCMP], cs("bd"), csq[:, :], True, True).then_inc(S("nsa_ss"), 1)
            pe.wait_ge(S("nsa_qk"), 4)
            pe.wait_ge(S("cmp_kv"), 3)
            pe.wait_ge(S("nsa_rms"), 4)
            pe.wait_ge(S("gla_zc"), 1)

            nunits = [(h0 + i, qt) for h0 in range(4) for qt in range(NT) for i in (0, 4)]

            def nsa_scores(u):
                h, qt = nunits[u]
                keys = P * (qt + 1)
                if u >= 2:
                    pe.wait_ge(S("nsa_b"), 2 * (u - 1))
                q = qpad[:, h, qt * P:(qt + 1) * P]
                for br in range(2):
                    mm(bank[u % 2][:, br * T:br * T + keys], q, feat[:, 4 + br, 0:keys], True, True)
                if u:
                    pe.wait_ge(S("nsa_b"), 2 * u)
                mm(bank[6][:, 0:NCMP], q, kcn[:, :], True, True).then_inc(S("nsa_s"), 1)

            def nsa_turn(u):
                h, qt = nunits[u]
                pe.wait_ge(S("nsa_p"), 3 * (u + 1))
                if u >= 2:
                    pe.wait_ge(S("nsa_pT"), 2 * (u - 1))
                for br in range(2):
                    for k in range(qt + 1):
                        c = br * T + k * P
                        tr(bank[2 + u % 2][:, c:c + P], nprob[u % 2][:, c:c + P])
                if u:
                    pe.wait_ge(S("nsa_pT"), 2 * u)
                tr(bank[7][0:NCMP, 0:P], nprob[u % 2][:, 512:512 + NCMP]
                   ).then_inc(S("nsa_turned"), 1)

            def nsa_values(u):
                h, qt = nunits[u]
                g = h // 4
                pe.wait_ge(S("nsa_pT"), 2 * (u + 1))
                if u % 4 == 0 and u >= 8:
                    pe.wait_ge(S("nsa_o"), u // 4 - 1)
                out = bank[4 + u // 4 % 2][:, qt * P:(qt + 1) * P]
                mm(out, vcpad[0:NCMP, g, :], nprobT[u % 2][0:NCMP, 512:512 + P], g == 0, False)
                for br in range(2):
                    for k in range(qt + 1):
                        c = br * T + k * P
                        last = mm(out, nvpad[:, k, br, g, :], nprobT[u % 2][:, c:c + P], False,
                                  g == 1 and br == 1 and k == qt)
                last.then_inc(S("nsa_pv"), 1)

            for u in range(len(nunits) + 2):
                if u < len(nunits):
                    nsa_scores(u)
                if 1 <= u <= len(nunits):
                    nsa_turn(u - 1)
                if u >= 2:
                    nsa_values(u - 2)

            pe.wait_ge(S("gla_loga"), 1)
            pe.wait_ge(S("nsa_pT"), 2 * len(nunits))
            pe.wait_ge(S("nsa_o"), 4)
            for f in range(2):
                for t in range(NT):
                    last = mm(bank[0][:, (f * NT + t) * P:(f * NT + t + 1) * P], loga[:, t, f * P:(f + 1) * P],
                              cs("tri"), True, True)
            last.then_inc(S("gla_G"), 1)
            pe.wait_ge(S("gla_qk"), 4)
            for t in range(NT):
                for h in range(LH):
                    last = mm(bank[1 + t][:, h * P:(h + 1) * P], lki[:, h // 2, t * P:(t + 1) * P],
                              lqd[:, h, t * P:(t + 1) * P], True, True)
            for t in range(NT):
                for f in range(2):
                    last = tr(bank[3][:, (t * 2 + f) * P:(t * 2 + f + 1) * P], lkd[:, f, t * P:(t + 1) * P])
            last.then_inc(S("gla_at"), 1)
            pe.wait_ge(S("gla_ready"), 4)
            for n in range(NCH):
                t, half = n // 2, n % 2
                c0 = t * P + half * CHUNK
                if n:
                    pe.wait_ge(S("gla_state"), 1 + LH * (n - 1))
                if n < NCH - 1:
                    for h in range(LH):
                        last = mm(bank[5][:, h * P:(h + 1) * P], lkt[:, half, t, h // 2, :],
                                  toks[:, t, h * P:(h + 1) * P], True, True)
                    last.then_inc(S("gla_su"), 1)
                if n:
                    pe.wait_ge(S("gla_oc"), n)
                for h in range(LH):
                    o = bank[6][:, h * CHUNK:(h + 1) * CHUNK]
                    if n:
                        mm(o, lstate[:, h, :], lqd[:, h, c0:c0 + CHUNK], True, False)
                    last = mm(o, toks[:, t, h * P:(h + 1) * P],
                              lattn[:, t, h, half * CHUNK:(half + 1) * CHUNK], n == 0, True)
                last.then_inc(S("gla_o"), 1)
            pe.wait_ge(S("og_sq"), 4)
            for b in range(2):
                last = mm(bank[1 + b][:, :], ones, osq[:, 2 * b:2 * b + 2, :], True, True)
            last.then_inc(S("og_ss"), 1)
            out_projection(1)
            moe(1)

        @block.scalar
        def _(sc):
            count = [0]

            def act(out, in_, func, name=None, **kw):
                kw.setdefault("bias", eps(ZERO)[0:out.shape[0], :])
                ins = sc.activation(out, in_, func, **kw)
                if name is None:
                    count[0] += 1
                    ins.then_inc(S("act_chain"), 1)
                    sc.wait_ge(S("act_chain"), count[0])
                else:
                    ins.then_inc(S(name), 1)

            def copy(out, in_, name):
                sc.activation(out, in_, ACT.Copy).then_inc(S(name), 1)

            def rms_root(n):
                sc.wait_ge(S("ss_ready"), n)
                act(rms[:, :], bank[4][:, 0:T], ACT.Sqrt, "rms_root", scale=1.0 / D, bias=eps(EPS1))

            def log_part(x, out, name):
                act(out, x, ACT.Abs)
                act(out, out, ACT.Exp, scale=-1.0)
                act(out, out, ACT.Ln, name, bias=eps(ONE))

            def copy_features(first, tiles):
                for j in range(first, first + tiles):
                    sc.wait_ge(S("feat_ready"), j + 1)
                    copy(feat[:, j - first, :], bank[4 + (j - first) % 3][:, 0:T], "feat_copied")

            def mod_evac(i):
                sc.wait_ge(S("ada_used"), i + 1)
                if i:
                    sc.wait_ge(S("mod_turned"), i)
                for half, b in enumerate(mod_banks(i)):
                    copy(modrow[0:1, half * SC // 2:(half + 1) * SC // 2], b[0:1, 0:SC // 2], "mod_row")

            def moe(layer):
                n = place["shared", layer][0]
                full0 = [place["shared", layer][1]] + place["experts", layer][1]
                gu0, dn0, hi0 = 2 * X * layer, 2 * X * layer, 4 * X * layer

                def high(x, c, k, step=None):
                    r = (n + k) % SLOTS
                    if c in (0, 1):
                        sc.wait_ge(S(f"slot_full{r}"), full0[k] if step is None else step * 16 + full0[k])
                    if k or layer:
                        name, value = (("gu_ready", x * 2 + (gu0 - 1 + c)) if c < 2 else
                                       ("down_done", x * 2 + (dn0 - 3 + c)))
                        sc.wait_ge(S(name), value)
                    w = ring[r][:, AT_PIECE[c]:AT_PIECE[c] + PIECE[c]]
                    copy(piece[c][0][:, :], w, "hi_ready")

                def silu(x, ft):
                    sc.wait_ge(S("gu_ready"), x * 2 + (gu0 + ft + 1))
                    act(silu_g[:, ft, :], bank[4 + ft][:, 0:T], ACT.Silu, "silu_ready")

                def step(x, k, loop=None, has_next=True, has_after=True):
                    silu(x, 1)
                    if has_next:
                        high(x + 1, 1, k + 1, loop)
                        high(x + 1, 2, k + 1, loop)
                        silu(x + 1, 0)
                        if has_after:
                            high(x + 2, 0, k + 2, loop)
                        high(x + 1, 3, k + 1, loop)

                sc.wait_ge(S("y_ready"), 2 * (layer + 1))
                high(0, 0, 0)
                high(0, 1, 0)
                high(0, 2, 0)
                rms_root(2 * layer + 2)
                sc.wait_ge(S("router_ready"), layer + 1)
                act(rscore[:, :, :], bank[6][:, 0:NT * E].rearrange("p (a b) -> p a b", a=NT), ACT.Sigmoid,
                    "score_ready")
                sc.wait_ge(S("h_ready"), 2 * layer + 2)
                copy(h2[0][:, :, :], hT[:, :, :], "h_high")
                silu(0, 0)
                high(1, 0, 1)
                high(0, 3, 0)
                silu(0, 1)
                high(1, 1, 1)
                high(1, 2, 1)
                sc.wait_ge(S("route_turned"), layer + 1)
                copy(wTs[:, :], bank[7][0:E, 0:T], "route_copied")
                sc.wait_ge(S("route_copied"), layer + 1)
                sc.dma_start(w_dram[layer].ap(), wTs[:, :]).then_inc(S("route_stored"), 16)
                silu(1, 0)
                high(2, 0, 2)
                high(1, 3, 1)
                with sc.Fori(0, LOOPS) as i:
                    for k in range(1, BODY + 1):
                        step(i * BODY + k, k, i)
                for x in range(TAIL, X):
                    step(x, x, has_next=x + 1 < X, has_after=x + 2 < X)

            sc.wait_ge(S("params_landed"), 32)
            act(cond[:, :], pr("c"), ACT.Silu, "cond_ready")
            act(sl("ea", (GH,)), pr("a_log"), ACT.Exp, "ea_ready")
            for i in range(4):
                mod_evac(i)
            rms_root(1)
            sc.wait_ge(S("pads_zero"), 2)
            sc.wait_ge(S("tok_ready"), 1)
            for t in range(NT):
                v = bank[t][:, :].rearrange("p (h d) -> p h d", d=FDH)
                for odd in range(2):
                    copy(vpad[:, t, odd::2, odd * FDH:(odd + 1) * FDH], v[:, odd::2, :], "tok_copied")
                copy(sml[:, t, :], bank[2 + t][:, 0:EV_SMALL], "tok_copied")
            copy_features(0, EV_TILES)
            z, lg = sl("z", (NT, EV_SMALL)), sl("lg", (NT, EV_SMALL))
            sc.wait_ge(S("z_ready"), 3)
            act(sl("beta", (NT, GH)), z[:, :, FH + GH:EV_SMALL], ACT.Sigmoid, "beta_ready")
            log_part(z[:, :, 0:FH + GH], lg[:, :, 0:FH + GH], "lg_ready")
            sc.wait_ge(S("rel_ready"), 1)
            copy(relrow[:, :], bank[0][0:NH, :], "rel_copied")
            copy(relc[:, :, :, :].rearrange("p a b c -> p (a b c)"), bank[1][:, 0:NT * NCMP * NH], "rel_copied")
            for b in range(4):
                sc.wait_ge(S("fox_ss"), 1)
                act(frms[:, 2 * b:2 * b + 2, :].rearrange("p a b -> p (a b)"), bank[b][:, :], ACT.Sqrt, "fox_rms",
                    scale=1.0 if b < 2 else 1.0 / FDH, bias=eps(EPS64 if b < 2 else EPS1))
            for u in range(4 * FH // 2 + 1):
                if u < 4 * FH // 2:
                    keys = P * (u // 2 % 2 + 1)
                    sc.wait_ge(S("fox_nmax"), u + 1)
                    if u >= 2:
                        sc.wait_ge(S("fox_turned"), u - 1)
                    act(prob[u % 2][:, 0:keys], bank[u % 2][:, 0:keys], ACT.Exp, "fox_exp",
                        bias=sl("nmx", (12,))[:, u % 2:u % 2 + 1], accum_out=sl("rs", (12,))[:, u % 2:u % 2 + 1])
                if u >= 1:
                    keys = P * ((u - 1) // 2 % 2 + 1)
                    sc.wait_ge(S("fox_turned"), u)
                    if u >= 3:
                        sc.wait_ge(S("fox_pv"), u - 2)
                    copy(probT[(u - 1) % 2][:, 0:keys], bank[2 + (u - 1) % 2][:, 0:keys], "fox_pT")
                if 1 <= u < 12 and u % 2:
                    mod_evac(4 + (u - 1) // 2)
                if u >= 4 and u % 4 == 0 and u < 4 * FH // 2:
                    sc.wait_ge(S("fox_pv"), u)
                    copy(yT[:, u // 4 - 1, :], bank[4 + (u // 4 - 1) % 2][:, 0:T], "fox_o")
            sc.wait_ge(S("fox_pv"), 4 * FH // 2)
            copy(yT[:, FH // 2 - 1, :], bank[4 + (FH // 2 - 1) % 2][:, 0:T], "fox_o")

            sc.wait_ge(S("conv_ready"), 12)
            for b in range(6):
                act(feat[:, 8 + 2 * b:10 + 2 * b, :], conv[:, 2 * b:2 * b + 2, :], ACT.Silu, "gdn_silu")
            for b in range(2):
                act(feat[:, 20 + 2 * b:22 + 2 * b, :], feat[:, 20 + 2 * b:22 + 2 * b, :], ACT.Silu, "gdn_silu")
            sc.wait_ge(S("gdn_ss"), 1)
            for b in range(4):
                act(frms[:, 2 * b:2 * b + 2, :].rearrange("p a b -> p (a b)"), bank[b][:, :], ACT.Sqrt, "gdn_rms",
                    scale=float(GD) if b < 2 else 1.0, bias=eps(EPS128 if b < 2 else EPS1))
            mod_evac(10)
            sc.wait_ge(S("gdn_gc"), 2)
            gc, ngc = sl("gc", (8,)), sl("ngc", (8,))
            act(sl("eg", (8,)), gc, ACT.Exp, "gdn_eg")
            sc.wait_ge(S("gdn_gb"), 1)
            for t in range(NT):
                act(Eb[:, t, :, :].rearrange("p a b -> p (a b)"), bank[3 * t][:, :], ACT.Exp, "gdn_decay")
                for h in range(GH):
                    i, cols = t * GH + h, slice(h * P, (h + 1) * P)
                    act(Dm[:, t, h, :], bank[3 * t + 1][:, cols], ACT.Exp, "gdn_decay", scale=-1.0,
                        bias=gc[:, i:i + 1])
                    act(DT[:, t, h, :], bank[3 * t + 2][:, cols], ACT.Exp, "gdn_decay", bias=ngc[:, i:i + 1])
            sc.wait_ge(S("gdn_at"), 1)
            for t in range(NT):
                copy(AT[:, t, :, :].rearrange("p a b -> p (a b)"), bank[6 + t][:, :], "gdn_atc")
            for lv in range(1, len(LEVELS)):
                sc.wait_ge(S("inv_p"), lv)
                if lv > 1:
                    sc.wait_ge(S("inv_xp"), lv - 1)
                for t in range(NT):
                    copy(Pm[:, t, :, :].rearrange("p a b -> p (a b)"), bank[t][:, :], "inv_pc")
                if lv <= 4:
                    mod_evac(10 + lv)
            sc.wait_ge(S("gdn_uw"), 1)
            for t in range(NT):
                copy(wT[:, t, :, :].rearrange("p a b -> p (a b)"), bank[t][:, :], "gdn_uwc")
            for n in range(NCH):
                sc.wait_ge(S("gdn_o"), n + 1)
                copy(og[:, :, n * CHUNK:(n + 1) * CHUNK], bank[3][:, 0:GH * CHUNK].rearrange(
                    "p (h c) -> p h c", h=GH), "gdn_oc")
            sc.wait_ge(S("og_ss"), 1)
            for b in range(2):
                act(orms[:, 2 * b:2 * b + 2, :].rearrange("p a b -> p (a b)"), bank[5 + b][:, :], ACT.Sqrt, "og_rms",
                    scale=1.0 / GD, bias=eps(EPS1))
            mod_evac(15)
            moe(0)

            rms_root(3)
            sc.wait_ge(S("pads_zero"), 5)
            sc.wait_ge(S("tok_ready"), 2)
            for t in range(NT):
                v = bank[t][:, 0:2 * NKV * NDH].rearrange("p (b g d) -> p b g d", b=2, g=NKV)
                for g in range(NKV):
                    copy(nvpad[:, t, :, g, g * NDH:(g + 1) * NDH], v[:, :, g, :], "tok_copied")
                copy(toks[:, t, 0:256], bank[t][:, 256:512], "tok_copied")
                copy(toks[:, t, 256:512], bank[2 + t][:, 0:256], "tok_copied")
            copy(lgT[0:LRANK, :], bank[7][0:LRANK, 0:T], "tok_copied")
            for t in range(NT):
                act(sl("ngate", (NT, OD_GATES))[:, t, :], bank[2 + t][:, 256:256 + OD_GATES], ACT.Sigmoid,
                    "tok_copied")
            copy_features(EV_TILES, OD_TILES)
            sc.wait_ge(S("gla_zc"), 1)
            log_part(lz, loga, "gla_lg")
            for kv in range(2):
                sc.wait_ge(S("cmp_h"), kv + 1)
                h = bank[2 + kv][:, 0:64].rearrange("p (a b) -> p a b", a=2)[:, :, 0:NKV * NCMP]
                act(chid[:, kv, :, :], h, ACT.Silu, "cmp_a")
            sc.wait_ge(S("cmp_o"), 1)
            copy(kcn, bank[2][:, 256:256 + NCMP], "cmp_kv")
            sc.wait_ge(S("cmp_o"), 2)
            for g in range(NKV):
                copy(vcpad[0:NCMP, g, g * NDH:(g + 1) * NDH], bank[3][0:NCMP, 256 + g * NDH:256 + (g + 1) * NDH],
                     "cmp_kv")
            sc.wait_ge(S("nsa_ss"), 1)
            for b in range(3):
                act(nrms[:, 2 * b:2 * b + 2, :].rearrange("p a b -> p (a b)"), bank[4 + b][:, :], ACT.Sqrt, "nsa_rms",
                    scale=1.0 if b < 2 else 1.0 / NDH, bias=eps(EPS64 if b < 2 else EPS1))
            act(sl("crms", (16,))[:, 0:NCMP], bank[7][:, 0:NCMP], ACT.Sqrt, "nsa_rms", scale=1.0 / NDH,
                bias=eps(EPS1))
            units = 2 * NH
            for u in range(units + 1):
                if u < units:
                    keys, c = P * (u // 2 % 2 + 1), 3 * (u % 2)
                    nm, rs = sl("nmx", (12,)), sl("rs", (12,))
                    sc.wait_ge(S("nsa_nmax"), u + 1)
                    act(nprob[u % 2][:, 512:512 + NCMP], nprob[u % 2][:, 512:512 + NCMP], ACT.Exp, "nsa_exp",
                        bias=nm[:, c:c + 1], accum_out=rs[:, c:c + 1])
                    for br in range(2):
                        p = nprob[u % 2][:, br * T:br * T + keys]
                        act(p, p, ACT.Exp, "nsa_exp", bias=nm[:, c + br + 1:c + br + 2],
                            accum_out=rs[:, c + br + 1:c + br + 2])
                if u >= 1:
                    v, qt = u - 1, (u - 1) // 2 % 2
                    sc.wait_ge(S("nsa_turned"), u)
                    if u >= 3:
                        sc.wait_ge(S("nsa_pv"), u - 2)
                    src, dst = (x[:, 0:512].rearrange("p (b k) -> p b k", b=2)[:, :, 0:P * (qt + 1)]
                                for x in (bank[2 + v % 2], nprobT[v % 2]))
                    copy(dst, src, "nsa_pT")
                    copy(nprobT[v % 2][0:NCMP, 512:512 + P], bank[7][0:NCMP, 0:P], "nsa_pT")
                if u >= 4 and u % 4 == 0 and u < units:
                    sc.wait_ge(S("nsa_pv"), u)
                    copy(yT[:, u // 4 - 1, :], bank[4 + (u // 4 - 1) % 2][:, 0:T], "nsa_o")
            sc.wait_ge(S("nsa_pv"), units)
            copy(yT[:, 3, :], bank[5][:, 0:T], "nsa_o")
            sc.wait_ge(S("gla_Gc"), 1)
            act(EG, G, ACT.Exp, "gla_exp")
            act(EnG, G, ACT.Exp, "gla_exp", scale=-1.0)
            sc.wait_ge(S("gla_dG"), 1)
            act(edG, edG, ACT.Exp, "gla_exp")
            for b in range(2):
                act(feat[:, 10 + 2 * b:12 + 2 * b, :], feat[:, 10 + 2 * b:12 + 2 * b, :], ACT.Silu, "gla_silu")
            for n in range(NCH):
                sc.wait_ge(S("gla_o"), n + 1)
                copy(og[:, :, n * CHUNK:(n + 1) * CHUNK], bank[6][:, 0:LH * CHUNK].rearrange(
                    "p (h c) -> p h c", h=LH), "gla_oc")
            sc.wait_ge(S("og_ss"), 2)
            for b in range(2):
                act(orms[:, 2 * b:2 * b + 2, :].rearrange("p a b -> p (a b)"), bank[1 + b][:, :], ACT.Sqrt, "og_rms",
                    scale=1.0 / LDV, bias=eps(EPS1))
            moe(1)

        @block.vector
        def _(ve):
            count = [0]

            def chain(ins):
                count[0] += 1
                ins.then_inc(S("vec_chain"), 1)
                ve.wait_ge(S("vec_chain"), count[0])

            def sig(ins, name):
                ins.then_inc(S(name), 1)

            def mod_add(i):
                ve.wait_ge(S("mod_turned"), i + 1)
                sig(ve.tensor_tensor(mod[:, 6 * i:6 * i + 6], mod_banks(i)[1][:, 400:406],
                                     pr("ada_b")[:, 6 * i:6 * i + 6], ALU.add), "mod_copied")

            def norm(n):
                layer, half = (n - 1) // 2, (n - 1) % 2
                for b in range(4):
                    x2 = xT[:, 2 * b:2 * b + 2, :]
                    last = ve.tensor_tensor(yT[:, 2 * b:2 * b + 2, :], x2, x2, ALU.mult)
                    if b < 3:
                        chain(last)
                sig(last, "sq_ready")
                if n == 1:
                    for i in range(4):
                        mod_add(i)
                ve.wait_ge(S("mod_copied"), 4 if n == 1 else 16)
                m0 = 48 * layer + 24 * half
                g0 = pr("norm_ffn" if half else "norm_mix")[:, layer * KT:(layer + 1) * KT]
                chain(ve.scalar_tensor_tensor(gain[:, :], mod[:, m0 + KT:m0 + 2 * KT], 1.0, g0, ALU.add, ALU.mult))
                ve.wait_ge(S("rms_root"), n)
                chain(ve.reciprocal(rms[:, :], rms[:, :]))
                for k in range(KT):
                    chain(ve.scalar_tensor_tensor(hT[:, k, :], xT[:, k, :], gain[:, k:k + 1], rms[:, :],
                                                  ALU.mult, ALU.mult))
                for k in range(KT):
                    last = ve.tensor_scalar(hT[:, k, :], hT[:, k, :], mod[:, m0 + k:m0 + k + 1], None, ALU.add)
                    if k < KT - 1:
                        chain(last)
                sig(last, "h_ready")

            def add_to_x(source, layer, half, m):
                g = 48 * layer + 24 * half + 2 * KT + m
                sig(ve.scalar_tensor_tensor(xT[:, m, :], source, mod[:, g:g + 1], xT[:, m, :], ALU.mult, ALU.add),
                    "x_added")
                ve.wait_ge(S("x_added"), 2 * KT * layer + KT * half + m + 1)

            def mixer_residual(layer):
                for m in range(KT):
                    ve.wait_ge(S("proj_ready"), KT * layer + m + 1)
                    add_to_x(bank[m % 4][:, 0:T], layer, 0, m)

            def pick(v, thr, k, n, out, buf):
                eq, gt, run = buf[0][:, :, 0:n], buf[1][:, :, 0:n], [buf[2][:, :, 0:n], buf[3][:, :, 0:n]]
                left = sl("left", (NT, 2))[:, :, 0:1]
                chain(ve.tensor_tensor(eq, v, thr.to_broadcast([P, NT, n]), ALU.is_equal))
                chain(ve.tensor_tensor(gt, v, thr.to_broadcast([P, NT, n]), ALU.is_gt))
                chain(ve.tensor_reduce(left, gt, AX.X, ALU.add))
                chain(ve.tensor_scalar(left, left, -1.0, float(k), ALU.mult, ALU.add))
                src, step, i = eq, 1, 0
                while step < n:
                    dst = run[i % 2]
                    chain(ve.tensor_copy(dst[:, :, 0:step], src[:, :, 0:step]))
                    chain(ve.tensor_tensor(dst[:, :, step:n], src[:, :, step:n], src[:, :, 0:n - step], ALU.add))
                    src, step, i = dst, 2 * step, i + 1
                other = run[i % 2]
                chain(ve.tensor_tensor(other, src, left.to_broadcast([P, NT, n]), ALU.is_le))
                chain(ve.tensor_tensor(other, other, eq, ALU.mult))
                chain(ve.tensor_tensor(out, other, gt, ALU.add))

            def routing(layer):
                ve.wait_ge(S("score_ready"), layer + 1)
                bias = pr("e_bias")[:, layer * E:(layer + 1) * E]
                for t in range(NT):
                    chain(ve.tensor_tensor(rbias[:, t, :], rscore[:, t, :], bias, ALU.add))
                m8, gs, gm = sl("m8", (NT * GROUPS, 8)), sl("gs", (NT, GROUPS)), sl("gm", (NT, GROUPS))
                for t in range(NT):
                    for g in range(GROUPS):
                        chain(ve.max(m8[:, t * GROUPS + g, :], rbias[:, t, g * 8:(g + 1) * 8]))
                chain(ve.tensor_tensor(gs.rearrange("p a b -> p (a b)"), m8[:, :, 0], m8[:, :, 1], ALU.add))
                g8, e8 = sl("g8", (NT, 8)), sl("e8", (NT, 8))
                for t in range(NT):
                    chain(ve.max(g8[:, t, :], gs[:, t, :]))
                pick(gs, g8[:, :, TOPG - 1:TOPG], TOPG, GROUPS, gm, rbuf)
                chain(ve.tensor_scalar(gs, gm, -1.0, -NEG, ALU.add, ALU.mult))
                per = E // GROUPS
                for t in range(NT):
                    r = rbias[:, t, :].rearrange("p (g j) -> p g j", j=per)
                    chain(ve.tensor_tensor(r, r, gs[:, t, :].unsqueeze(2).to_broadcast([P, GROUPS, per]), ALU.add))
                for t in range(NT):
                    chain(ve.max(e8[:, t, :], rbias[:, t, :]))
                pick(rbias[:, :, :], e8[:, :, TOPK - 1:TOPK], TOPK, E, wroute[:, :, :], rbuf)
                chain(ve.tensor_tensor(wroute[:, :, :], wroute[:, :, :], rscore[:, :, :], ALU.mult))
                ws = sl("wsum", (NT, 2))[:, :, 0:1]
                chain(ve.tensor_reduce(ws, wroute[:, :, :], AX.X, ALU.add))
                chain(ve.reciprocal(ws, ws))
                chain(ve.tensor_scalar(ws, ws, ROUTE_SCALE, None, ALU.mult))
                sig(ve.tensor_tensor(wroute[:, :, :], wroute[:, :, :], ws.to_broadcast([P, NT, E]), ALU.mult), "route_ready")

            def moe(layer):
                n = place["shared", layer][0]
                hi0, su0, route0 = 4 * X * layer, 2 * X * layer, []
                for x in range(1, X):
                    r = (n + x) % SLOTS
                    route0.append(16 * (1 + sum((n + y) % SLOTS == r for y in range(1, x))
                                        + (0 if layer == 0 else sum((place["shared", 0][0] + y) % SLOTS == r
                                                                    for y in range(1, X)))))

                def low(x, c, k, value=None):
                    r = (n + k) % SLOTS
                    ve.wait_ge(S("hi_ready"), x * 4 + (hi0 + (0, 2, 3, 5)[c]) if value is None else value)
                    w = ring[r][:, AT_PIECE[c]:AT_PIECE[c] + PIECE[c]]
                    sig(ve.tensor_tensor(piece[c][1][:, :], w, piece[c][0][:, :].bitcast(F32), ALU.subtract),
                        "lo_ready")

                def product(x, ft, k, step=None):
                    up, g = bank[4 + ft][:, T:2 * T], silu_g[:, ft, :]
                    ve.wait_ge(S("silu_ready"), x * 2 + (su0 + ft + 1))
                    chained(ve.tensor_tensor(g, g, up, ALU.mult), x, ft, 1)
                    if k:
                        r = (n + k) % SLOTS
                        value = route0[k - 1]
                        ve.wait_ge(S(f"route_full{r}"), value if step is None else step * 16 + value)
                        chained(ve.tensor_tensor(g, g, route_w[r][:, :], ALU.mult), x, ft, 2)
                    if k or layer:
                        ve.wait_ge(S("down_done"), x * 2 + (2 * X * layer - 1 + ft))
                    chained(ve.tensor_copy(a2[0][:, ft, :], g), x, ft, 3)
                    sig(ve.tensor_tensor(a2[1][:, ft, :], g, a2[0][:, ft, :].bitcast(F32), ALU.subtract), "a_ready")

                def chained(ins, x, ft, i):
                    ins.then_inc(S(f"product{i}"), 1)
                    done = 2 * X * layer + ft + 1
                    if i == 2:
                        done -= 2 * (layer + 1)
                    ve.wait_ge(S(f"product{i}"), x * 2 + done)

                def step(x, k, loop=None, has_next=True, has_after=True):
                    product(x, 1, k, loop)
                    if has_next:
                        low(x + 1, 1, k + 1)
                        low(x + 1, 2, k + 1)
                        product(x + 1, 0, k + 1, loop)
                        if has_after:
                            low(x + 2, 0, k + 2)
                        low(x + 1, 3, k + 1, None if has_after else hi0 + 4 * X)

                low(0, 0, 0, hi0 + 1)
                low(0, 1, 0)
                low(0, 2, 0)
                norm(2 * layer + 2)
                ve.wait_ge(S("h_high"), layer + 1)
                for b in range(2):
                    sig(ve.tensor_tensor(h2[1][:, 4 * b:4 * b + 4, :], hT[:, 4 * b:4 * b + 4, :],
                                         h2[0][:, 4 * b:4 * b + 4, :].bitcast(F32), ALU.subtract), "h_split")
                product(0, 0, 0)
                low(1, 0, 1)
                low(0, 3, 0)
                routing(layer)
                product(0, 1, 0)
                low(1, 1, 1)
                low(1, 2, 1)
                product(1, 0, 1)
                low(2, 0, 2)
                low(1, 3, 1)
                with ve.Fori(0, LOOPS) as i:
                    for k in range(1, BODY + 1):
                        step(i * BODY + k, k, i)
                for x in range(TAIL, X):
                    step(x, x, has_next=x + 1 < X, has_after=x + 2 < X)
                ve.wait_ge(S("down_done"), 2 * X * (layer + 1))
                for m in range(KT):
                    add_to_x(bank[m // 2][:, (m % 2) * T:(m % 2 + 1) * T], layer, 1, m)

            def square(out, in_, name):
                sig(ve.tensor_tensor(out, in_, in_, ALU.mult), name)

            def output_norm(layer, on, silu_first):
                for b in range(2):
                    square(osq[:, 2 * b:2 * b + 2, :], og[:, 2 * b:2 * b + 2, :], "og_sq")
                ve.wait_ge(S("og_rms"), 2 * (layer + 1))
                for b in range(2):
                    r = orms[:, 2 * b:2 * b + 2, :]
                    o = og[:, 2 * b:2 * b + 2, :]
                    chain(ve.reciprocal(r, r))
                    chain(ve.scalar_tensor_tensor(o, o, on, r, ALU.mult, ALU.mult))
                    sig(ve.tensor_tensor(yT[:, 4 + 2 * b:6 + 2 * b, :], o,
                                         feat[:, silu_first + 2 * b:silu_first + 2 * b + 2, :], ALU.mult), "y_ready")

            ve.wait_ge(S("params_landed"), 32)
            ve.wait_ge(S("x_landed"), 16)
            norm(1)
            z, lg = sl("z", (NT, EV_SMALL)), sl("lg", (NT, EV_SMALL))
            ve.wait_ge(S("tok_copied"), 6)
            sig(ve.tensor_tensor(z[:, :, 0:FH], sml[:, :, 0:FH],
                                 pr("fox_fb").unsqueeze(1).to_broadcast([P, NT, FH]), ALU.add), "z_ready")
            sig(ve.tensor_tensor(z[:, :, FH:FH + GH], sml[:, :, FH:FH + GH],
                                 pr("dt_bias").unsqueeze(1).to_broadcast([P, NT, GH]), ALU.add), "z_ready")
            sig(ve.tensor_copy(z[:, :, FH + GH:EV_SMALL], sml[:, :, FH + GH:EV_SMALL]), "z_ready")
            for b in range(4):
                ve.wait_ge(S("feat_copied"), 2 * b + 2)
                f = feat[:, 2 * b:2 * b + 2, :]
                square(yT[:, 2 * b:2 * b + 2, :], f, "fox_sq")
            for j in range(12):
                ve.wait_ge(S("feat_copied"), 8 + j + 1)
                for tap in range(4):
                    w = pr("conv")[:, 4 * j + 3 - tap:4 * j + 4 - tap]
                    src, dst = feat[:, 8 + j, 0:T - tap], conv[:, j, tap:T]
                    if tap == 0:
                        chain(ve.tensor_scalar(dst, src, w, None, ALU.mult))
                    elif tap < 3:
                        chain(ve.scalar_tensor_tensor(dst, src, w, dst, ALU.mult, ALU.add))
                    else:
                        sig(ve.scalar_tensor_tensor(dst, src, w, dst, ALU.mult, ALU.add), "conv_ready")
            ve.wait_ge(S("lg_ready"), 1)
            ve.wait_ge(S("ea_ready"), 1)
            chain(ve.tensor_scalar(logf, z[:, :, 0:FH], 0.0, None, ALU.min))
            sig(ve.tensor_tensor(logf, logf, lg[:, :, 0:FH], ALU.subtract), "logf_ready")
            chain(ve.tensor_scalar(gate, z[:, :, FH:FH + GH], 0.0, None, ALU.max))
            chain(ve.tensor_tensor(gate, gate, lg[:, :, FH:FH + GH], ALU.add))
            chain(ve.tensor_scalar(gate, gate, -1.0, None, ALU.mult))
            sig(ve.tensor_tensor(gate, gate, sl("ea", (GH,)).unsqueeze(1).to_broadcast([P, NT, GH]), ALU.mult),
                "gdn_g")
            ve.wait_ge(S("fox_rms"), 4)
            for b in range(4):
                chain(ve.reciprocal(frms[:, 2 * b:2 * b + 2, :], frms[:, 2 * b:2 * b + 2, :]))
            for odd in range(2):
                rows = slice(64 * odd, 64 * odd + 64)
                sig(ve.scalar_tensor_tensor(qpad[rows, odd::2, :], feat[rows, 0:4, :], pr("fox_qn")[rows, :],
                                            frms[rows, 0:4, :], ALU.mult, ALU.mult), "fox_qk")
            sig(ve.scalar_tensor_tensor(feat[:, 4:8, :], feat[:, 4:8, :], pr("fox_kn"), frms[:, 4:8, :],
                                        ALU.mult, ALU.mult), "fox_qk")
            mx, nmx, rs = sl("mx", (12,)), sl("nmx", (12,)), sl("rs", (12,))
            for u in range(4 * FH // 2 + 1):
                if u < 4 * FH // 2:
                    keys, c = P * (u // 2 % 2 + 1), u % 2
                    ve.wait_ge(S("fox_s"), u + 1)
                    chain(ve.reduce_max(mx[:, c:c + 1], bank[c][:, 0:keys], AX.X))
                    if u >= 2:
                        ve.wait_ge(S("fox_exp"), u - 1)
                    sig(ve.tensor_scalar(nmx[:, c:c + 1], mx[:, c:c + 1], -1.0, None, ALU.mult), "fox_nmax")
                if u >= 1:
                    keys, c = P * ((u - 1) // 2 % 2 + 1), (u - 1) % 2
                    ve.wait_ge(S("fox_exp"), u)
                    chain(ve.reciprocal(rs[:, 4 + c:5 + c], rs[:, c:c + 1]))
                    p = prob[c][:, 0:keys]
                    sig(ve.tensor_scalar(p, p, rs[:, 4 + c:5 + c], None, ALU.mult), "fox_p")
                if 2 <= u < 12 and u % 2 == 0:
                    mod_add(4 + (u - 2) // 2)

            for b in range(4):
                ve.wait_ge(S("gdn_silu"), b + 1)
                f = feat[:, 8 + 2 * b:10 + 2 * b, :]
                square(squares[:, 2 * b:2 * b + 2, :], f, "gdn_sq")
            for b in range(4):
                ve.wait_ge(S("gdn_rms"), b + 1)
                r, f = frms[:, 2 * b:2 * b + 2, :], feat[:, 8 + 2 * b:10 + 2 * b, :]
                chain(ve.reciprocal(r, r))
                sig(ve.tensor_tensor(f, f, r, ALU.mult), "gdn_qk")
                if b == 0:
                    mod_add(9)
            mod_add(10)
            gc, ngc, be, beta = sl("gc", (8,)), sl("ngc", (8,)), sl("be", (8,)), sl("beta", (8,))
            ve.wait_ge(S("gdn_cum"), 1)
            sig(ve.tensor_copy(gc, bank[6][:, 0:8]), "gdn_gc")
            sig(ve.tensor_scalar(ngc, bank[6][:, 0:8], -1.0, None, ALU.mult), "gdn_gc")
            ve.wait_ge(S("gdn_eg"), 1)
            ve.wait_ge(S("beta_ready"), 1)
            chain(ve.tensor_tensor(be, beta, sl("eg", (8,)), ALU.mult))
            ve.wait_ge(S("gdn_kk"), 1)
            ve.wait_ge(S("gdn_decay"), 18)
            for t in range(NT):
                for h in range(GH):
                    i = t * GH + h
                    sig(ve.scalar_tensor_tensor(Am[:, t, h, :], bank[6 + t][:, h * P:(h + 1) * P], beta[:, i:i + 1],
                                                Dm[:, t, h, :], ALU.mult, ALU.mult), "gdn_a")
            kdc = sl("kdc", (2, 8))
            for half in range(2):
                chain(ve.tensor_copy(kdc[:, half, :], DT.rearrange("p a b c -> p (a b) c")
                                     [:, :, half * CHUNK + CHUNK - 1]))
            ve.wait_ge(S("gdn_turned"), 1)
            ve.wait_ge(S("fox_pv"), 4 * FH // 2)

            def by4(b):
                return bank[b][:, :].rearrange("p (h d) -> p h d", h=GH)

            def col4(v, t):
                return v[:, t * GH:(t + 1) * GH].unsqueeze(2).to_broadcast([P, GH, P])

            for t in range(NT):
                sig(ve.tensor_tensor(attnT[:, t, :, :], by4(t), DT[:, t, :, :], ALU.mult), "gdn_attn")
                sig(ve.tensor_tensor(vb[:, t, :, :], by4(4 + t), col4(beta, t), ALU.mult), "gdn_kv")
                sig(ve.tensor_tensor(kbe[:, t, :, :], by4(2 + t), col4(be, t), ALU.mult), "gdn_kv")
                for half in range(2):
                    sig(ve.tensor_tensor(kd[half][:, t, :, :], by4(2 + t), col4(kdc[:, half, :], t), ALU.mult),
                        "gdn_kv")
                q = feat[:, 8:12, t * P:(t + 1) * P]
                sig(ve.tensor_tensor(q, q, Eb[:, t, :, :], ALU.mult), "gdn_qd")
            ve.wait_ge(S("gdn_qk"), 4)

            def by8(a):
                return a.rearrange("p a b c -> p (a b) c")

            def over8(m):
                return m.unsqueeze(1).to_broadcast([P, 2 * GH, P])

            ve.wait_ge(S("gdn_a"), 8)
            chain(ve.tensor_tensor(by8(Xi), by8(Am), over8(cs("lev1")), ALU.mult))
            sig(ve.tensor_tensor(by8(Xi), over8(ident), by8(Xi), ALU.subtract), "inv_x")
            ve.wait_ge(S("gdn_atc"), 2)
            chain(ve.tensor_tensor(by8(XT), by8(AT), over8(cs("levt", 0, P)), ALU.mult))
            sig(ve.tensor_tensor(by8(XT), over8(ident), by8(XT), ALU.subtract), "inv_x")
            for lv in range(1, len(LEVELS)):
                ve.wait_ge(S("inv_xp"), lv)
                for t in range(NT):
                    if lv < len(LEVELS) - 1:
                        sig(ve.tensor_tensor(Xi[:, t, :, :], Xi[:, t, :, :], by4(2 + t), ALU.subtract), "inv_x")
                    sig(ve.tensor_tensor(XT[:, t, :, :], XT[:, t, :, :], by4(4 + t), ALU.subtract), "inv_x")
                if lv <= 4:
                    mod_add(10 + lv)
                ve.wait_ge(S("inv_x"), 2 + 4 * lv if lv < len(LEVELS) - 1 else INVX)
            ve.wait_ge(S("gdn_uw"), 1)
            for t in range(NT):
                sig(ve.tensor_copy(u_sb[:, t, :, :], by4(6 + t)), "gdn_uwc")
            ve.wait_ge(S("gdn_uwc"), 4)
            for n in range(NCH):
                t, half = n // 2, n % 2
                if n == 0:
                    sig(ve.tensor_copy(vnew, u_sb[:, 0, :, :]), "gdn_vn")
                else:
                    ve.wait_ge(S("gdn_ws"), n)
                    ve.wait_ge(S("gdn_o"), n)
                    sig(ve.tensor_tensor(vnew, u_sb[:, t, :, :], by4(2), ALU.subtract), "gdn_vn")
                if n < NCH - 1:
                    ve.wait_ge(S("gdn_su"), n + 1)
                    ve.wait_ge(S("gdn_o"), n + 1)
                    if n == 0:
                        sig(ve.tensor_copy(state, by4(4)), "gdn_state")
                    else:
                        for h in range(GH):
                            c = half * CHUNK + CHUNK - 1
                            sig(ve.scalar_tensor_tensor(state[:, h, :], state[:, h, :], Eb[:, t, h, c:c + 1],
                                                        bank[4][:, h * P:(h + 1) * P], ALU.mult, ALU.add),
                                "gdn_state")
                    ve.wait_ge(S("gdn_state"), 1 + GH * n)
            ve.wait_ge(S("gdn_oc"), NCH)
            ve.wait_ge(S("gdn_silu"), 8)
            output_norm(0, pr("gdn_on"), 20)
            mod_add(15)
            mixer_residual(0)
            moe(0)

            norm(3)
            ve.wait_ge(S("feat_copied"), EV_TILES + 6)
            for b in range(3):
                f = feat[:, 2 * b:2 * b + 2, :]
                square(yT[:, 2 * b:2 * b + 2, :], f, "nsa_sq")
            ve.wait_ge(S("feat_copied"), EV_TILES + OD_TILES)
            for kv in range(2):
                for g in range(NKV):
                    for s in range(2):
                        rows = slice(64 * s, 64 * s + 64)
                        src = feat[rows, 14 + 2 * kv + g, 16 * s:16 * s + 16 * NCMP].rearrange(
                            "p (n l) -> p l n", l=16)
                        pos = pr("pos")[rows, 16 * kv:16 * kv + 16].unsqueeze(2).to_broadcast([64, 16, NCMP])
                        sig(ve.tensor_tensor(blk[rows, kv, :, g * NCMP:(g + 1) * NCMP], src, pos, ALU.add),
                            "cmp_blk")
            ve.wait_ge(S("gla_z"), 1)
            sig(ve.tensor_tensor(lz, bank[0][:, :].rearrange("p (a b) -> p a b", a=NT),
                                 pr("bg").unsqueeze(1).to_broadcast([P, NT, 256]), ALU.add), "gla_zc")
            ve.wait_ge(S("gla_lg"), 1)
            chain(ve.tensor_scalar(lz, lz, 0.0, None, ALU.min))
            chain(ve.tensor_tensor(loga, lz, loga, ALU.subtract))
            sig(ve.tensor_scalar(loga, loga, 1.0 / TAU, None, ALU.mult), "gla_loga")
            ve.wait_ge(S("cmp_kv"), 1)
            square(csq, kcn, "cmp_sq")
            ve.wait_ge(S("nsa_rms"), 4)
            chain(ve.reciprocal(nrms, nrms))
            crms = sl("crms", (16,))[:, 0:NCMP]
            chain(ve.reciprocal(crms, crms))
            for odd in range(2):
                rows = slice(64 * odd, 64 * odd + 64)
                sig(ve.scalar_tensor_tensor(qpad[rows, 4 * odd:4 * odd + 4, :], feat[rows, 0:4, :],
                                            pr("nsa_qn")[rows, :], nrms[rows, 0:4, :], ALU.mult, ALU.mult), "nsa_qk")
            sig(ve.scalar_tensor_tensor(feat[:, 4:6, :], feat[:, 4:6, :], pr("nsa_kn"), nrms[:, 4:6, :],
                                        ALU.mult, ALU.mult), "nsa_qk")
            sig(ve.scalar_tensor_tensor(kcn, kcn, pr("nsa_kn"), crms, ALU.mult, ALU.mult), "nsa_qk")
            ve.wait_ge(S("nsa_qk"), 4)
            ve.wait_ge(S("brel_landed"), 32)
            units = [(h0 + i, qt) for h0 in range(4) for qt in range(NT) for i in (0, 4)]
            ngate = sl("ngate", (NT, OD_GATES))
            for u in range(len(units) + 1):
                if u < len(units):
                    h, qt = units[u]
                    keys, c = P * (qt + 1), 3 * (u % 2)
                    p = nprob[u % 2][:, 0:512].rearrange("p (b k) -> p b k", b=2)[:, :, 0:keys]
                    pc = nprob[u % 2][:, 512:512 + NCMP]
                    ve.wait_ge(S("nsa_s"), u + 1)
                    if u >= 2:
                        ve.wait_ge(S("nsa_turned"), u - 1)
                    sig(ve.tensor_tensor(p, bank[u % 2][:, :].rearrange("p (b k) -> p b k", b=2)[:, :, 0:keys],
                                         Brel[:, qt, h, 0:keys].unsqueeze(1).to_broadcast([P, 2, keys]), ALU.add),
                        "nsa_b")
                    sig(ve.tensor_tensor(pc, bank[6][:, 0:NCMP], relc[:, qt, :, h],
                                         ALU.add), "nsa_b")
                    ve.wait_ge(S("nsa_b"), 2 * (u + 1))
                    chain(ve.reduce_max(mx[:, c:c + 1], pc, AX.X))
                    chain(ve.reduce_max(mx[:, c + 1:c + 3], p, AX.X))
                    sig(ve.tensor_scalar(nmx[:, c:c + 3], mx[:, c:c + 3], -1.0, None, ALU.mult), "nsa_nmax")
                if u >= 1:
                    h, qt = units[u - 1]
                    keys, c = P * (qt + 1), 3 * ((u - 1) % 2)
                    rg = sl("rg", (12,))[:, c:c + 3]
                    ve.wait_ge(S("nsa_exp"), 3 * u)
                    chain(ve.reciprocal(rg, rs[:, c:c + 3]))
                    chain(ve.tensor_tensor(rg, rg, ngate[:, qt, 3 * h:3 * h + 3], ALU.mult))
                    pc = nprob[(u - 1) % 2][:, 512:512 + NCMP]
                    sig(ve.scalar_tensor_tensor(pc, pc, rg[:, 0:1], cs("cmask")[:, qt * NCMP:(qt + 1) * NCMP],
                                                ALU.mult, ALU.mult), "nsa_p")
                    for br in range(2):
                        p = nprob[(u - 1) % 2][:, br * T:br * T + keys]
                        sig(ve.tensor_scalar(p, p, rg[:, br + 1:br + 2], None, ALU.mult), "nsa_p")

            ve.wait_ge(S("gla_G"), 1)
            sig(ve.tensor_copy(G.rearrange("p a b -> p (a b)"), bank[0][:, :]), "gla_Gc")
            ve.wait_ge(S("gla_Gc"), 1)
            for f in range(2):
                g = G[:, f, :].rearrange("p (n c) -> p n c", c=CHUNK)
                last = ve.tensor_tensor(edG[:, f, :].rearrange("p (n c) -> p n c", c=CHUNK),
                                        g[:, :, CHUNK - 1:CHUNK].to_broadcast([P, NCH, CHUNK]), g, ALU.subtract)
                if f == 0:
                    chain(last)
            sig(last, "gla_dG")
            ve.wait_ge(S("gla_exp"), 3)
            ve.wait_ge(S("pads_zero"), 6)
            for odd in range(2):
                rows = slice(64 * odd, 64 * odd + 64)
                sig(ve.scalar_tensor_tensor(lqd[rows, odd::2, :], feat[rows, 6:8, :], LDK ** -0.5, EG[rows, :, :],
                                            ALU.mult, ALU.mult), "gla_qk")
            sig(ve.tensor_tensor(lki, feat[:, 8:10, :], EnG, ALU.mult), "gla_qk")
            sig(ve.tensor_tensor(lkd, feat[:, 8:10, :], edG, ALU.mult), "gla_qk")
            ve.wait_ge(S("gla_at"), 1)
            for t in range(NT):
                sig(ve.tensor_tensor(lattn[:, t, :, :], by4(1 + t), cs("tril").unsqueeze(1).to_broadcast([P, LH, P]),
                                     ALU.mult), "gla_ready")
            for half in range(2):
                sig(ve.tensor_scalar(lkt[:, half, :, :, :].rearrange("p a b c -> p (a b c)"), bank[3][:, :],
                                     cs("half")[:, half:half + 1], None, ALU.mult), "gla_ready")
            for n in range(NCH - 1):
                ve.wait_ge(S("gla_su"), n + 1)
                ve.wait_ge(S("gla_o"), n + 1)
                if n == 0:
                    sig(ve.tensor_copy(lstate, by4(5)), "gla_state")
                else:
                    for h in range(LH):
                        c = n * CHUNK + CHUNK - 1
                        sig(ve.scalar_tensor_tensor(lstate[:, h, :], lstate[:, h, :], EG[:, h // 2, c:c + 1],
                                                    bank[5][:, h * P:(h + 1) * P], ALU.mult, ALU.add), "gla_state")
                ve.wait_ge(S("gla_state"), 1 + LH * n)
            ve.wait_ge(S("gla_oc"), NCH)
            ve.wait_ge(S("gla_silu"), 2)
            output_norm(1, pr("gla_on"), 10)
            mixer_residual(1)
            moe(1)

        @block.gpsimd
        def _(gp):
            gp.memset(qpad, 0.0).then_inc(S("pads_zero"), 1)
            gp.memset(vpad, 0.0).then_inc(S("pads_zero"), 1)
            gp.wait_ge(S("gdn_atc"), 2)
            gp.wait_ge(S("params_landed"), 32)
            gp.wait_ge(S("gdn_ss"), 1)
            for lv in range(1, len(LEVELS)):
                if lv > 2:
                    gp.wait_ge(S("inv_p"), lv - 2)
                gp.tensor_tensor(ATm[lv % 2].rearrange("p a b c -> p (a b) c"), AT.rearrange("p a b c -> p (a b) c"),
                                 cs("levt", lv * P, (lv + 1) * P).unsqueeze(1).to_broadcast([P, 2 * GH, P]),
                                 ALU.mult).then_inc(S("inv_atm"), 1)
            gp.wait_ge(S("x_added"), 2 * KT)
            gp.memset(qpad, 0.0).then_inc(S("pads_zero"), 1)
            gp.memset(nvpad, 0.0).then_inc(S("pads_zero"), 1)
            gp.memset(vcpad, 0.0).then_inc(S("pads_zero"), 1)
            gp.wait_ge(S("nsa_nmax"), 2 * NH)
            gp.memset(lqd, 0.0).then_inc(S("pads_zero"), 1)


def tiles(a, width=P):
    r, c = a.shape
    return a.reshape(r // width, width, c).transpose(1, 0, 2).reshape(width, -1)


def lay_out(i):
    def rep(v):
        return np.broadcast_to(np.asarray(v).reshape(1, -1), (P, np.asarray(v).size))

    def cols(v):
        return np.asarray(v).reshape(-1, P).T

    def twice(v):
        return np.concatenate([v, v])[:, None]

    par = np.zeros((P, PARW), np.float32)

    def put(name, a):
        par[: a.shape[0], PAR[name][0]:PAR[name][0] + a.shape[1]] = a

    put("c", cols(i["c"][0]))
    put("ada_b", cols(i["ada_b"]))
    put("norm_mix", cols(i["norm_mix"]))
    put("norm_ffn", cols(i["norm_ffn"]))
    put("router", tiles(i["moe_router"].reshape(LAYERS * D, E)))
    put("e_bias", rep(i["moe_bias"]))
    put("fox_fb", rep(i["fox_fb"]))
    put("fox_qn", twice(i["fox_qn"][0]))
    put("fox_kn", twice(i["fox_kn"][0]))
    put("conv", i["gdn_conv"][0].T.reshape(12, P, 4).transpose(1, 0, 2).reshape(P, 48))
    put("a_log", rep(i["gdn_a_log"]))
    put("dt_bias", rep(i["gdn_dt_bias"]))
    put("gdn_on", i["gdn_on"][0][:, None])
    put("nsa_qn", twice(i["nsa_qn"][0]))
    put("nsa_kn", twice(i["nsa_kn"][0]))
    pos = i["nsa_pos"][0].reshape(2, 2, 16, NDH)
    put("pos", pos.transpose(1, 3, 0, 2).reshape(P, 32))
    put("wg_up", i["gla_wg_up"][0])
    put("bg", rep(i["gla_bg"]))
    put("gla_on", i["gla_on"][0][:, None])
    put("rel", np.concatenate([i["rel_bias"], np.ones((1, NH), np.float32)]))

    pair = np.concatenate([np.r_[64 * h:64 * h + 64, 64 * (h + 4):64 * (h + 4) + 64] for h in range(4)])
    ev, od = i["ev_w_in"][0], i["od_w_in"][0]
    ev_cut = np.cumsum([0, 512, 512, 512, 8, 1536, 4, 4, 512])
    fq, fk, fv, ff, gqkv, ga, gb, gz = (ev[:, a:b] for a, b in zip(ev_cut, ev_cut[1:]))
    od_cut = np.cumsum([0, 512] + [128] * 6 + [24, 256, 256, 512, 16, 512])
    nq, kc, vc, ks, vs, kw, vw, ng, lq, lk, lv, lg, lr = (od[:, a:b] for a, b in zip(od_cut, od_cut[1:]))
    double = [x[:, 64 * g:64 * g + 64] for x in (kc, vc) for g in range(2) for _ in range(2)]
    full = {"in0.0": np.concatenate([fv, ff, ga, gb], 1), "in1.0": np.concatenate([vs, vw, lv], 1),
            "in1.1": np.concatenate([ng, lg], 1)}
    feat0 = np.concatenate([fq, fk, gqkv, gz], 1)
    feat1 = np.concatenate([nq[:, pair], ks, kw, lq, lk, lr] + double, 1)
    out1 = i["od_w_out"][0]
    outs = [i["ev_w_out"][0], np.concatenate([out1[:512][pair], out1[512:]])]
    w1, w2 = i["nsa_cmp_w1"][0], i["nsa_cmp_w2"][0]
    mix = np.zeros((len(NAMES), P, SLOTW), np.float32)
    for n, name in enumerate(NAMES):
        s = int(name[-1])
        if name in full:
            a = tiles(full[name])
        elif name.startswith("ada"):
            a = tiles(i["ada_w"][int(name[3])][:, SC * s:SC * (s + 1)])
        elif name.startswith("in0"):
            a = tiles(feat0[:, SC * (s - 1):SC * s])
        elif name.startswith("in1"):
            a = tiles(feat1[:, SC * (s - 2):SC * (s - 1)])
        elif name.startswith("out"):
            a = tiles(outs[int(name[3])][:, 512 * s:512 * (s + 1)])
        else:
            first = w1[s].reshape(2, 16, NDH, CHID).transpose(0, 2, 1, 3).reshape(P, 16 * CHID)
            second = tiles(w2[s])
            if s == 0:
                second = second.reshape(P, 2, NDH)
                padded = np.zeros((P, 2, 2, P), np.float32)
                padded[:, :, 0, 0:NDH] = second
                padded[:, :, 1, NDH:P] = second
                second = padded.reshape(P, 512)
            a = np.concatenate([first, second], 1)
        mix[n, :, 0:a.shape[1]] = a

    moe = np.empty((LAYERS * X, P, SLOTW), np.float32)
    for l in range(LAYERS):
        at = l * X
        third = KT * FE
        up = moe[at:at + X, :, 0:2 * third].reshape(X, P, 2, 2, KT, P)
        for j, (sh, ex) in enumerate((("sh_wg", "moe_wg"), ("sh_wu", "moe_wu"))):
            up[0, :, :, j] = i[sh][l].reshape(KT, P, 2, P).transpose(1, 2, 0, 3)
            up[1:, :, :, j] = i[ex][l].reshape(E, KT, P, 2, P).transpose(0, 2, 3, 1, 4)
        moe[at:at + X, :, 0:2 * third] = up.reshape(X, P, 2 * third)
        moe[at, :, 2 * third:] = tiles(i["sh_wd"][l])
        moe[at + 1:at + 1 + E, :, 2 * third:] = i["moe_wd"][l].reshape(E, 2, P, D).transpose(
            0, 2, 1, 3).reshape(E, P, third)
    x = i["x"][0].T.reshape(KT, P, T).transpose(1, 0, 2)
    return {"xT_in": np.ascontiguousarray(x), "par_in": par, "cst_in": constants(), "mix_in": mix, "moe_in": moe}


def kernel(**inputs):
    import concourse.bacc as _bacc
    from concourse.bass_utils import run_bass_kernel_spmd as _run

    arrays = lay_out({k: np.asarray(v) for k, v in inputs.items()})
    nc = _bacc.Bacc("TRN2", target_bir_lowering=False, num_devices=1)
    args = [nc.dram_tensor(n, a.shape, F32, kind="ExternalInput").ap() for n, a in arrays.items()]
    args.append(nc.dram_tensor("outT", (P, KT, T), F32, kind="ExternalOutput").ap())
    program(nc, *args)
    r = _run(nc, [arrays], core_ids=[0])
    out = r.results[0]["outT"]
    return np.ascontiguousarray(out.transpose(1, 0, 2).reshape(D, T).T.reshape(1, T, D))
```

```python
import math
from contextlib import ExitStack

import numpy as np
import concourse.bass as bass
from concourse import mybir

F32 = mybir.dt.float32
F32R = mybir.dt.float32r
ALU = mybir.AluOpType
ACT = mybir.ActivationFunctionType
AX = mybir.AxisListType

P = 128
D = 1024
T = 256
NT = T // P
KT = D // P
LAYERS = 2
EPS = 1e-6
NEG = -1e30
CHUNK = 64
NCH = T // CHUNK
FH, FDH = 8, 64
GH, GD = 4, 128
NH, NDH, NKV = 8, 64, 2
CMP_LEN, CMP_STRIDE = 32, 16
NCMP = (T - CMP_LEN) // CMP_STRIDE + 1
ROW = 2 * T
CHID = 256
LH, LDK, LDV, LRANK = 4, 64, 128, 16
TAU = 16.0
BUCKETS, MAXDIST = 32, 128
E, TOPK, GROUPS, TOPG = 64, 6, 8, 4
FE = 256
ROUTE_SCALE = 2.5
SLOTW = 3 * KT * FE
SLOTS = 3
SC = SLOTW // KT
X = E + 1
BODY = SLOTS
LOOPS = (X - 5) // BODY
TAIL = LOOPS * BODY + 1
PIECE = (2048, 2048, 1024, 1024)
AT_PIECE = (0, 2048, 4096, 5120)
LEVELS = (1, 2, 4, 8, 16, 32)
INVX = 4 * (len(LEVELS) - 1)

EV_SMALL = FH + 2 * GH
OD_TOK = 2 * NKV * NDH + LH * LDV
OD_GATES = 3 * NH
EV_TILES = 24
OD_TILES = 18


def columns(parts):
    at, where = 0, {}
    for name, width in parts:
        where[name] = (at, at + width)
        at += width
    return where, at


PAR, PARW = columns([
    ("c", KT), ("ada_b", LAYERS * 48), ("norm_mix", LAYERS * KT), ("norm_ffn", LAYERS * KT),
    ("router", LAYERS * KT * E), ("e_bias", LAYERS * E), ("fox_fb", FH), ("fox_qn", 1), ("fox_kn", 1),
    ("conv", 48), ("a_log", GH), ("dt_bias", GH), ("gdn_on", 1), ("nsa_qn", 1), ("nsa_kn", 1),
    ("pos", 2 * 16), ("wg_up", 256), ("bg", 256), ("gla_on", 1), ("rel", NH)])
CST, CSTW = columns([
    ("ident", P), ("ones", P), ("eps", 8), ("bd", P), ("tri", P), ("ntri", 2 * P), ("maskq", P),
    ("mpos", P), ("mneg", P), ("tril", P), ("levt", 6 * P), ("lev1", P), ("ohr", 512), ("cmask", NT * NCMP), ("half", 2)])
EPS1, EPS64, EPS128, ONE, ZERO = range(5)


SML, SMALLW = columns([
    ("sml", 2 * 16), ("logf", 16), ("gate", 8), ("z", 32), ("lg", 32), ("beta", 8), ("be", 8), ("gc", 8),
    ("ngc", 8), ("eg", 8), ("ea", 4), ("kdc", 16), ("mx", 12), ("nmx", 12), ("rs", 12), ("rg", 12),
    ("ngate", 48), ("chid", 120), ("kcn", 16), ("csq", 16), ("crms", 16),
    ("m8", 128), ("gs", 16), ("g8", 16), ("e8", 16), ("gm", 16), ("left", 4), ("wsum", 4)])


def constants():
    c = np.zeros((P, CSTW), np.float32)

    def put(name, a):
        c[: a.shape[0], CST[name][0]:CST[name][0] + a.shape[1]] = a

    i, j = np.arange(P)[:, None], np.arange(P)[None, :]
    same = i // CHUNK == j // CHUNK
    put("ident", np.eye(P))
    put("ones", np.ones((P, P)))
    put("bd", (i // 64 == j // 64) * 1.0)
    put("tri", (same & (i <= j)) * 1.0)
    put("ntri", np.concatenate([(i <= j) * -1.0, -np.ones((P, P))], 1))
    put("maskq", np.where(j > i, NEG, 0.0))
    put("mpos", np.where(same & (j <= i), 0.0, -NEG))
    put("mneg", np.where(same & (j >= i), 0.0, NEG))
    put("tril", (same & (j >= i)) * 1.0)

    def level(m):
        return ((i // (2 * m) == j // (2 * m)) & (i // m % 2 == 1) & (j // m % 2 == 0)) * 1.0

    put("levt", np.concatenate([level(m).T for m in LEVELS], 1))
    put("lev1", level(1))
    dist = 255 - np.arange(512)
    exact = BUCKETS // 2
    n = np.maximum(dist, 0)
    large = exact + (np.log(np.maximum(n, 1).astype(np.float32) / np.float32(exact))
                     / np.float32(math.log(MAXDIST / exact)) * np.float32(BUCKETS - exact)).astype(np.int32)
    bucket = np.where(n < exact, n, np.minimum(large, BUCKETS - 1))
    oh = np.zeros((BUCKETS + 1, 512), np.float32)
    oh[bucket, np.arange(512)] = 1.0
    oh[BUCKETS] = np.where(dist < 0, NEG, 0.0)
    put("ohr", oh)
    q = np.arange(T).reshape(NT, P).T
    end = np.arange(NCMP) * CMP_STRIDE + CMP_LEN - 1
    put("cmask", (end[None, None, :] <= q[:, :, None]).reshape(P, -1) * 1.0)
    put("eps", np.tile(np.array([[EPS, 64 * EPS, 128 * EPS, 1.0, 0.0, 0, 0, 0]]), (P, 1)))
    put("half", np.stack([(np.arange(P) < 64), (np.arange(P) >= 64)], 1) * 1.0)
    return c


def mixer_loads():
    names = [f"ada0.{s}" for s in range(3)] + [f"in0.{s}" for s in range(5)]
    names += [f"ada0.{s}" for s in range(3, 8)] + [f"ada1.{s}" for s in range(8)] + ["out0.0", "out0.1"]
    names += [f"in1.{s}" for s in range(5)] + ["cmp.0", "cmp.1", "out1.0", "out1.1"]
    return names


NAMES = mixer_loads()


def width_of(name):
    if name == "in0.0":
        return KT * (FH * FDH + EV_SMALL)
    if name == "in1.1":
        return KT * (OD_GATES + LRANK)
    if name.startswith("cmp"):
        return 16 * CHID + (512 if name == "cmp.0" else 128)
    if name.startswith("out"):
        return KT * 512
    return SLOTW


def program(nc, xT_in, par_in, cst_in, mix_in, moe_in, outT):
    with ExitStack() as ctx:
        def sb(name, shape):
            return ctx.enter_context(nc.sbuf_tensor(name, shape, F32))

        sems = {}

        def S(name):
            if name not in sems:
                sems[name] = ctx.enter_context(nc.semaphore(name))
            return sems[name]

        bank = [ctx.enter_context(nc.psum_tensor(f"bank{i}", [P, 512], F32)) for i in range(8)]
        ring = [sb(f"ring{i}", [P, SLOTW]) for i in range(SLOTS)]
        route_w = [sb(f"route_w{i}", [P, T]) for i in range(SLOTS)]
        par = sb("par_sb", [P, PARW])
        cst = sb("cst_sb", [P, CSTW])
        xT = sb("xT", [P, KT, T])
        hT = sb("hT", [P, KT, T])
        yT = sb("yT", [P, KT, T])
        mod = sb("mod", [P, LAYERS * 48])
        cond = sb("cond", [P, KT])
        gain = sb("gain", [P, KT])
        rms = sb("rms", [P, T])
        relrow = sb("relrow", [NH, 512])
        small = sb("small", [P, SMALLW])
        partial = [sb(f"partial{i}", [P, SC]) for i in range(2)]
        mixer_memory = ExitStack()

        def mb(name, shape):
            return mixer_memory.enter_context(nc.sbuf_tensor(name, shape, F32))

        feat = mb("feat", [P, EV_TILES, T])
        scr = mb("scr", [P, 48, T])

        def flat(tensor, first, blocks):
            return tensor[:, first:first + blocks, :].rearrange("p a b -> p (a b)")

        def blocks(first, shape):
            n = int(np.prod(shape))
            letters = "abcd"[:len(shape)]
            dims = " ".join(letters)
            return flat(scr, first, -(-n // T))[:, 0:n].rearrange(
                f"p ({dims}) -> p {dims}", **dict(zip(letters, shape)))

        def sl(name, shape):
            lo, hi = SML[name]
            letters = "abcd"[:len(shape)]
            dims = " ".join(letters)
            return small[:, lo:hi].rearrange(f"p ({dims}) -> p {dims}", **dict(zip(letters, shape)))

        sml = sl("sml", (NT, EV_SMALL))
        logf = sl("logf", (NT, FH))
        gate = sl("gate", (NT, GH))
        qpad = blocks(0, (FH, T))
        vpad = blocks(8, (NT, FH, P))
        prob = [blocks(16 + i, (T,)) for i in range(2)]
        probT = [blocks(18 + i, (T,)) for i in range(2)]
        conv = blocks(20, (12, T))
        frms = blocks(32, (8, T))
        squares = blocks(40, (8, T))
        vb, kbe = blocks(0, (NT, GH, P)), blocks(4, (NT, GH, P))
        kd = [blocks(8, (NT, GH, P)), blocks(12, (NT, GH, P))]
        state, vnew = blocks(16, (GH, P)), blocks(18, (GH, P))
        Eb, Dm, DT = (blocks(b, (NT, GH, P)) for b in (20, 24, 28))
        Am, attnT = Dm, DT
        Xi, XT = blocks(32, (NT, GH, P)), blocks(36, (NT, GH, P))
        ATm = [blocks(40, (NT, GH, P)), blocks(44, (NT, GH, P))]
        og, osq = blocks(32, (GH, T)), blocks(36, (GH, T))
        orms = blocks(40, (GH, T))

        def feat4(first):
            return flat(feat, first, 4).rearrange("p (a b c) -> p a b c", a=NT, b=GH)

        Pm, AT, u_sb, wT = feat4(0), feat4(4), feat4(12), feat4(16)
        nvpad = blocks(8, (NT, 2, NKV, P))
        vcpad = blocks(12, (NKV, P))
        lgT = blocks(13, (T,))
        Brel = blocks(16, (NT, NH, T))
        nrms = blocks(32, (6, T))
        npr = blocks(32, (2, 640))
        npT = blocks(37, (2, 640))
        nprob = [npr[:, i, :] for i in range(2)]
        nprobT = [npT[:, i, :] for i in range(2)]
        blk = blocks(42, (2, 16, NKV * NCMP))
        chidT = blocks(38, (2, CHID))
        chid = sl("chid", (2, 2, NKV * NCMP))
        kcn = sl("kcn", (16,))[:, 0:NCMP]
        csq = sl("csq", (16,))[:, 0:NCMP]
        toks = flat(feat, 18, 4).rearrange("p (a b) -> p a b", a=NT)
        lz, loga = blocks(46, (NT, T)), blocks(14, (NT, T))
        G, EG, EnG, edG = (blocks(b, (2, T)) for b in (0, 2, 4, 6))
        lki, lkd = blocks(8, (2, T)), blocks(10, (2, T))
        lqd, lkt = blocks(16, (LH, T)), blocks(20, (2, NT, 2, P))
        lattn, lstate = blocks(24, (NT, LH, P)), blocks(28, (LH, P))
        mixer_memory.close()

        def split(name, shape):
            return tuple(ctx.enter_context(nc.sbuf_tensor(name + part, shape, F32R)) for part in ("_hi", "_lo"))

        piece = [split(f"piece{c}", [P, PIECE[c]]) for c in range(4)]
        h2 = split("h2", [P, KT, T])
        a2 = split("a2", [P, 2, T])
        silu_g = sb("silu_g", [P, 2, T])
        rscore, rbias, wroute = (sb(n, [P, NT, E]) for n in ("rscore", "rbias", "wroute"))
        rbuf = [sb(f"rbuf{i}", [P, NT, E]) for i in range(4)]
        wTs = sb("wTs", [E, T])

        w_dram = [nc.dram_tensor(f"route{l}", [E, T], F32) for l in range(LAYERS)]
        rel_dram = nc.dram_tensor("rel_rows", [NH, P * (ROW + 1)], F32)

        def pr(name, a=0, b=None):
            lo, hi = PAR[name]
            return par[:, lo + a:(hi if b is None else lo + b)]

        def cs(name, a=0, b=None):
            lo, hi = CST[name]
            return cst[:, lo + a:(hi if b is None else lo + b)]

        def eps(k):
            return cs("eps", k, k + 1)

        ident, ones = cs("ident"), cs("ones")

        order = [("mix", n) for n in NAMES[:NAMES.index("in1.0")]] + [("shared", 0), ("experts", 0)]
        order += [("mix", n) for n in NAMES[NAMES.index("in1.0"):]] + [("shared", 1), ("experts", 1)]
        place, n_load, landed = {}, 0, [0] * SLOTS
        for key in order:
            slot = n_load % SLOTS
            if key[0] == "experts":
                first = [landed[(n_load + e) % SLOTS] + 16 * (e // SLOTS + 1) for e in range(E)]
                place[key] = (n_load, first)
                for e in range(E):
                    landed[(n_load + e) % SLOTS] += 16
                n_load += E
            else:
                landed[slot] += 16
                place[key] = (n_load, landed[slot])
                n_load += 1

        def piece_split(layer, x, c):
            value = 4 * x + 1 if x == 0 and c == 0 else 4 * x + (0, 2, 3, 5)[c]
            return 4 * X * layer + (4 * X if (x, c) == (X - 1, 3) else value)

        ADAS = [(0, s) for s in range(8)] + [(1, s) for s in range(8)]
        FIRST_ADAS = 3

        def slot_of(key):
            return ring[place[key][0] % SLOTS]

        def ada_slot(engine, i):
            n, value = place["mix", "ada%d.%d" % ADAS[i]]
            engine.wait_ge(S(f"slot_full{n % SLOTS}"), value)
            return ring[n % SLOTS][:, :].rearrange("p (k n) -> p k n", k=KT)

        block = ctx.enter_context(nc.Block())

        @block.sync
        def _(sp):
            par_head, cst_head = PAR["router"][0], CST["bd"][0]
            sp.dma_start(par[:, 0:par_head], par_in[:, 0:par_head]).then_inc(S("heads_landed"), 16)
            sp.dma_start(cst[:, 0:cst_head], cst_in[:, 0:cst_head]).then_inc(S("heads_landed"), 16)

            adas = [n for n in NAMES if n.startswith("ada")]

            def released(key, e=0):
                if key[0] == "experts":
                    return "lo_ready", piece_split(key[1], e + 1, 3)
                if key[0] == "shared":
                    return "lo_ready", piece_split(key[1], 0, 3)
                name = key[1]
                layer, s = int(name[-3]) if name[0] != "c" else 1, int(name[-1])
                if name.startswith("ada"):
                    return "mod_partial", adas.index(name) + 1
                if name.startswith("in0"):
                    return ("tok_ready", 1) if s == 0 else ("feat_ready", 6 * s)
                if name.startswith("in1"):
                    return [("tok_half", 1), ("tok_ready", 2)][s] if s < 2 else ("feat_ready", EV_TILES + 6 * (s - 1))
                if name.startswith("out"):
                    return "proj_ready", KT * layer + 4 * (s + 1)
                return "cmp_o", s + 1

            loads = []
            for key in order:
                loads += [(key, e) for e in range(E)] if key[0] == "experts" else [(key, 0)]

            def await_slot(n):
                if n >= SLOTS:
                    name, value = released(*loads[n - SLOTS])
                    sp.wait_ge(S(name), value)

            def stream(key):
                n = place[key][0]
                await_slot(n)
                if key[0] == "mix":
                    w = width_of(key[1])
                    src = mix_in[NAMES.index(key[1]), :, 0:w]
                else:
                    w, src = SLOTW, moe_in[key[1] * X, :, :]
                sp.dma_start(ring[n % SLOTS][:, 0:w], src).then_inc(S(f"slot_full{n % SLOTS}"), 16)

            def stream_experts(layer):
                n = place["shared", layer][0]

                def load_expert(x, r):
                    sp.dma_start(ring[r][:, :], moe_in[bass.ds(x + layer * X, 1), :, :]
                                 .rearrange("a p n -> (a p) n")).then_inc(S(f"slot_full{r}"), 16)

                def load_route(x, r):
                    sp.dma_start(route_w[r][:, :], w_dram[layer].ap()[bass.ds(x - 1, 1), :].to_broadcast([P, T])
                                 ).then_inc(S(f"route_full{r}"), 16)

                def both(x, k):
                    sp.wait_ge(S("lo_ready"), (x - SLOTS) * 4 + (4 * X * layer + 5))
                    load_expert(x, (n + k) % SLOTS)
                    sp.wait_ge(S("a_ready"), (x - SLOTS) * 2 + (2 * X * layer + 2))
                    load_route(x, (n + k) % SLOTS)

                for x in range(1, SLOTS):
                    await_slot(n + x)
                    load_expert(x, (n + x) % SLOTS)
                sp.wait_ge(S("route_stored"), 16 * (layer + 1))
                if layer:
                    sp.wait_ge(S("a_ready"), 2 * X * layer)
                for x in range(1, SLOTS):
                    load_route(x, (n + x) % SLOTS)
                both(SLOTS, SLOTS)
                with sp.Fori(0, (X - SLOTS - 2) // BODY) as step:
                    for k in range(SLOTS + 1, SLOTS + 1 + BODY):
                        both(step * BODY + k, k)
                for x in range(SLOTS + 1 + (X - SLOTS - 2) // BODY * BODY, X):
                    both(x, x)

            for key in order:
                if key == ("mix", "ada0.1"):
                    sp.dma_start(xT[:, :, :], xT_in).then_inc(S("x_landed"), 16)
                if key == ("mix", "in0.0"):
                    sp.dma_start(cst[:, cst_head:], cst_in[:, cst_head:]).then_inc(S("params_landed"), 16)
                    sp.dma_start(par[:, par_head:], par_in[:, par_head:]).then_inc(S("params_landed"), 16)
                if key == ("mix", "out0.0"):
                    sp.wait_ge(S("rel_copied"), 1)
                    dst = bass.AP(rel_dram, 0, [[P * (ROW + 1), NH], [ROW + 1, P], [1, ROW]])
                    sp.dma_start(dst, relrow[:, :].unsqueeze(1).to_broadcast([NH, P, ROW])
                                 ).then_inc(S("rel_stored"), 16)
                if key == ("mix", "in1.3"):
                    sp.wait_ge(S("rel_stored"), 16)
                    sp.wait_ge(S("x_added"), 2 * KT)
                    for t in range(NT):
                        src = bass.AP(rel_dram, 255 - P * t, [[ROW, P], [P * (ROW + 1), NH], [1, T]])
                        sp.dma_start(Brel[:, t, :, :], src).then_inc(S("brel_landed"), 16)
                if key[0] == "experts":
                    stream_experts(key[1])
                else:
                    stream(key)
            for m in range(KT):
                sp.wait_ge(S("x_added"), 3 * KT + m + 1)
                sp.dma_start(outT[:, m, :], xT[:, m, :]).then_inc(S("out_stored"), 16)
            sp.wait_ge(S("out_stored"), 16 * KT)

        @block.tensor
        def _(pe):
            def mm(out, lhsT, rhs, start, stop):
                return pe.matmul(out, lhsT, rhs, start=start, stop=stop)

            def tr(out, in_):
                return pe.transpose(out, in_, ident)

            def full(key):
                n, value = place[key]
                pe.wait_ge(S(f"slot_full{n % SLOTS}"), value)
                return slot_of(key)

            def mod_columns(i):
                pe.wait_ge(S("mod_partial"), i + 1)
                if i:
                    pe.wait_ge(S("mod_copied"), i)
                for m in range(6):
                    last = mm(bank[7][:, m:m + 1], partial[i % 2][:, m * P:(m + 1) * P], ones[:, 0:1], True, True)
                last.then_inc(S("mod_turned"), 1)

            def feature_sum(n, tiles=range(KT)):
                for k in tiles:
                    pe.wait_ge(S("sq_ready"), KT * (n - 1) + k + 1)
                    last = mm(bank[4][:, 0:T], ones, hT[:, k, :], k == 0, k == KT - 1)
                    if k == KT - 1:
                        last.then_inc(S("ss_ready"), 1)

            def project_tokens(w, c0, c1, dst, norms=None):
                for t in range(NT):
                    for k in range(KT):
                        if norms and t == 0:
                            pe.wait_ge(S("h_ready"), KT * (norms - 1) + k + 1)
                        last = mm(dst[t], hT[:, k, t * P:(t + 1) * P], w[:, k, c0:c1], k == 0, k == KT - 1)
                return last

            def project_features(w, tiles, j0, first_tile):
                for m in range(tiles):
                    j = j0 + m
                    if j >= 3:
                        pe.wait_ge(S("feat_copied"), first_tile + j - 2)
                    for k in range(KT):
                        last = mm(bank[4 + j % 3][:, 0:T], w[:, k, m * P:(m + 1) * P], hT[:, k, :],
                                  k == 0, k == KT - 1)
                    last.then_inc(S("feat_ready"), 1)

            def out_projection(layer, part):
                def product(w, j, tiles):
                    for k in tiles:
                        last = mm(bank[j % 4][:, 0:T], w[:, k, j % 4 * P:(j % 4 + 1) * P], yT[:, k, :],
                                  k == 0, k == KT - 1)
                    return last

                w = full(("mix", f"out{layer}.0"))[:, 0:KT * 512].rearrange("p (k n) -> p k n", k=KT)
                if part == 0:
                    pe.wait_ge(S("fox_o" if layer == 0 else "nsa_o"), 4)
                    for j in range(4):
                        product(w, j, range(KT // 2))
                    return
                pe.wait_ge(S("y_ready"), 2 * (layer + 1))
                for j in range(KT):
                    if j == 4:
                        w = full(("mix", f"out{layer}.1"))[:, 0:KT * 512].rearrange("p (k n) -> p k n", k=KT)
                    if j >= 4:
                        pe.wait_ge(S("x_added"), 2 * KT * layer + j - 3)
                    product(w, j, range(0 if j >= 4 else KT // 2, KT)).then_inc(S("proj_ready"), 1)
                    if j >= 2:
                        feature_sum(2 * layer + 2, [j - 2])
                feature_sum(2 * layer + 2, [KT - 2, KT - 1])

            def head_sums(weights, sq, tiles, banks):
                for b in range(tiles // 2):
                    last = mm(bank[banks[b]][:, :], weights, sq[:, 2 * b:2 * b + 2, :], True, True)
                return last

            def three(out, w, c, x2, start):
                (w_hi, w_lo), (x_hi, x_lo) = w, x2
                pe.matmul(out, w_hi[:, c:c + P], x_hi, start=start, stop=start, skip_group_check=not start)
                pe.matmul(out, w_hi[:, c:c + P], x_lo, start=False, stop=False, skip_group_check=True)
                return pe.matmul(out, w_lo[:, c:c + P], x_hi, start=False, stop=False, skip_group_check=True)

            def expert_up(ft, split_value):
                pe.wait_ge(S("lo_ready"), split_value)
                for part in range(2):
                    for k in range(KT):
                        last = three(bank[4 + ft][:, part * T:(part + 1) * T], piece[ft], (part * KT + k) * P,
                                     (h2[0][:, k, :], h2[1][:, k, :]), k == 0)
                last.then_inc(S("gu_ready"), 1)

            def expert_down(ft, split_value, a_value, opens):
                pe.wait_ge(S("lo_ready"), split_value)
                pe.wait_ge(S("a_ready"), a_value)
                for m in range(KT):
                    last = three(bank[m // 2][:, (m % 2) * T:(m % 2 + 1) * T], piece[2 + ft], m * P,
                                 (a2[0][:, ft, :], a2[1][:, ft, :]), opens and m % 2 == 0)
                last.then_inc(S("down_done"), 1)

            def moe(layer):
                for t in range(NT):
                    for k in range(KT):
                        if t == 0:
                            pe.wait_ge(S("h_ready"), KT * (2 * layer + 1) + k + 1)
                        last = mm(bank[6][:, t * E:(t + 1) * E], hT[:, k, t * P:(t + 1) * P],
                                  pr("router")[:, (layer * KT + k) * E:(layer * KT + k + 1) * E],
                                  k == 0, k == KT - 1)
                last.then_inc(S("router_ready"), 1)
                pe.wait_ge(S("h_split"), 4 * (layer + 1))
                sp0, a0 = 4 * X * layer, 2 * X * layer

                def step(x, opens=False, last_expert=False):
                    expert_up(1, x * 4 + (sp0 + 2))
                    expert_down(0, x * 4 + (sp0 + 3), x * 2 + (a0 + 1), opens)
                    if not last_expert:
                        expert_up(0, x * 4 + (sp0 + 4))
                    expert_down(1, sp0 + 4 * X if last_expert else x * 4 + (sp0 + 5), x * 2 + (a0 + 2), False)

                expert_up(0, sp0 + 1)
                expert_up(1, sp0 + 2)
                expert_down(0, sp0 + 3, a0 + 1, True)
                pe.wait_ge(S("route_ready"), layer + 1)
                for t in range(NT):
                    last = tr(bank[7][0:E, t * P:(t + 1) * P], wroute[:, t, :])
                last.then_inc(S("route_turned"), 1)
                expert_up(0, sp0 + 4)
                expert_down(1, sp0 + 5, a0 + 2, False)
                with pe.Fori(1, X - 1) as x:
                    step(x)
                step(X - 1, last_expert=True)

            pe.wait_ge(S("heads_landed"), 32)
            feature_sum(1)
            for i in range(FIRST_ADAS):
                mod_columns(i)
            w = full(("mix", "in0.0"))[:, 0:KT * (FH * FDH + EV_SMALL)].rearrange("p (k n) -> p k n", k=KT)
            project_tokens(w, 0, FH * FDH, [bank[0][:, :], bank[1][:, :]], norms=1)
            project_tokens(w, FH * FDH, FH * FDH + EV_SMALL, [bank[2][:, 0:16], bank[3][:, 0:16]]
                           ).then_inc(S("tok_ready"), 1)
            for s in range(4):
                if s == 2:
                    pe.wait_ge(S("params_landed"), 32)
                    pe.wait_ge(S("tok_copied"), 6)
                    pe.wait_ge(S("fox_sq"), 4)
                    head_sums(cs("bd"), yT, 8, [0, 1, 2, 3]).then_inc(S("fox_ss"), 1)
                if s == 3:
                    pe.wait_ge(S("fox_rms"), 4)
                    pe.wait_ge(S("gdn_sq"), 4)
                    head_sums(ones, squares, 8, [0, 1, 2, 3]).then_inc(S("gdn_ss"), 1)
                w = full(("mix", f"in0.{s + 1}"))[:, :].rearrange("p (k n) -> p k n", k=KT)
                project_features(w, 6, 6 * s, 0)

            pe.wait_ge(S("feat_copied"), EV_TILES)
            mm(bank[4][0:NH, :], pr("rel")[0:BUCKETS + 1, :], cs("ohr")[0:BUCKETS + 1, :], True, True
               ).then_inc(S("rel_ready"), 1)
            mod_columns(3)
            mod_columns(4)
            pe.wait_ge(S("gdn_rms"), 4)
            pe.wait_ge(S("fox_qk"), 3)
            pe.wait_ge(S("logf_ready"), 1)

            units = [(h0 + i, qt) for h0 in range(0, FH, 2) for qt in range(NT) for i in range(2)]

            def fox_scores(u):
                h, qt = units[u]
                keys = P * (qt + 1)
                if u >= 2:
                    pe.wait_ge(S("fox_exp"), u - 1)
                s = bank[u % 2]
                mm(s[:, 0:keys], qpad[:, h, qt * P:(qt + 1) * P], feat[:, 4 + h // 2, 0:keys], True, False)
                mm(s[:, qt * P:(qt + 1) * P], ident, cs("maskq"), False, False)
                last = mm(s[:, 0:keys], logf[:, 0, h:h + 1].to_broadcast([P, P]), cs("ntri")[:, 0:keys],
                          False, qt == 0)
                if qt:
                    last = mm(s[:, P:2 * P], logf[:, 1, h:h + 1].to_broadcast([P, P]), cs("ntri")[:, 0:P],
                              False, True)
                last.then_inc(S("fox_s"), 1)

            def fox_turn(u):
                h, qt = units[u]
                pe.wait_ge(S("fox_p"), u + 1)
                if u >= 2:
                    pe.wait_ge(S("fox_pT"), u - 1)
                for k in range(qt + 1):
                    last = tr(bank[2 + u % 2][:, k * P:(k + 1) * P], prob[u % 2][:, k * P:(k + 1) * P])
                last.then_inc(S("fox_turned"), 1)

            def fox_values(u):
                h, qt = units[u]
                pe.wait_ge(S("fox_pT"), u + 1)
                if u == 0:
                    pe.wait_ge(S("rel_copied"), 1)
                if u % 4 == 0 and u >= 8:
                    pe.wait_ge(S("fox_o"), u // 4 - 1)
                for k in range(qt + 1):
                    last = mm(bank[4 + u // 4 % 2][:, qt * P:(qt + 1) * P], vpad[:, k, h, :],
                              probT[u % 2][:, k * P:(k + 1) * P], h % 2 == 0 and k == 0, h % 2 == 1 and k == qt)
                last.then_inc(S("fox_pv"), 1)

            for u in range(len(units) + 2):
                if u < len(units):
                    fox_scores(u)
                if u >= 2:
                    fox_values(u - 2)
                if 1 <= u <= len(units):
                    fox_turn(u - 1)
                if u % 3 == 0 and 3 < u < 16:
                    mod_columns(3 + u // 3)

            pe.wait_ge(S("gdn_g"), 1)
            for t in range(NT):
                last = mm(bank[6][:, t * GH:(t + 1) * GH], cs("tri"), gate[:, t, :], True, True)
            last.then_inc(S("gdn_cum"), 1)
            pe.wait_ge(S("gdn_qk"), 4)
            pe.wait_ge(S("gdn_rms"), 4)
            pe.wait_ge(S("fox_o"), 4)
            for t in range(NT):
                for h in range(GH):
                    cols = slice(h * P, (h + 1) * P)
                    g = gate[:, t, h:h + 1].to_broadcast([P, P])
                    mm(bank[3 * t][:, cols], g, cs("tri"), True, True)
                    mm(bank[3 * t + 1][:, cols], g, cs("tri"), True, False)
                    mm(bank[3 * t + 1][:, cols], ident, cs("mpos"), False, True)
                    mm(bank[3 * t + 2][:, cols], g, cs("tri"), True, False)
                    last = mm(bank[3 * t + 2][:, cols], ident, cs("mneg"), False, True)
            last.then_inc(S("gdn_gb"), 1)
            pe.wait_ge(S("mod_copied"), 9)
            pe.wait_ge(S("gdn_gc"), 2)
            for t in range(NT):
                for h in range(GH):
                    k = feat[:, 12 + h, t * P:(t + 1) * P]
                    last = mm(bank[6 + t][:, h * P:(h + 1) * P], k, k, True, True)
            last.then_inc(S("gdn_kk"), 1)
            pe.wait_ge(S("gdn_decay"), 18)
            for t in range(NT):
                for h in range(GH):
                    k = feat[:, 12 + h, t * P:(t + 1) * P]
                    mm(bank[t][:, h * P:(h + 1) * P], k, feat[:, 8 + h, t * P:(t + 1) * P], True, True)
                    tr(bank[2 + t][:, h * P:(h + 1) * P], k)
                    last = tr(bank[4 + t][:, h * P:(h + 1) * P], feat[:, 16 + h, t * P:(t + 1) * P])
            last.then_inc(S("gdn_turned"), 1)
            pe.wait_ge(S("gdn_a"), 8)
            for t in range(NT):
                for h in range(GH):
                    last = tr(bank[6 + t][:, h * P:(h + 1) * P], Am[:, t, h, :])
            last.then_inc(S("gdn_at"), 1)
            pe.wait_ge(S("gdn_attn"), 2)
            for lv in range(1, len(LEVELS)):
                pe.wait_ge(S("inv_x"), 2 + 4 * (lv - 1))
                pe.wait_ge(S("inv_atm"), lv)
                for t in range(NT):
                    for h in range(GH):
                        last = mm(bank[t][:, h * P:(h + 1) * P], ATm[lv % 2][:, t, h, :], Xi[:, t, h, :],
                                  True, True)
                last.then_inc(S("inv_p"), 1)
                if lv == 1:
                    pe.wait_ge(S("gdn_atc"), 2)
                    pe.wait_ge(S("gdn_kv"), 8)
                pe.wait_ge(S("inv_pc"), 2 * lv)
                for t in range(NT):
                    for h in range(GH):
                        cols = slice(h * P, (h + 1) * P)
                        if lv < len(LEVELS) - 1:
                            mm(bank[2 + t][:, cols], XT[:, t, h, :], Pm[:, t, h, :], True, True)
                        last = mm(bank[4 + t][:, cols], Pm[:, t, h, :], XT[:, t, h, :], True, True)
                last.then_inc(S("inv_xp"), 1)
                if lv == 1:
                    mod_columns(9)
                mod_columns(9 + lv)
            pe.wait_ge(S("inv_x"), INVX)
            pe.wait_ge(S("mod_copied"), len(ADAS) - 1)
            for t in range(NT):
                for h in range(GH):
                    cols = slice(h * P, (h + 1) * P)
                    mm(bank[6 + t][:, cols], XT[:, t, h, :], vb[:, t, h, :], True, True)
                    last = mm(bank[t][:, cols], kbe[:, t, h, :], XT[:, t, h, :], True, True)
            last.then_inc(S("gdn_uw"), 1)
            for n in range(NCH):
                t, half = n // 2, n % 2
                c0 = half * CHUNK
                if n:
                    pe.wait_ge(S("gdn_state"), 1 + GH * (n - 1))
                    pe.wait_ge(S("gdn_uwc"), 4)
                    for h in range(GH):
                        last = mm(bank[2][:, h * P:(h + 1) * P], wT[:, t, h, :], state[:, h, :], True, True)
                    last.then_inc(S("gdn_ws"), 1)
                pe.wait_ge(S("gdn_vn"), n + 1)
                if n < NCH - 1:
                    for h in range(GH):
                        last = mm(bank[4][:, h * P:(h + 1) * P], kd[half][:, t, h, :], vnew[:, h, :], True, True)
                    last.then_inc(S("gdn_su"), 1)
                if n:
                    pe.wait_ge(S("gdn_oc"), n)
                    pe.wait_ge(S("gdn_qd"), 2)
                for h in range(GH):
                    o = bank[3][:, h * CHUNK:(h + 1) * CHUNK]
                    if n:
                        mm(o, state[:, h, :], feat[:, 8 + h, t * P + c0:t * P + c0 + CHUNK], True, False)
                    last = mm(o, vnew[:, h, :], attnT[:, t, h, c0:c0 + CHUNK], n == 0, True)
                last.then_inc(S("gdn_o"), 1)
            mod_columns(15)
            pe.wait_ge(S("og_sq"), 2)
            for b in range(2):
                last = mm(bank[5 + b][:, :], ones, osq[:, 2 * b:2 * b + 2, :], True, True)
            last.then_inc(S("og_ss"), 1)
            pe.wait_ge(S("og_rms"), 2)
            out_projection(0, 0)
            out_projection(0, 1)
            moe(0)

            feature_sum(3)
            w = full(("mix", "in1.0"))[:, :].rearrange("p (k n) -> p k n", k=KT)
            project_tokens(w, 0, 512, [bank[0][:, :], bank[1][:, :]], norms=3)
            project_tokens(w, 512, OD_TOK, [bank[2][:, 0:256], bank[3][:, 0:256]]).then_inc(S("tok_half"), 1)
            w = full(("mix", "in1.1"))[:, 0:KT * (OD_GATES + LRANK)].rearrange("p (k n) -> p k n", k=KT)
            project_tokens(w, 0, OD_GATES, [bank[2][:, 256:256 + OD_GATES], bank[3][:, 256:256 + OD_GATES]])
            for k in range(KT):
                last = mm(bank[7][0:LRANK, 0:T], w[:, k, OD_GATES:OD_GATES + LRANK], hT[:, k, :],
                          k == 0, k == KT - 1)
            last.then_inc(S("tok_ready"), 1)
            for s in range(3):
                w = full(("mix", f"in1.{s + 2}"))[:, :].rearrange("p (k n) -> p k n", k=KT)
                project_features(w, 6, 6 * s, EV_TILES)
            pe.wait_ge(S("nsa_sq"), 3)
            pe.wait_ge(S("feat_copied"), EV_TILES + OD_TILES)
            for b in range(3):
                last = mm(bank[4 + b][:, :], cs("bd"), yT[:, 2 * b:2 * b + 2, :], True, True)
            last.then_inc(S("nsa_ss"), 1)
            pe.wait_ge(S("tok_copied"), 17)
            for t in range(NT):
                last = mm(bank[0][:, t * 256:(t + 1) * 256], lgT[0:LRANK, t * P:(t + 1) * P],
                          pr("wg_up")[0:LRANK, :], True, True)
            last.then_inc(S("gla_z"), 1)
            pe.wait_ge(S("cmp_blk"), 8)
            for kv in range(2):
                w = full(("mix", f"cmp.{kv}"))
                for l in range(16):
                    last = mm(bank[2 + kv][0:NKV * NCMP, 0:CHID], blk[:, kv, l, :], w[:, l * CHID:(l + 1) * CHID],
                              l == 0, l == 15)
                last.then_inc(S("cmp_h"), 1)
            for kv in range(2):
                pe.wait_ge(S("cmp_hc"), kv + 1)
                for ht in range(2):
                    last = pe.transpose(bank[2 + kv][:, 256 + ht * 32:256 + ht * 32 + NKV * NCMP],
                                        chidT[0:NKV * NCMP, kv, ht * P:(ht + 1) * P], ident[0:NKV * NCMP, 0:NKV * NCMP])
                last.then_inc(S("cmp_t"), 1)
            for kv in range(2):
                w = full(("mix", f"cmp.{kv}"))
                pe.wait_ge(S("cmp_a"), kv + 1)
                if kv == 0:
                    for n, (ht, g) in enumerate([(a, b) for a in range(2) for b in range(2)]):
                        c = 16 * CHID + (ht * 2 + g) * P
                        last = mm(bank[2][:, 384:384 + NCMP], w[:, c:c + P],
                                  chid[:, kv, ht, g * NCMP:(g + 1) * NCMP], n == 0, n == 3)
                else:
                    for g in range(NKV):
                        for ht in range(2):
                            c = 16 * CHID + ht * NDH
                            last = mm(bank[3][0:NCMP, 384 + g * NDH:384 + (g + 1) * NDH],
                                      chid[:, kv, ht, g * NCMP:(g + 1) * NCMP], w[:, c:c + NDH],
                                      ht == 0, ht == 1)
                last.then_inc(S("cmp_o"), 1)
            pe.wait_ge(S("cmp_sq"), 1)
            mm(bank[7][:, 0:NCMP], cs("bd"), csq[:, :], True, True).then_inc(S("nsa_ss"), 1)
            pe.wait_ge(S("nsa_qk"), 4)
            pe.wait_ge(S("cmp_kv"), 3)
            pe.wait_ge(S("nsa_rms"), 4)
            pe.wait_ge(S("gla_zc"), 1)

            nunits = [(h0 + i, qt) for h0 in range(4) for qt in range(NT) for i in (0, 4)]

            def nsa_scores(u):
                h, qt = nunits[u]
                keys = P * (qt + 1)
                if u >= 2:
                    pe.wait_ge(S("nsa_b"), 2 * (u - 1))
                q = qpad[:, h, qt * P:(qt + 1) * P]
                for br in range(2):
                    mm(bank[u % 2][:, br * T:br * T + keys], q, feat[:, 4 + br, 0:keys], True, True)
                if u:
                    pe.wait_ge(S("nsa_b"), 2 * u)
                mm(bank[6][:, 0:NCMP], q, kcn[:, :], True, True).then_inc(S("nsa_s"), 1)

            def nsa_turn(u):
                h, qt = nunits[u]
                pe.wait_ge(S("nsa_p"), 3 * (u + 1))
                if u >= 2:
                    pe.wait_ge(S("nsa_pT"), 2 * (u - 1))
                for br in range(2):
                    for k in range(qt + 1):
                        c = br * T + k * P
                        tr(bank[2 + u % 2][:, c:c + P], nprob[u % 2][:, c:c + P])
                if u:
                    pe.wait_ge(S("nsa_pT"), 2 * u)
                tr(bank[7][0:NCMP, 0:P], nprob[u % 2][:, 512:512 + NCMP]
                   ).then_inc(S("nsa_turned"), 1)

            def nsa_values(u):
                h, qt = nunits[u]
                g = h // 4
                pe.wait_ge(S("nsa_pT"), 2 * (u + 1))
                if u % 4 == 0 and u >= 8:
                    pe.wait_ge(S("nsa_o"), u // 4 - 1)
                out = bank[4 + u // 4 % 2][:, qt * P:(qt + 1) * P]
                mm(out, vcpad[0:NCMP, g, :], nprobT[u % 2][0:NCMP, 512:512 + P], g == 0, False)
                for br in range(2):
                    for k in range(qt + 1):
                        c = br * T + k * P
                        last = mm(out, nvpad[:, k, br, g, :], nprobT[u % 2][:, c:c + P], False,
                                  g == 1 and br == 1 and k == qt)
                last.then_inc(S("nsa_pv"), 1)

            for u in range(len(nunits) + 2):
                if u < len(nunits):
                    nsa_scores(u)
                if u >= 2:
                    nsa_values(u - 2)
                if 1 <= u <= len(nunits):
                    nsa_turn(u - 1)

            pe.wait_ge(S("gla_loga"), 1)
            pe.wait_ge(S("nsa_pT"), 2 * len(nunits))
            pe.wait_ge(S("nsa_o"), 4)
            for f in range(2):
                for t in range(NT):
                    last = mm(bank[0][:, (f * NT + t) * P:(f * NT + t + 1) * P], loga[:, t, f * P:(f + 1) * P],
                              cs("tri"), True, True)
            last.then_inc(S("gla_G"), 1)
            pe.wait_ge(S("gla_qk"), 4)
            for t in range(NT):
                for h in range(LH):
                    last = mm(bank[1 + t][:, h * P:(h + 1) * P], lki[:, h // 2, t * P:(t + 1) * P],
                              lqd[:, h, t * P:(t + 1) * P], True, True)
            for t in range(NT):
                for f in range(2):
                    last = tr(bank[3][:, (t * 2 + f) * P:(t * 2 + f + 1) * P], lkd[:, f, t * P:(t + 1) * P])
            last.then_inc(S("gla_at"), 1)
            pe.wait_ge(S("gla_ready"), 4)
            for n in range(NCH):
                t, half = n // 2, n % 2
                c0 = t * P + half * CHUNK
                if n:
                    pe.wait_ge(S("gla_state"), 1 + LH * (n - 1))
                if n < NCH - 1:
                    for h in range(LH):
                        last = mm(bank[5][:, h * P:(h + 1) * P], lkt[:, half, t, h // 2, :],
                                  toks[:, t, h * P:(h + 1) * P], True, True)
                    last.then_inc(S("gla_su"), 1)
                if n:
                    pe.wait_ge(S("gla_oc"), n)
                for h in range(LH):
                    o = bank[6][:, h * CHUNK:(h + 1) * CHUNK]
                    if n:
                        mm(o, lstate[:, h, :], lqd[:, h, c0:c0 + CHUNK], True, False)
                    last = mm(o, toks[:, t, h * P:(h + 1) * P],
                              lattn[:, t, h, half * CHUNK:(half + 1) * CHUNK], n == 0, True)
                last.then_inc(S("gla_o"), 1)
            pe.wait_ge(S("og_sq"), 4)
            for b in range(2):
                last = mm(bank[5 + b][:, :], ones, osq[:, 2 * b:2 * b + 2, :], True, True)
            last.then_inc(S("og_ss"), 1)
            out_projection(1, 0)
            out_projection(1, 1)
            moe(1)

        @block.scalar
        def _(sc):
            count = [0, 0]

            def act(out, in_, func, name=None, **kw):
                kw.setdefault("bias", eps(ZERO)[0:out.shape[0], :])
                ins = sc.activation(out, in_, func, **kw)
                if name is None:
                    count[0] += 1
                    ins.then_inc(S("act_chain"), 1)
                    sc.wait_ge(S("act_chain"), count[0])
                else:
                    ins.then_inc(S(name), 1)

            def copy(out, in_, name):
                sc.activation(out, in_, ACT.Copy).then_inc(S(name), 1)

            def inverse_roots(sums, name):
                for out, total, scale, shift in sums:
                    act(out, total, ACT.Ln, "root_log", scale=scale, bias=eps(shift))
                    count[1] += 1
                sc.wait_ge(S("root_log"), count[1])
                for out, _, _, _ in sums:
                    act(out, out, ACT.Exp, name, scale=-0.5)

            def pair(buffer, b):
                return buffer[:, 2 * b:2 * b + 2, :].rearrange("p a b -> p (a b)")

            def rms_root(n):
                sc.wait_ge(S("ss_ready"), n)
                inverse_roots([(rms[:, :], bank[4][:, 0:T], 1.0 / D, EPS1)], "rms_root")

            def log_part(x, out, name):
                act(out, x, ACT.Abs)
                act(out, out, ACT.Exp, scale=-1.0)
                act(out, out, ACT.Ln, name, bias=eps(ONE))

            def copy_features(first, a, b):
                for j in range(a, b):
                    sc.wait_ge(S("feat_ready"), first + j + 1)
                    copy(feat[:, j, :], bank[4 + j % 3][:, 0:T], "feat_copied")

            def moe(layer):
                n = place["shared", layer][0]
                full0 = [place["shared", layer][1]] + place["experts", layer][1]
                gu0, dn0 = 2 * X * layer, 2 * X * layer

                def high(x, c, k, step=None):
                    r = (n + k) % SLOTS
                    if c in (0, 1):
                        sc.wait_ge(S(f"slot_full{r}"), full0[k] if step is None else step * 16 + full0[k])
                    if k or layer:
                        name, value = (("gu_ready", x * 2 + (gu0 - 1 + c)) if c < 2 else
                                       ("down_done", x * 2 + (dn0 - 3 + c)))
                        sc.wait_ge(S(name), value)
                    w = ring[r][:, AT_PIECE[c]:AT_PIECE[c] + PIECE[c]]
                    copy(piece[c][0][:, :], w, "hi_ready")

                def silu(x, ft):
                    sc.wait_ge(S("gu_ready"), x * 2 + (gu0 + ft + 1))
                    act(silu_g[:, ft, :], bank[4 + ft][:, 0:T], ACT.Silu, "silu_ready")

                def step(x, k, loop=None, has_next=True, has_after=True):
                    silu(x, 1)
                    if has_next:
                        high(x + 1, 1, k + 1, loop)
                        high(x + 1, 2, k + 1, loop)
                        silu(x + 1, 0)
                        if has_after:
                            high(x + 2, 0, k + 2, loop)
                        high(x + 1, 3, k + 1, loop)

                sc.wait_ge(S("y_ready"), 2 * (layer + 1))
                high(0, 0, 0)
                high(0, 1, 0)
                high(0, 2, 0)
                rms_root(2 * layer + 2)
                for b in range(4):
                    sc.wait_ge(S("h_ready"), KT * (2 * layer + 1) + 2 * b + 2)
                    copy(h2[0][:, 2 * b:2 * b + 2, :], hT[:, 2 * b:2 * b + 2, :], "h_high")
                sc.wait_ge(S("router_ready"), layer + 1)
                act(rscore[:, :, :], bank[6][:, 0:NT * E].rearrange("p (a b) -> p a b", a=NT), ACT.Sigmoid,
                    "score_ready")
                silu(0, 0)
                high(1, 0, 1)
                high(0, 3, 0)
                silu(0, 1)
                high(1, 1, 1)
                high(1, 2, 1)
                sc.wait_ge(S("route_turned"), layer + 1)
                copy(wTs[:, :], bank[7][0:E, 0:T], "route_copied")
                sc.wait_ge(S("route_copied"), layer + 1)
                sc.dma_start(w_dram[layer].ap(), wTs[:, :]).then_inc(S("route_stored"), 16)
                silu(1, 0)
                high(2, 0, 2)
                high(1, 3, 1)
                with sc.Fori(0, LOOPS) as i:
                    for k in range(1, BODY + 1):
                        step(i * BODY + k, k, i)
                for x in range(TAIL, X):
                    step(x, x, has_next=x + 1 < X, has_after=x + 2 < X)

            sc.wait_ge(S("heads_landed"), 32)
            act(cond[:, :], pr("c"), ACT.Silu, "cond_ready")
            rms_root(1)
            sc.wait_ge(S("pads_zero"), 2)
            sc.wait_ge(S("tok_ready"), 1)
            for t in range(NT):
                v = bank[t][:, :].rearrange("p (h d) -> p h d", d=FDH)
                for odd in range(2):
                    copy(vpad[:, t, odd::2, odd * FDH:(odd + 1) * FDH], v[:, odd::2, :], "tok_copied")
                copy(sml[:, t, :], bank[2 + t][:, 0:EV_SMALL], "tok_copied")
            copy_features(0, 0, 12)
            sc.wait_ge(S("fox_ss"), 1)
            inverse_roots([(pair(frms, b), bank[b][:, :], 1.0 if b < 2 else 1.0 / FDH, EPS64 if b < 2 else EPS1)
                           for b in range(4)], "fox_rms")
            copy_features(0, 12, 15)
            sc.wait_ge(S("params_landed"), 32)
            act(sl("ea", (GH,)), pr("a_log"), ACT.Exp, "ea_ready")
            z, lg = sl("z", (NT, EV_SMALL)), sl("lg", (NT, EV_SMALL))
            sc.wait_ge(S("z_ready"), 3)
            log_part(z[:, :, 0:FH + GH], lg[:, :, 0:FH + GH], "lg_ready")
            copy_features(0, 15, 18)
            for b in range(4):
                sc.wait_ge(S("conv_ready"), 2 * b + 2)
                act(feat[:, 8 + 2 * b:10 + 2 * b, :], conv[:, 2 * b:2 * b + 2, :], ACT.Silu, "gdn_silu")
            sc.wait_ge(S("gdn_ss"), 1)
            inverse_roots([(pair(squares, b), bank[b][:, :], float(GD) if b < 2 else 1.0,
                            EPS128 if b < 2 else EPS1) for b in range(4)], "gdn_rms")
            copy_features(0, 18, EV_TILES)
            sc.wait_ge(S("rel_ready"), 1)
            copy(relrow[:, :], bank[4][0:NH, :], "rel_copied")
            for u in range(4 * FH // 2 + 1):
                if u < 4 * FH // 2:
                    keys = P * (u // 2 % 2 + 1)
                    sc.wait_ge(S("fox_nmax"), u + 1)
                    if u >= 2:
                        sc.wait_ge(S("fox_turned"), u - 1)
                    act(prob[u % 2][:, 0:keys], bank[u % 2][:, 0:keys], ACT.Exp, "fox_exp",
                        bias=sl("nmx", (12,))[:, u % 2:u % 2 + 1], accum_out=sl("rs", (12,))[:, u % 2:u % 2 + 1])
                if u >= 1:
                    keys = P * ((u - 1) // 2 % 2 + 1)
                    sc.wait_ge(S("fox_turned"), u)
                    if u >= 3:
                        sc.wait_ge(S("fox_pv"), u - 2)
                    copy(probT[(u - 1) % 2][:, 0:keys], bank[2 + (u - 1) % 2][:, 0:keys], "fox_pT")
                if u >= 4 and u % 4 == 0 and u < 4 * FH // 2:
                    sc.wait_ge(S("fox_pv"), u)
                    copy(yT[:, u // 4 - 1, :], bank[4 + (u // 4 - 1) % 2][:, 0:T], "fox_o")
            sc.wait_ge(S("fox_pv"), 4 * FH // 2)
            copy(yT[:, FH // 2 - 1, :], bank[4 + (FH // 2 - 1) % 2][:, 0:T], "fox_o")

            for b in range(4, 6):
                sc.wait_ge(S("conv_ready"), 2 * b + 2)
                act(feat[:, 8 + 2 * b:10 + 2 * b, :], conv[:, 2 * b:2 * b + 2, :], ACT.Silu, "gdn_silu")
            sc.wait_ge(S("feat_copied"), EV_TILES)
            for b in range(2):
                act(feat[:, 20 + 2 * b:22 + 2 * b, :], feat[:, 20 + 2 * b:22 + 2 * b, :], ACT.Silu, "gdn_silu")
            act(sl("beta", (NT, GH)), z[:, :, FH + GH:EV_SMALL], ACT.Sigmoid, "beta_ready")
            sc.wait_ge(S("gdn_gc"), 2)
            gc, ngc = sl("gc", (8,)), sl("ngc", (8,))
            act(sl("eg", (8,)), gc, ACT.Exp, "gdn_eg")
            sc.wait_ge(S("gdn_gb"), 1)
            sc.wait_ge(S("gdn_silu"), 8)
            for t in range(NT):
                act(Eb[:, t, :, :].rearrange("p a b -> p (a b)"), bank[3 * t][:, :], ACT.Exp, "gdn_decay")
                for h in range(GH):
                    i, cols = t * GH + h, slice(h * P, (h + 1) * P)
                    act(Dm[:, t, h, :], bank[3 * t + 1][:, cols], ACT.Exp, "gdn_decay", scale=-1.0,
                        bias=gc[:, i:i + 1])
                    act(DT[:, t, h, :], bank[3 * t + 2][:, cols], ACT.Exp, "gdn_decay", bias=ngc[:, i:i + 1])
            sc.wait_ge(S("gdn_at"), 1)
            for t in range(NT):
                copy(AT[:, t, :, :].rearrange("p a b -> p (a b)"), bank[6 + t][:, :], "gdn_atc")
            for lv in range(1, len(LEVELS)):
                sc.wait_ge(S("inv_p"), lv)
                if lv > 1:
                    sc.wait_ge(S("inv_xp"), lv - 1)
                for t in range(NT):
                    copy(Pm[:, t, :, :].rearrange("p a b -> p (a b)"), bank[t][:, :], "inv_pc")
            sc.wait_ge(S("gdn_uw"), 1)
            for t in range(NT):
                copy(wT[:, t, :, :].rearrange("p a b -> p (a b)"), bank[t][:, :], "gdn_uwc")
            for n in range(NCH):
                sc.wait_ge(S("gdn_o"), n + 1)
                copy(og[:, :, n * CHUNK:(n + 1) * CHUNK], bank[3][:, 0:GH * CHUNK].rearrange(
                    "p (h c) -> p h c", h=GH), "gdn_oc")
            sc.wait_ge(S("og_ss"), 1)
            inverse_roots([(pair(orms, b), bank[5 + b][:, :], 1.0 / GD, EPS1) for b in range(2)], "og_rms")
            moe(0)

            rms_root(3)
            sc.wait_ge(S("pads_zero"), 5)
            sc.wait_ge(S("tok_ready"), 2)
            for t in range(NT):
                v = bank[t][:, 0:2 * NKV * NDH].rearrange("p (b g d) -> p b g d", b=2, g=NKV)
                for g in range(NKV):
                    copy(nvpad[:, t, :, g, g * NDH:(g + 1) * NDH], v[:, :, g, :], "tok_copied")
                copy(toks[:, t, 0:256], bank[t][:, 256:512], "tok_copied")
                copy(toks[:, t, 256:512], bank[2 + t][:, 0:256], "tok_copied")
            copy(lgT[0:LRANK, :], bank[7][0:LRANK, 0:T], "tok_copied")
            for t in range(NT):
                act(sl("ngate", (NT, OD_GATES))[:, t, :], bank[2 + t][:, 256:256 + OD_GATES], ACT.Sigmoid,
                    "tok_copied")
            copy_features(EV_TILES, 0, OD_TILES)
            sc.wait_ge(S("nsa_ss"), 1)
            inverse_roots([(pair(nrms, b), bank[4 + b][:, :], 1.0 if b < 2 else 1.0 / NDH,
                            EPS64 if b < 2 else EPS1) for b in range(3)], "nsa_rms")
            sc.wait_ge(S("gla_zc"), 1)
            log_part(lz, loga, "gla_lg")
            for kv in range(2):
                sc.wait_ge(S("cmp_h"), kv + 1)
                copy(chidT[0:NKV * NCMP, kv, :], bank[2 + kv][0:NKV * NCMP, 0:CHID], "cmp_hc")
            for kv in range(2):
                sc.wait_ge(S("cmp_t"), kv + 1)
                h = bank[2 + kv][:, 256:320].rearrange("p (a b) -> p a b", a=2)[:, :, 0:NKV * NCMP]
                act(chid[:, kv, :, :], h, ACT.Silu, "cmp_a")
            sc.wait_ge(S("cmp_o"), 1)
            copy(kcn, bank[2][:, 384:384 + NCMP], "cmp_kv")
            sc.wait_ge(S("cmp_o"), 2)
            for g in range(NKV):
                copy(vcpad[0:NCMP, g, g * NDH:(g + 1) * NDH], bank[3][0:NCMP, 384 + g * NDH:384 + (g + 1) * NDH],
                     "cmp_kv")
            sc.wait_ge(S("nsa_ss"), 2)
            inverse_roots([(sl("crms", (16,))[:, 0:NCMP], bank[7][:, 0:NCMP], 1.0 / NDH, EPS1)], "nsa_rms")
            units = 2 * NH
            for u in range(units + 1):
                if u < units:
                    keys, c = P * (u // 2 % 2 + 1), 3 * (u % 2)
                    nm, rs = sl("nmx", (12,)), sl("rs", (12,))
                    sc.wait_ge(S("nsa_nmax"), u + 1)
                    act(nprob[u % 2][:, 512:512 + NCMP], nprob[u % 2][:, 512:512 + NCMP], ACT.Exp, "nsa_exp",
                        bias=nm[:, c:c + 1], accum_out=rs[:, c:c + 1])
                    for br in range(2):
                        p = nprob[u % 2][:, br * T:br * T + keys]
                        act(p, p, ACT.Exp, "nsa_exp", bias=nm[:, c + br + 1:c + br + 2],
                            accum_out=rs[:, c + br + 1:c + br + 2])
                if u >= 1:
                    v, qt = u - 1, (u - 1) // 2 % 2
                    sc.wait_ge(S("nsa_turned"), u)
                    if u >= 3:
                        sc.wait_ge(S("nsa_pv"), u - 2)
                    src, dst = (x[:, 0:512].rearrange("p (b k) -> p b k", b=2)[:, :, 0:P * (qt + 1)]
                                for x in (bank[2 + v % 2], nprobT[v % 2]))
                    copy(dst, src, "nsa_pT")
                    copy(nprobT[v % 2][0:NCMP, 512:512 + P], bank[7][0:NCMP, 0:P], "nsa_pT")
                if u >= 4 and u % 4 == 0 and u < units:
                    sc.wait_ge(S("nsa_pv"), u)
                    copy(yT[:, u // 4 - 1, :], bank[4 + (u // 4 - 1) % 2][:, 0:T], "nsa_o")
            sc.wait_ge(S("nsa_pv"), units)
            copy(yT[:, 3, :], bank[5][:, 0:T], "nsa_o")
            sc.wait_ge(S("gla_Gc"), 1)
            act(EG, G, ACT.Exp, "gla_exp")
            act(EnG, G, ACT.Exp, "gla_exp", scale=-1.0)
            sc.wait_ge(S("gla_dG"), 1)
            act(edG, edG, ACT.Exp, "gla_exp")
            for b in range(2):
                act(feat[:, 10 + 2 * b:12 + 2 * b, :], feat[:, 10 + 2 * b:12 + 2 * b, :], ACT.Silu, "gla_silu")
            for n in range(NCH):
                sc.wait_ge(S("gla_o"), n + 1)
                copy(og[:, :, n * CHUNK:(n + 1) * CHUNK], bank[6][:, 0:LH * CHUNK].rearrange(
                    "p (h c) -> p h c", h=LH), "gla_oc")
            sc.wait_ge(S("og_ss"), 2)
            inverse_roots([(pair(orms, b), bank[5 + b][:, :], 1.0 / LDV, EPS1) for b in range(2)], "og_rms")
            moe(1)

        @block.vector
        def _(ve):
            count = [0]

            def chain(ins, more=False):
                count[0] += 1
                ins.then_inc(S("vec_chain"), 1)
                if not more:
                    ve.wait_ge(S("vec_chain"), count[0])

            def sig(ins, name):
                ins.then_inc(S(name), 1)

            def mod_products(i):
                w, out = ada_slot(ve, i), partial[i % 2][:, :]
                for k in range(KT):
                    if k == 0:
                        last = ve.tensor_scalar(out, w[:, k, :], cond[:, k:k + 1], None, ALU.mult)
                    else:
                        last = ve.scalar_tensor_tensor(out, w[:, k, :], cond[:, k:k + 1], out, ALU.mult, ALU.add)
                    if k < KT - 1:
                        chain(last)
                sig(last, "mod_partial")

            def mod_scale(i):
                w = ada_slot(ve, i)
                for k in range(KT):
                    sig(ve.tensor_scalar(w[:, k, :], w[:, k, :], cond[:, k:k + 1], None, ALU.mult), "mod_scaled")

            def mod_add(i):
                ve.wait_ge(S("mod_turned"), i + 1)
                sig(ve.tensor_tensor(mod[:, 6 * i:6 * i + 6], bank[7][:, 0:6],
                                     pr("ada_b")[:, 6 * i:6 * i + 6], ALU.add), "mod_copied")

            def norm(n, meanwhile=None):
                layer, half = (n - 1) // 2, (n - 1) % 2
                if n == 1:
                    for m in range(KT):
                        square(hT[:, m, :], xT[:, m, :], "sq_ready")
                    ve.wait_ge(S("cond_ready"), 1)
                    for i in range(FIRST_ADAS):
                        if i >= 2:
                            ve.wait_ge(S("mod_turned"), i - 1)
                        mod_products(i)
                        if i:
                            mod_add(i - 1)
                    mod_add(FIRST_ADAS - 1)
                ve.wait_ge(S("mod_copied"), FIRST_ADAS if n == 1 else 16)
                m0 = 48 * layer + 24 * half
                g0 = pr("norm_ffn" if half else "norm_mix")[:, layer * KT:(layer + 1) * KT]
                chain(ve.scalar_tensor_tensor(gain[:, :], mod[:, m0 + KT:m0 + 2 * KT], 1.0, g0, ALU.add, ALU.mult))
                if meanwhile:
                    meanwhile()
                ve.wait_ge(S("rms_root"), n)
                for k in range(KT + 1):
                    if k < KT:
                        sig(ve.scalar_tensor_tensor(hT[:, k, :], xT[:, k, :], gain[:, k:k + 1], rms[:, :],
                                                    ALU.mult, ALU.mult), "h_scaled")
                    if k:
                        ve.wait_ge(S("h_scaled"), KT * (n - 1) + k)
                        sig(ve.tensor_scalar(hT[:, k - 1, :], hT[:, k - 1, :], mod[:, m0 + k - 1:m0 + k], None,
                                             ALU.add), "h_ready")

            def add_to_x(source, layer, half, m):
                g = 48 * layer + 24 * half + 2 * KT + m
                sig(ve.scalar_tensor_tensor(xT[:, m, :], source, mod[:, g:g + 1], xT[:, m, :], ALU.mult, ALU.add),
                    "x_added")
                ve.wait_ge(S("x_added"), 2 * KT * layer + KT * half + m + 1)
                if (layer, half) != (1, 1):
                    square(hT[:, m, :], xT[:, m, :], "sq_ready")

            def mixer_residual(layer):
                ve.wait_ge(S("mod_copied"), 16)
                for m in range(KT):
                    ve.wait_ge(S("proj_ready"), KT * layer + m + 1)
                    add_to_x(bank[m % 4][:, 0:T], layer, 0, m)

            def pick(v, thr, k, n, out, buf):
                eq, gt, run = buf[0][:, :, 0:n], buf[1][:, :, 0:n], [buf[2][:, :, 0:n], buf[3][:, :, 0:n]]
                left = sl("left", (NT, 2))[:, :, 0:1]
                chain(ve.tensor_tensor(eq, v, thr.to_broadcast([P, NT, n]), ALU.is_equal), more=True)
                chain(ve.tensor_tensor(gt, v, thr.to_broadcast([P, NT, n]), ALU.is_gt))
                chain(ve.tensor_reduce(left, gt, AX.X, ALU.add))
                chain(ve.tensor_scalar(left, left, -1.0, float(k), ALU.mult, ALU.add))
                src, step, i = eq, 1, 0
                while step < n:
                    dst = run[i % 2]
                    chain(ve.tensor_copy(dst[:, :, 0:step], src[:, :, 0:step]), more=True)
                    chain(ve.tensor_tensor(dst[:, :, step:n], src[:, :, step:n], src[:, :, 0:n - step], ALU.add))
                    src, step, i = dst, 2 * step, i + 1
                other = run[i % 2]
                chain(ve.tensor_tensor(other, src, left.to_broadcast([P, NT, n]), ALU.is_le))
                chain(ve.tensor_tensor(other, other, eq, ALU.mult))
                chain(ve.tensor_tensor(out, other, gt, ALU.add))

            def routing(layer):
                ve.wait_ge(S("score_ready"), layer + 1)
                bias = pr("e_bias")[:, layer * E:(layer + 1) * E]
                for t in range(NT):
                    chain(ve.tensor_tensor(rbias[:, t, :], rscore[:, t, :], bias, ALU.add), more=t < NT - 1)
                m8, gs, gm = sl("m8", (NT * GROUPS, 8)), sl("gs", (NT, GROUPS)), sl("gm", (NT, GROUPS))
                for t in range(NT):
                    for g in range(GROUPS):
                        chain(ve.max(m8[:, t * GROUPS + g, :], rbias[:, t, g * 8:(g + 1) * 8]),
                              more=(t, g) != (NT - 1, GROUPS - 1))
                chain(ve.tensor_tensor(gs.rearrange("p a b -> p (a b)"), m8[:, :, 0], m8[:, :, 1], ALU.add))
                g8, e8 = sl("g8", (NT, 8)), sl("e8", (NT, 8))
                for t in range(NT):
                    chain(ve.max(g8[:, t, :], gs[:, t, :]), more=t < NT - 1)
                pick(gs, g8[:, :, TOPG - 1:TOPG], TOPG, GROUPS, gm, rbuf)
                chain(ve.tensor_scalar(gs, gm, -1.0, -NEG, ALU.add, ALU.mult))
                per = E // GROUPS
                for t in range(NT):
                    r = rbias[:, t, :].rearrange("p (g j) -> p g j", j=per)
                    chain(ve.tensor_tensor(r, r, gs[:, t, :].unsqueeze(2).to_broadcast([P, GROUPS, per]), ALU.add),
                          more=t < NT - 1)
                for t in range(NT):
                    chain(ve.max(e8[:, t, :], rbias[:, t, :]), more=t < NT - 1)
                pick(rbias[:, :, :], e8[:, :, TOPK - 1:TOPK], TOPK, E, wroute[:, :, :], rbuf)
                chain(ve.tensor_tensor(wroute[:, :, :], wroute[:, :, :], rscore[:, :, :], ALU.mult))
                ws = sl("wsum", (NT, 2))[:, :, 0:1]
                chain(ve.tensor_reduce(ws, wroute[:, :, :], AX.X, ALU.add))
                chain(ve.reciprocal(ws, ws))
                chain(ve.tensor_scalar(ws, ws, ROUTE_SCALE, None, ALU.mult))
                sig(ve.tensor_tensor(wroute[:, :, :], wroute[:, :, :], ws.to_broadcast([P, NT, E]), ALU.mult),
                    "route_ready")

            def moe(layer):
                n = place["shared", layer][0]
                hi0, su0, route0 = 4 * X * layer, 2 * X * layer, []
                for x in range(1, X):
                    r = (n + x) % SLOTS
                    route0.append(16 * (1 + sum((n + y) % SLOTS == r for y in range(1, x))
                                        + (0 if layer == 0 else sum((place["shared", 0][0] + y) % SLOTS == r
                                                                    for y in range(1, X)))))

                def low(x, c, k, value=None):
                    r = (n + k) % SLOTS
                    ve.wait_ge(S("hi_ready"), x * 4 + (hi0 + (0, 2, 3, 5)[c]) if value is None else value)
                    w = ring[r][:, AT_PIECE[c]:AT_PIECE[c] + PIECE[c]]
                    sig(ve.tensor_tensor(piece[c][1][:, :], w, piece[c][0][:, :].bitcast(F32), ALU.subtract),
                        "lo_ready")

                def product(x, ft, k, step=None):
                    up, g = bank[4 + ft][:, T:2 * T], silu_g[:, ft, :]
                    ve.wait_ge(S("silu_ready"), x * 2 + (su0 + ft + 1))
                    chained(ve.tensor_tensor(g, g, up, ALU.mult), x, ft, 1)
                    if k:
                        r = (n + k) % SLOTS
                        value = route0[k - 1]
                        ve.wait_ge(S(f"route_full{r}"), value if step is None else step * 16 + value)
                        chained(ve.tensor_tensor(g, g, route_w[r][:, :], ALU.mult), x, ft, 2)
                    if k or layer:
                        ve.wait_ge(S("down_done"), x * 2 + (2 * X * layer - 1 + ft))
                    chained(ve.tensor_copy(a2[0][:, ft, :], g), x, ft, 3)
                    sig(ve.tensor_tensor(a2[1][:, ft, :], g, a2[0][:, ft, :].bitcast(F32), ALU.subtract), "a_ready")

                def chained(ins, x, ft, i):
                    ins.then_inc(S(f"product{i}"), 1)
                    done = 2 * X * layer + ft + 1
                    if i == 2:
                        done -= 2 * (layer + 1)
                    ve.wait_ge(S(f"product{i}"), x * 2 + done)

                def step(x, k, loop=None, has_next=True, has_after=True):
                    product(x, 1, k, loop)
                    if has_next:
                        low(x + 1, 1, k + 1)
                        low(x + 1, 2, k + 1)
                        product(x + 1, 0, k + 1, loop)
                        if has_after:
                            low(x + 2, 0, k + 2)
                        low(x + 1, 3, k + 1, None if has_after else hi0 + 4 * X)

                norm(2 * layer + 2, lambda: low(0, 0, 0, hi0 + 1))
                for b in range(4):
                    ve.wait_ge(S("h_high"), 4 * layer + b + 1)
                    sig(ve.tensor_tensor(h2[1][:, 2 * b:2 * b + 2, :], hT[:, 2 * b:2 * b + 2, :],
                                         h2[0][:, 2 * b:2 * b + 2, :].bitcast(F32), ALU.subtract), "h_split")
                low(0, 1, 0)
                low(0, 2, 0)
                product(0, 0, 0)
                low(1, 0, 1)
                low(0, 3, 0)
                routing(layer)
                product(0, 1, 0)
                low(1, 1, 1)
                low(1, 2, 1)
                product(1, 0, 1)
                low(2, 0, 2)
                low(1, 3, 1)
                with ve.Fori(0, LOOPS) as i:
                    for k in range(1, BODY + 1):
                        step(i * BODY + k, k, i)
                for x in range(TAIL, X):
                    step(x, x, has_next=x + 1 < X, has_after=x + 2 < X)
                ve.wait_ge(S("down_done"), 2 * X * (layer + 1))
                for m in range(KT):
                    add_to_x(bank[m // 2][:, (m % 2) * T:(m % 2 + 1) * T], layer, 1, m)

            def square(out, in_, name):
                sig(ve.tensor_tensor(out, in_, in_, ALU.mult), name)

            def output_norm(layer, on, silu_first):
                for b in range(2):
                    square(osq[:, 2 * b:2 * b + 2, :], og[:, 2 * b:2 * b + 2, :], "og_sq")
                ve.wait_ge(S("og_rms"), 2 * (layer + 1))
                for b in range(2):
                    r = orms[:, 2 * b:2 * b + 2, :]
                    o = og[:, 2 * b:2 * b + 2, :]
                    chain(ve.scalar_tensor_tensor(o, o, on, r, ALU.mult, ALU.mult))
                    sig(ve.tensor_tensor(yT[:, 4 + 2 * b:6 + 2 * b, :], o,
                                         feat[:, silu_first + 2 * b:silu_first + 2 * b + 2, :], ALU.mult), "y_ready")

            ve.wait_ge(S("heads_landed"), 32)
            ve.wait_ge(S("x_landed"), 16)
            norm(1)
            ve.wait_ge(S("params_landed"), 32)
            z, lg = sl("z", (NT, EV_SMALL)), sl("lg", (NT, EV_SMALL))
            ve.wait_ge(S("tok_copied"), 6)
            sig(ve.tensor_tensor(z[:, :, 0:FH], sml[:, :, 0:FH],
                                 pr("fox_fb").unsqueeze(1).to_broadcast([P, NT, FH]), ALU.add), "z_ready")
            sig(ve.tensor_tensor(z[:, :, FH:FH + GH], sml[:, :, FH:FH + GH],
                                 pr("dt_bias").unsqueeze(1).to_broadcast([P, NT, GH]), ALU.add), "z_ready")
            sig(ve.tensor_copy(z[:, :, FH + GH:EV_SMALL], sml[:, :, FH + GH:EV_SMALL]), "z_ready")
            for b in range(4):
                ve.wait_ge(S("feat_copied"), 2 * b + 2)
                f = feat[:, 2 * b:2 * b + 2, :]
                square(yT[:, 2 * b:2 * b + 2, :], f, "fox_sq")
            def convolve(j):
                ve.wait_ge(S("feat_copied"), 8 + j + 1)
                for tap in range(4):
                    w = pr("conv")[:, 4 * j + 3 - tap:4 * j + 4 - tap]
                    src, dst = feat[:, 8 + j, 0:T - tap], conv[:, j, tap:T]
                    if tap == 0:
                        chain(ve.tensor_scalar(dst, src, w, None, ALU.mult))
                    elif tap < 3:
                        chain(ve.scalar_tensor_tensor(dst, src, w, dst, ALU.mult, ALU.add))
                    else:
                        sig(ve.scalar_tensor_tensor(dst, src, w, dst, ALU.mult, ALU.add), "conv_ready")

            for j in range(7):
                convolve(j)
            mod_scale(3)
            ve.wait_ge(S("pads_zero"), 2)
            ve.wait_ge(S("fox_rms"), 4)
            for odd in range(2):
                rows = slice(64 * odd, 64 * odd + 64)
                sig(ve.scalar_tensor_tensor(qpad[rows, odd::2, :], feat[rows, 0:4, :], pr("fox_qn")[rows, :],
                                            frms[rows, 0:4, :], ALU.mult, ALU.mult), "fox_qk")
            sig(ve.scalar_tensor_tensor(feat[:, 4:8, :], feat[:, 4:8, :], pr("fox_kn"), frms[:, 4:8, :],
                                        ALU.mult, ALU.mult), "fox_qk")
            convolve(7)
            for b in range(4):
                ve.wait_ge(S("gdn_silu"), b + 1)
                f = feat[:, 8 + 2 * b:10 + 2 * b, :]
                square(squares[:, 2 * b:2 * b + 2, :], f, "gdn_sq")
            mod_scale(4)
            ve.wait_ge(S("lg_ready"), 1)
            ve.wait_ge(S("ea_ready"), 1)
            chain(ve.tensor_scalar(logf, z[:, :, 0:FH], 0.0, None, ALU.min))
            sig(ve.tensor_tensor(logf, logf, lg[:, :, 0:FH], ALU.subtract), "logf_ready")
            chain(ve.tensor_scalar(gate, z[:, :, FH:FH + GH], 0.0, None, ALU.max))
            chain(ve.tensor_tensor(gate, gate, lg[:, :, FH:FH + GH], ALU.add))
            chain(ve.tensor_scalar(gate, gate, -1.0, None, ALU.mult))
            sig(ve.tensor_tensor(gate, gate, sl("ea", (GH,)).unsqueeze(1).to_broadcast([P, NT, GH]), ALU.mult),
                "gdn_g")
            for j in range(8, 12):
                convolve(j)
            for b in range(4):
                ve.wait_ge(S("gdn_rms"), b + 1)
                f = feat[:, 8 + 2 * b:10 + 2 * b, :]
                sig(ve.tensor_tensor(f, f, squares[:, 2 * b:2 * b + 2, :], ALU.mult), "gdn_qk")
            mod_add(3)
            mod_add(4)
            mx, nmx, rs = sl("mx", (12,)), sl("nmx", (12,)), sl("rs", (12,))
            for u in range(4 * FH // 2 + 1):
                if u < 4 * FH // 2:
                    keys, c = P * (u // 2 % 2 + 1), u % 2
                    ve.wait_ge(S("fox_s"), u + 1)
                    chain(ve.reduce_max(mx[:, c:c + 1], bank[c][:, 0:keys], AX.X))
                    if u >= 2:
                        ve.wait_ge(S("fox_exp"), u - 1)
                    sig(ve.tensor_scalar(nmx[:, c:c + 1], mx[:, c:c + 1], -1.0, None, ALU.mult), "fox_nmax")
                if u >= 1:
                    keys, c = P * ((u - 1) // 2 % 2 + 1), (u - 1) % 2
                    ve.wait_ge(S("fox_exp"), u)
                    chain(ve.reciprocal(rs[:, 4 + c:5 + c], rs[:, c:c + 1]))
                    p = prob[c][:, 0:keys]
                    sig(ve.tensor_scalar(p, p, rs[:, 4 + c:5 + c], None, ALU.mult), "fox_p")
                if u % 3 == 0 and 3 < u < 16:
                    mod_add(3 + u // 3)
                if u % 3 == 1 and u < 16:
                    mod_scale(5 + u // 3)

            mod_scale(10)
            gc, ngc, be, beta = sl("gc", (8,)), sl("ngc", (8,)), sl("be", (8,)), sl("beta", (8,))
            ve.wait_ge(S("gdn_cum"), 1)
            sig(ve.tensor_copy(gc, bank[6][:, 0:8]), "gdn_gc")
            sig(ve.tensor_scalar(ngc, bank[6][:, 0:8], -1.0, None, ALU.mult), "gdn_gc")
            ve.wait_ge(S("gdn_eg"), 1)
            ve.wait_ge(S("beta_ready"), 1)
            chain(ve.tensor_tensor(be, beta, sl("eg", (8,)), ALU.mult))
            mod_scale(11)
            ve.wait_ge(S("gdn_kk"), 1)
            ve.wait_ge(S("gdn_decay"), 18)
            for t in range(NT):
                for h in range(GH):
                    i = t * GH + h
                    sig(ve.scalar_tensor_tensor(Am[:, t, h, :], bank[6 + t][:, h * P:(h + 1) * P], beta[:, i:i + 1],
                                                Dm[:, t, h, :], ALU.mult, ALU.mult), "gdn_a")
            kdc = sl("kdc", (2, 8))
            for half in range(2):
                chain(ve.tensor_copy(kdc[:, half, :], DT.rearrange("p a b c -> p (a b) c")
                                     [:, :, half * CHUNK + CHUNK - 1]))
            def by8(a):
                return a.rearrange("p a b c -> p (a b) c")

            def over8(m):
                return m.unsqueeze(1).to_broadcast([P, 2 * GH, P])

            ve.wait_ge(S("gdn_a"), 8)
            chain(ve.tensor_tensor(by8(Xi), by8(Am), over8(cs("lev1")), ALU.mult))
            sig(ve.tensor_tensor(by8(Xi), over8(ident), by8(Xi), ALU.subtract), "inv_x")
            mod_scale(12)
            ve.wait_ge(S("gdn_turned"), 1)
            ve.wait_ge(S("fox_pv"), 4 * FH // 2)

            def by4(b):
                return bank[b][:, :].rearrange("p (h d) -> p h d", h=GH)

            def col4(v, t):
                return v[:, t * GH:(t + 1) * GH].unsqueeze(2).to_broadcast([P, GH, P])

            for t in range(NT):
                sig(ve.tensor_tensor(attnT[:, t, :, :], by4(t), DT[:, t, :, :], ALU.mult), "gdn_attn")
            ve.wait_ge(S("gdn_atc"), 2)
            chain(ve.tensor_tensor(by8(XT), by8(AT), over8(cs("levt", 0, P)), ALU.mult))
            sig(ve.tensor_tensor(by8(XT), over8(ident), by8(XT), ALU.subtract), "inv_x")

            def joined(lv):
                sig(ve.tensor_tensor(by8(ATm[lv % 2]), by8(AT), over8(cs("levt", lv * P, (lv + 1) * P)), ALU.mult),
                    "inv_atm")

            joined(1)
            for t in range(NT):
                sig(ve.tensor_tensor(vb[:, t, :, :], by4(4 + t), col4(beta, t), ALU.mult), "gdn_kv")
                sig(ve.tensor_tensor(kbe[:, t, :, :], by4(2 + t), col4(be, t), ALU.mult), "gdn_kv")
                for half in range(2):
                    sig(ve.tensor_tensor(kd[half][:, t, :, :], by4(2 + t), col4(kdc[:, half, :], t), ALU.mult),
                        "gdn_kv")
                q = feat[:, 8:12, t * P:(t + 1) * P]
                sig(ve.tensor_tensor(q, q, Eb[:, t, :, :], ALU.mult), "gdn_qd")
            joined(2)
            for lv in range(1, len(LEVELS)):
                if 2 <= lv < len(LEVELS) - 1:
                    ve.wait_ge(S("inv_p"), lv - 1)
                    joined(lv + 1)
                ve.wait_ge(S("inv_xp"), lv)
                for t in range(NT):
                    if lv < len(LEVELS) - 1:
                        sig(ve.tensor_tensor(Xi[:, t, :, :], Xi[:, t, :, :], by4(2 + t), ALU.subtract), "inv_x")
                    sig(ve.tensor_tensor(XT[:, t, :, :], XT[:, t, :, :], by4(4 + t), ALU.subtract), "inv_x")
                if lv == 1:
                    mod_add(9)
                mod_add(9 + lv)
                if lv <= 3:
                    mod_scale(12 + lv)
                ve.wait_ge(S("inv_x"), 2 + 4 * lv if lv < len(LEVELS) - 1 else INVX)
            ve.wait_ge(S("gdn_uw"), 1)
            for t in range(NT):
                sig(ve.tensor_copy(u_sb[:, t, :, :], by4(6 + t)), "gdn_uwc")
            ve.wait_ge(S("gdn_uwc"), 4)
            for n in range(NCH):
                t, half = n // 2, n % 2
                if n == 0:
                    sig(ve.tensor_copy(vnew, u_sb[:, 0, :, :]), "gdn_vn")
                else:
                    ve.wait_ge(S("gdn_ws"), n)
                    ve.wait_ge(S("gdn_o"), n)
                    sig(ve.tensor_tensor(vnew, u_sb[:, t, :, :], by4(2), ALU.subtract), "gdn_vn")
                if n < NCH - 1:
                    ve.wait_ge(S("gdn_su"), n + 1)
                    ve.wait_ge(S("gdn_o"), n + 1)
                    if n == 0:
                        sig(ve.tensor_copy(state, by4(4)), "gdn_state")
                    else:
                        for h in range(GH):
                            c = half * CHUNK + CHUNK - 1
                            sig(ve.scalar_tensor_tensor(state[:, h, :], state[:, h, :], Eb[:, t, h, c:c + 1],
                                                        bank[4][:, h * P:(h + 1) * P], ALU.mult, ALU.add),
                                "gdn_state")
                    ve.wait_ge(S("gdn_state"), 1 + GH * n)
            ve.wait_ge(S("gdn_oc"), NCH)
            ve.wait_ge(S("gdn_silu"), 8)
            mod_add(15)
            output_norm(0, pr("gdn_on"), 20)
            mixer_residual(0)
            moe(0)

            norm(3)
            ve.wait_ge(S("feat_copied"), EV_TILES + 6)
            for b in range(3):
                f = feat[:, 2 * b:2 * b + 2, :]
                square(yT[:, 2 * b:2 * b + 2, :], f, "nsa_sq")
            ve.wait_ge(S("feat_copied"), EV_TILES + OD_TILES)
            for kv in range(2):
                for g in range(NKV):
                    for s in range(2):
                        rows = slice(64 * s, 64 * s + 64)
                        src = feat[rows, 14 + 2 * kv + g, 16 * s:16 * s + 16 * NCMP].rearrange(
                            "p (n l) -> p l n", l=16)
                        pos = pr("pos")[rows, 16 * kv:16 * kv + 16].unsqueeze(2).to_broadcast([64, 16, NCMP])
                        sig(ve.tensor_tensor(blk[rows, kv, :, g * NCMP:(g + 1) * NCMP], src, pos, ALU.add),
                            "cmp_blk")
            ve.wait_ge(S("gla_z"), 1)
            sig(ve.tensor_tensor(lz, bank[0][:, :].rearrange("p (a b) -> p a b", a=NT),
                                 pr("bg").unsqueeze(1).to_broadcast([P, NT, 256]), ALU.add), "gla_zc")
            ve.wait_ge(S("gla_lg"), 1)
            chain(ve.tensor_scalar(lz, lz, 0.0, None, ALU.min))
            chain(ve.tensor_tensor(loga, lz, loga, ALU.subtract))
            sig(ve.tensor_scalar(loga, loga, 1.0 / TAU, None, ALU.mult), "gla_loga")
            ve.wait_ge(S("pads_zero"), 5)
            ve.wait_ge(S("nsa_rms"), 3)
            for odd in range(2):
                rows = slice(64 * odd, 64 * odd + 64)
                sig(ve.scalar_tensor_tensor(qpad[rows, 4 * odd:4 * odd + 4, :], feat[rows, 0:4, :],
                                            pr("nsa_qn")[rows, :], nrms[rows, 0:4, :], ALU.mult, ALU.mult), "nsa_qk")
            sig(ve.scalar_tensor_tensor(feat[:, 4:6, :], feat[:, 4:6, :], pr("nsa_kn"), nrms[:, 4:6, :],
                                        ALU.mult, ALU.mult), "nsa_qk")
            ve.wait_ge(S("cmp_kv"), 1)
            square(csq, kcn, "cmp_sq")
            ve.wait_ge(S("nsa_rms"), 4)
            crms = sl("crms", (16,))[:, 0:NCMP]
            sig(ve.scalar_tensor_tensor(kcn, kcn, pr("nsa_kn"), crms, ALU.mult, ALU.mult), "nsa_qk")
            ve.wait_ge(S("nsa_qk"), 4)
            ve.wait_ge(S("brel_landed"), 32)
            units = [(h0 + i, qt) for h0 in range(4) for qt in range(NT) for i in (0, 4)]
            ngate = sl("ngate", (NT, OD_GATES))
            for u in range(len(units) + 1):
                if u < len(units):
                    h, qt = units[u]
                    keys, c = P * (qt + 1), 3 * (u % 2)
                    p = nprob[u % 2][:, 0:512].rearrange("p (b k) -> p b k", b=2)[:, :, 0:keys]
                    pc = nprob[u % 2][:, 512:512 + NCMP]
                    ve.wait_ge(S("nsa_s"), u + 1)
                    if u >= 2:
                        ve.wait_ge(S("nsa_turned"), u - 1)
                    sig(ve.tensor_tensor(p, bank[u % 2][:, :].rearrange("p (b k) -> p b k", b=2)[:, :, 0:keys],
                                         Brel[:, qt, h, 0:keys].unsqueeze(1).to_broadcast([P, 2, keys]), ALU.add),
                        "nsa_b")
                    sig(ve.tensor_tensor(pc, bank[6][:, 0:NCMP], Brel[:, qt, h, CMP_LEN - 1::CMP_STRIDE],
                                         ALU.add), "nsa_b")
                    ve.wait_ge(S("nsa_b"), 2 * (u + 1))
                    chain(ve.reduce_max(mx[:, c:c + 1], pc, AX.X))
                    chain(ve.reduce_max(mx[:, c + 1:c + 3], p, AX.X))
                    sig(ve.tensor_scalar(nmx[:, c:c + 3], mx[:, c:c + 3], -1.0, None, ALU.mult), "nsa_nmax")
                if u >= 1:
                    h, qt = units[u - 1]
                    keys, c = P * (qt + 1), 3 * ((u - 1) % 2)
                    rg = sl("rg", (12,))[:, c:c + 3]
                    ve.wait_ge(S("nsa_exp"), 3 * u)
                    chain(ve.reciprocal(rg, rs[:, c:c + 3]))
                    chain(ve.tensor_tensor(rg, rg, ngate[:, qt, 3 * h:3 * h + 3], ALU.mult))
                    pc = nprob[(u - 1) % 2][:, 512:512 + NCMP]
                    sig(ve.scalar_tensor_tensor(pc, pc, rg[:, 0:1], cs("cmask")[:, qt * NCMP:(qt + 1) * NCMP],
                                                ALU.mult, ALU.mult), "nsa_p")
                    for br in range(2):
                        p = nprob[(u - 1) % 2][:, br * T:br * T + keys]
                        sig(ve.tensor_scalar(p, p, rg[:, br + 1:br + 2], None, ALU.mult), "nsa_p")

            ve.wait_ge(S("gla_G"), 1)
            sig(ve.tensor_copy(G.rearrange("p a b -> p (a b)"), bank[0][:, :]), "gla_Gc")
            ve.wait_ge(S("gla_Gc"), 1)
            for f in range(2):
                g = G[:, f, :].rearrange("p (n c) -> p n c", c=CHUNK)
                last = ve.tensor_tensor(edG[:, f, :].rearrange("p (n c) -> p n c", c=CHUNK),
                                        g[:, :, CHUNK - 1:CHUNK].to_broadcast([P, NCH, CHUNK]), g, ALU.subtract)
                if f == 0:
                    chain(last)
            sig(last, "gla_dG")
            ve.wait_ge(S("gla_exp"), 3)
            ve.wait_ge(S("pads_zero"), 6)
            for odd in range(2):
                rows = slice(64 * odd, 64 * odd + 64)
                sig(ve.scalar_tensor_tensor(lqd[rows, odd::2, :], feat[rows, 6:8, :], LDK ** -0.5, EG[rows, :, :],
                                            ALU.mult, ALU.mult), "gla_qk")
            sig(ve.tensor_tensor(lki, feat[:, 8:10, :], EnG, ALU.mult), "gla_qk")
            sig(ve.tensor_tensor(lkd, feat[:, 8:10, :], edG, ALU.mult), "gla_qk")
            ve.wait_ge(S("gla_at"), 1)
            for t in range(NT):
                sig(ve.tensor_tensor(lattn[:, t, :, :], by4(1 + t), cs("tril").unsqueeze(1).to_broadcast([P, LH, P]),
                                     ALU.mult), "gla_ready")
            for half in range(2):
                sig(ve.tensor_scalar(lkt[:, half, :, :, :].rearrange("p a b c -> p (a b c)"), bank[3][:, :],
                                     cs("half")[:, half:half + 1], None, ALU.mult), "gla_ready")
            for n in range(NCH - 1):
                ve.wait_ge(S("gla_su"), n + 1)
                ve.wait_ge(S("gla_o"), n + 1)
                if n == 0:
                    sig(ve.tensor_copy(lstate, by4(5)), "gla_state")
                else:
                    for h in range(LH):
                        c = n * CHUNK + CHUNK - 1
                        sig(ve.scalar_tensor_tensor(lstate[:, h, :], lstate[:, h, :], EG[:, h // 2, c:c + 1],
                                                    bank[5][:, h * P:(h + 1) * P], ALU.mult, ALU.add), "gla_state")
                ve.wait_ge(S("gla_state"), 1 + LH * n)
            ve.wait_ge(S("gla_oc"), NCH)
            ve.wait_ge(S("gla_silu"), 2)
            output_norm(1, pr("gla_on"), 10)
            mixer_residual(1)
            moe(1)

        @block.gpsimd
        def _(gp):
            gp.memset(qpad, 0.0).then_inc(S("pads_zero"), 1)
            gp.memset(vpad, 0.0).then_inc(S("pads_zero"), 1)
            for i in range(FIRST_ADAS, len(ADAS)):
                gp.wait_ge(S("mod_scaled"), KT * (i - FIRST_ADAS + 1))
                w = ada_slot(gp, i)
                for step, half in enumerate((4, 2)):
                    gp.tensor_tensor(w[:, 0:half, :], w[:, 0:half, :], w[:, half:2 * half, :], ALU.add
                                     ).then_inc(S("mod_halved"), 1)
                    gp.wait_ge(S("mod_halved"), 2 * (i - FIRST_ADAS) + step + 1)
                gp.wait_ge(S("mod_turned"), i - 1)
                gp.tensor_tensor(partial[i % 2][:, :], w[:, 0, :], w[:, 1, :], ALU.add
                                 ).then_inc(S("mod_partial"), 1)
            gp.wait_ge(S("x_added"), 2 * KT)
            gp.memset(qpad, 0.0).then_inc(S("pads_zero"), 1)
            gp.memset(nvpad, 0.0).then_inc(S("pads_zero"), 1)
            gp.memset(vcpad, 0.0).then_inc(S("pads_zero"), 1)
            gp.wait_ge(S("nsa_nmax"), 2 * NH)
            gp.memset(lqd, 0.0).then_inc(S("pads_zero"), 1)


def tiles(a, width=P):
    r, c = a.shape
    return a.reshape(r // width, width, c).transpose(1, 0, 2).reshape(width, -1)


def lay_out(i):
    def rep(v):
        return np.broadcast_to(np.asarray(v).reshape(1, -1), (P, np.asarray(v).size))

    def cols(v):
        return np.asarray(v).reshape(-1, P).T

    def twice(v):
        return np.concatenate([v, v])[:, None]

    par = np.zeros((P, PARW), np.float32)

    def put(name, a):
        par[: a.shape[0], PAR[name][0]:PAR[name][0] + a.shape[1]] = a

    put("c", cols(i["c"][0]))
    put("ada_b", cols(i["ada_b"]))
    put("norm_mix", cols(i["norm_mix"]))
    put("norm_ffn", cols(i["norm_ffn"]))
    put("router", tiles(i["moe_router"].reshape(LAYERS * D, E)))
    put("e_bias", rep(i["moe_bias"]))
    put("fox_fb", rep(i["fox_fb"]))
    put("fox_qn", twice(i["fox_qn"][0]))
    put("fox_kn", twice(i["fox_kn"][0]))
    put("conv", i["gdn_conv"][0].T.reshape(12, P, 4).transpose(1, 0, 2).reshape(P, 48))
    put("a_log", rep(i["gdn_a_log"]))
    put("dt_bias", rep(i["gdn_dt_bias"]))
    put("gdn_on", i["gdn_on"][0][:, None])
    put("nsa_qn", twice(i["nsa_qn"][0]))
    put("nsa_kn", twice(i["nsa_kn"][0]))
    pos = i["nsa_pos"][0].reshape(2, 2, 16, NDH)
    put("pos", pos.transpose(1, 3, 0, 2).reshape(P, 32))
    put("wg_up", i["gla_wg_up"][0])
    put("bg", rep(i["gla_bg"]))
    put("gla_on", i["gla_on"][0][:, None])
    put("rel", np.concatenate([i["rel_bias"], np.ones((1, NH), np.float32)]))

    pair = np.concatenate([np.r_[64 * h:64 * h + 64, 64 * (h + 4):64 * (h + 4) + 64] for h in range(4)])
    ev, od = i["ev_w_in"][0], i["od_w_in"][0]
    ev_cut = np.cumsum([0, 512, 512, 512, 8, 1536, 4, 4, 512])
    fq, fk, fv, ff, gqkv, ga, gb, gz = (ev[:, a:b] for a, b in zip(ev_cut, ev_cut[1:]))
    od_cut = np.cumsum([0, 512] + [128] * 6 + [24, 256, 256, 512, 16, 512])
    nq, kc, vc, ks, vs, kw, vw, ng, lq, lk, lv, lg, lr = (od[:, a:b] for a, b in zip(od_cut, od_cut[1:]))
    double = [x[:, 64 * g:64 * g + 64] for x in (kc, vc) for g in range(2) for _ in range(2)]
    full = {"in0.0": np.concatenate([fv, ff, ga, gb], 1), "in1.0": np.concatenate([vs, vw, lv], 1),
            "in1.1": np.concatenate([ng, lg], 1)}
    feat0 = np.concatenate([fq, fk, gqkv, gz], 1)
    feat1 = np.concatenate([nq[:, pair], ks, kw, lq, lk, lr] + double, 1)
    out1 = i["od_w_out"][0]
    outs = [i["ev_w_out"][0], np.concatenate([out1[:512][pair], out1[512:]])]
    w1, w2 = i["nsa_cmp_w1"][0], i["nsa_cmp_w2"][0]
    mix = np.zeros((len(NAMES), P, SLOTW), np.float32)
    for n, name in enumerate(NAMES):
        s = int(name[-1])
        if name in full:
            a = tiles(full[name])
        elif name.startswith("ada"):
            a = tiles(i["ada_w"][int(name[3])][:, SC * s:SC * (s + 1)])
        elif name.startswith("in0"):
            a = tiles(feat0[:, SC * (s - 1):SC * s])
        elif name.startswith("in1"):
            a = tiles(feat1[:, SC * (s - 2):SC * (s - 1)])
        elif name.startswith("out"):
            a = tiles(outs[int(name[3])][:, 512 * s:512 * (s + 1)])
        else:
            first = w1[s].reshape(2, 16, NDH, CHID).transpose(0, 2, 1, 3).reshape(P, 16 * CHID)
            second = tiles(w2[s])
            if s == 0:
                second = second.reshape(P, 2, NDH)
                padded = np.zeros((P, 2, 2, P), np.float32)
                padded[:, :, 0, 0:NDH] = second
                padded[:, :, 1, NDH:P] = second
                second = padded.reshape(P, 512)
            a = np.concatenate([first, second], 1)
        mix[n, :, 0:a.shape[1]] = a

    moe = np.empty((LAYERS * X, P, SLOTW), np.float32)
    for l in range(LAYERS):
        at = l * X
        third = KT * FE
        up = moe[at:at + X, :, 0:2 * third].reshape(X, P, 2, 2, KT, P)
        for j, (sh, ex) in enumerate((("sh_wg", "moe_wg"), ("sh_wu", "moe_wu"))):
            up[0, :, :, j] = i[sh][l].reshape(KT, P, 2, P).transpose(1, 2, 0, 3)
            up[1:, :, :, j] = i[ex][l].reshape(E, KT, P, 2, P).transpose(0, 2, 3, 1, 4)
        moe[at:at + X, :, 0:2 * third] = up.reshape(X, P, 2 * third)
        moe[at, :, 2 * third:] = tiles(i["sh_wd"][l])
        moe[at + 1:at + 1 + E, :, 2 * third:] = i["moe_wd"][l].reshape(E, 2, P, D).transpose(
            0, 2, 1, 3).reshape(E, P, third)
    x = i["x"][0].T.reshape(KT, P, T).transpose(1, 0, 2)
    return {"xT_in": np.ascontiguousarray(x), "par_in": par, "cst_in": constants(), "mix_in": mix, "moe_in": moe}


def kernel(**inputs):
    import concourse.bacc as _bacc
    from concourse.bass_utils import run_bass_kernel_spmd as _run

    arrays = lay_out({k: np.asarray(v) for k, v in inputs.items()})
    nc = _bacc.Bacc("TRN2", target_bir_lowering=False, num_devices=1)
    args = [nc.dram_tensor(n, a.shape, F32, kind="ExternalInput").ap() for n, a in arrays.items()]
    args.append(nc.dram_tensor("outT", (P, KT, T), F32, kind="ExternalOutput").ap())
    program(nc, *args)
    r = _run(nc, [arrays], core_ids=[0])
    out = r.results[0]["outT"]
    return np.ascontiguousarray(out.transpose(1, 0, 2).reshape(D, T).T.reshape(1, T, D))
```
